# Optimizing a Trainium2 kernel written in Bass

```python
import jax, jax.numpy as jnp
from jax import lax
import numpy as np

D_MODEL = 1024
BATCH = 1
SEQ = 128
DEPTH = 2
DEC_BATCH = 1
DEC_SEQ = 256
PAST_LEN = 128

GRID_W = 64
MLA_HEADS = 8
QK_NOPE_DIM = 64
QK_ROPE_DIM = 32
QK_HEAD_DIM = QK_NOPE_DIM + QK_ROPE_DIM
V_HEAD_DIM = 64
KV_LORA_RANK = 256
MLA_WIDTH = MLA_HEADS * V_HEAD_DIM
RET_HEADS = 4
RET_DK = 128
RET_DV = 128
RET_CHUNK = 128
RET_WIDTH = RET_HEADS * RET_DV
MIX_WIDTH = MLA_WIDTH + RET_WIDTH
IN_SIZES = (MLA_HEADS * QK_HEAD_DIM, KV_LORA_RANK, QK_ROPE_DIM,
            RET_HEADS * RET_DK, RET_HEADS * RET_DK, RET_HEADS * RET_DV, RET_WIDTH)
IN_COLS = sum(IN_SIZES)
D_FF = 2816
N_EXPERTS = 8
TOP_K = 2
EXPERT_FF = 1408
N_DENSE = (DEPTH + 1) // 2
N_MOE = DEPTH // 2
Q_BLOCK = 128
ROPE_BASE = 10000.0
EPS = 1e-6

kernel_name = "hybrid_mla_retention_diffusion_step"

def rmsnorm(x, g=None):
    xf = x.astype(jnp.float32)
    y = (xf * lax.rsqrt(jnp.mean(xf * xf, axis=-1, keepdims=True) + EPS)).astype(x.dtype)
    if g is not None:
        y = y * g
    return y

def axial_rope_tables(n_tok, dim, dtype):
    rows = n_tok // GRID_W
    row = jnp.repeat(jnp.arange(rows), GRID_W)
    col = jnp.tile(jnp.arange(GRID_W), rows)
    half = dim // 2
    freqs = ROPE_BASE ** (-jnp.arange(0, half, 2, dtype=jnp.float32) / half)

    def ang(p):
        a = p.astype(jnp.float32)[:, None] * freqs[None, :]
        return jnp.concatenate([a, a], axis=-1)

    angles = jnp.concatenate([ang(row), ang(col)], axis=-1)
    return jnp.cos(angles).astype(dtype), jnp.sin(angles).astype(dtype)

def apply_rope(x, cos, sin):
    half = x.shape[-1] // 2

    def rot_half(v):
        v1, v2 = jnp.split(v, 2, axis=-1)
        return jnp.concatenate([-v2, v1], axis=-1)

    rot = jnp.concatenate([rot_half(x[..., :half]), rot_half(x[..., half:])], axis=-1)
    return x * cos[None, :, None, :] + rot * sin[None, :, None, :]

def split_in_proj(p):
    idx = [int(v) for v in np.cumsum(IN_SIZES)[:-1]]
    return jnp.split(p, idx, axis=-1)

def adaln(cvec, w_ada, b_ada):
    mod = jax.nn.silu(cvec) @ w_ada + b_ada
    return [m[:, None, :] for m in jnp.split(mod, 6, axis=-1)]

def modulate(xn, shift, scale):
    return xn * (1.0 + scale) + shift

def block_attention(q, k, v):
    B, Tq, H, d = q.shape
    dv = v.shape[-1]
    nb = Tq // Q_BLOCK
    qb = q.reshape(B, nb, Q_BLOCK, H, d).transpose(1, 0, 2, 3, 4)
    scale = d ** -0.5

    def one(qi):
        s = jnp.einsum('bqhd,bkhd->bhqk', qi, k).astype(jnp.float32) * scale
        p = jax.nn.softmax(s, axis=-1).astype(v.dtype)
        return jnp.einsum('bhqk,bkhe->bqhe', p, v)

    out = lax.map(one, qb)
    return out.transpose(1, 0, 2, 3, 4).reshape(B, Tq, H, dv)

def mla_kv(ckv, krope, w_ukv, k_norm):
    B, L, _ = ckv.shape
    kv = (ckv @ w_ukv).reshape(B, L, MLA_HEADS, QK_NOPE_DIM + V_HEAD_DIM)
    k_nope, v = kv[..., :QK_NOPE_DIM], kv[..., QK_NOPE_DIM:]
    k_pe = jnp.broadcast_to(krope[:, :, None, :], (B, L, MLA_HEADS, QK_ROPE_DIM))
    k = rmsnorm(jnp.concatenate([k_nope, k_pe], axis=-1), k_norm)
    return k, v

def rope_tail(x, cos, sin):
    return jnp.concatenate([x[..., :QK_NOPE_DIM], apply_rope(x[..., QK_NOPE_DIM:], cos, sin)], axis=-1)

def retention_chunked(q, k, v, log_gamma, s0):
    B, T, H, dk = q.shape
    dv = v.shape[-1]
    C = RET_CHUNK
    nc = T // C

    def chunks(a):
        return a.astype(jnp.float32).reshape(B, nc, C, H, a.shape[-1]).transpose(1, 0, 3, 2, 4)

    qc, kc, vc = chunks(q), chunks(k), chunks(v)
    pos = jnp.arange(C, dtype=jnp.float32)
    diff = pos[:, None] - pos[None, :]
    lg = log_gamma[:, None, None]
    decay_mask = jnp.where(diff >= 0, jnp.exp(lg * jnp.maximum(diff, 0.0)), 0.0)
    q_decay = jnp.exp(log_gamma[:, None] * (pos[None, :] + 1.0))
    k_decay = jnp.exp(log_gamma[:, None] * (C - 1.0 - pos[None, :]))
    chunk_decay = jnp.exp(log_gamma * C)

    def step(S, inp):
        qi, ki, vi = inp
        scores = jnp.einsum('bhid,bhjd->bhij', qi, ki) * decay_mask[None]
        intra = jnp.einsum('bhij,bhje->bhie', scores, vi)
        cross = jnp.einsum('bhid,bhde->bhie', qi, S) * q_decay[None, :, :, None]
        S_new = S * chunk_decay[None, :, None, None] + jnp.einsum(
            'bhjd,bhje->bhde', ki * k_decay[None, :, :, None], vi)
        return S_new, intra + cross

    S_fin, out = lax.scan(step, s0.astype(jnp.float32), (qc, kc, vc))
    out = out.transpose(1, 0, 3, 2, 4).reshape(B, T, H, dv)
    return out, S_fin

def bidir_retention(q, k, v, decay_logit, s0_f, s0_b):
    lg = jax.nn.log_sigmoid(decay_logit.astype(jnp.float32))
    o_f, s_f = retention_chunked(q, k, v, lg[0], s0_f)
    o_b, s_b = retention_chunked(jnp.flip(q, 1), jnp.flip(k, 1), jnp.flip(v, 1), lg[1], s0_b)
    return o_f + jnp.flip(o_b, 1), s_f, s_b

def retention_output(r, g):
    B, T = r.shape[0], r.shape[1]
    r = rmsnorm(r).reshape(B, T, RET_WIDTH).astype(g.dtype)
    return r * jax.nn.silu(g)

def mix_context(h, w_in, kv_norm, w_ukv, q_norm, k_norm, decay_logit, w_out):
    B, T, _ = h.shape
    q, ckv, krope, qr, kr, vr, g = split_in_proj(h @ w_in)
    q = rmsnorm(q.reshape(B, T, MLA_HEADS, QK_HEAD_DIM), q_norm)
    ckv = rmsnorm(ckv, kv_norm)
    k, v = mla_kv(ckv, krope, w_ukv, k_norm)
    a = block_attention(q, k, v).reshape(B, T, MLA_WIDTH)
    qr = qr.reshape(B, T, RET_HEADS, RET_DK)
    kr = kr.reshape(B, T, RET_HEADS, RET_DK) * (RET_DK ** -0.5)
    vr = vr.reshape(B, T, RET_HEADS, RET_DV)
    zero = jnp.zeros((B, RET_HEADS, RET_DK, RET_DV), jnp.float32)
    r, s_f, s_b = bidir_retention(qr, kr, vr, decay_logit, zero, zero)
    out = jnp.concatenate([a, retention_output(r, g)], axis=-1) @ w_out
    state = jnp.stack([s_f, s_b], axis=1).astype(h.dtype)
    return out, ckv, krope, state

def mix_latent(h, ckv_ctx, krope_ctx, state_ctx, w_in, kv_norm, w_ukv, q_norm, k_norm, decay_logit, w_out):
    B, T, _ = h.shape
    cos_m, sin_m = axial_rope_tables(T, QK_ROPE_DIM, h.dtype)
    cos_r, sin_r = axial_rope_tables(T, RET_DK, h.dtype)
    q, ckv, krope, qr, kr, vr, g = split_in_proj(h @ w_in)
    q = rope_tail(rmsnorm(q.reshape(B, T, MLA_HEADS, QK_HEAD_DIM), q_norm), cos_m, sin_m)
    ckv = rmsnorm(ckv, kv_norm)
    k_lat, v_lat = mla_kv(ckv, krope, w_ukv, k_norm)
    k_lat = rope_tail(k_lat, cos_m, sin_m)
    k_ctx, v_ctx = mla_kv(ckv_ctx, krope_ctx, w_ukv, k_norm)
    k = jnp.concatenate([k_ctx, k_lat], axis=1)
    v = jnp.concatenate([v_ctx, v_lat], axis=1)
    a = block_attention(q, k, v).reshape(B, T, MLA_WIDTH)
    qr = apply_rope(qr.reshape(B, T, RET_HEADS, RET_DK), cos_r, sin_r)
    kr = apply_rope(kr.reshape(B, T, RET_HEADS, RET_DK), cos_r, sin_r) * (RET_DK ** -0.5)
    vr = vr.reshape(B, T, RET_HEADS, RET_DV)
    r, _, _ = bidir_retention(qr, kr, vr, decay_logit, state_ctx[:, 0], state_ctx[:, 1])
    return jnp.concatenate([a, retention_output(r, g)], axis=-1) @ w_out

def swiglu(x, wg, wu, wd):
    return (jax.nn.silu(x @ wg) * (x @ wu)) @ wd

def moe_ffn(h, w_router, wg, wu, wd):
    B, T, D = h.shape
    x = h.reshape(B * T, D)
    logits = (x @ w_router).astype(jnp.float32)
    vals, idx = lax.top_k(logits, TOP_K)
    w = jax.nn.softmax(vals, axis=-1)
    combine = jnp.sum(jax.nn.one_hot(idx, N_EXPERTS, dtype=jnp.float32) * w[..., None], axis=1).astype(h.dtype)
    out = jnp.zeros_like(x)
    for e in range(N_EXPERTS):
        out = out + combine[:, e:e + 1] * swiglu(x, wg[e], wu[e], wd[e])
    return out.reshape(B, T, D)

def channel_mixer(h, l, w_ffn_gate, w_ffn_up, w_ffn_down, w_router, w_exp_gate, w_exp_up, w_exp_down):
    if l % 2 == 0:
        i = l // 2
        return swiglu(h, w_ffn_gate[i], w_ffn_up[i], w_ffn_down[i])
    i = l // 2
    return moe_ffn(h, w_router[i], w_exp_gate[i], w_exp_up[i], w_exp_down[i])

def setup_inputs(seed: int = 0) -> dict:
    key = jax.random.key(seed)
    ks = jax.random.split(key, 32)
    f32 = jnp.float32

    def nrm(k, shape, scale=1.0):
        return jax.random.normal(k, shape, f32) * scale

    base_logit = jnp.log(2.0 ** (5.0 + jnp.arange(RET_HEADS, dtype=f32)) - 1.0)
    return {
        "x_prompt": nrm(ks[0], (BATCH, SEQ, D_MODEL)),
        "x_sample": nrm(ks[1], (DEC_BATCH, DEC_SEQ, D_MODEL)),
        "cache_ckv": nrm(ks[2], (DEC_BATCH, DEPTH, PAST_LEN, KV_LORA_RANK)),
        "cache_krope": nrm(ks[3], (DEC_BATCH, DEPTH, PAST_LEN, QK_ROPE_DIM)),
        "state_ret": nrm(ks[4], (DEC_BATCH, DEPTH, 2, RET_HEADS, RET_DK, RET_DV), 0.5),
        "c": nrm(ks[5], (DEC_BATCH, D_MODEL)),
        "c_ctx": nrm(ks[6], (D_MODEL,)),
        "attn_norm": 1.0 + nrm(ks[7], (DEPTH, D_MODEL), 0.02),
        "ffn_norm": 1.0 + nrm(ks[8], (DEPTH, D_MODEL), 0.02),
        "w_ada": nrm(ks[9], (DEPTH, D_MODEL, 6 * D_MODEL), 0.5 * D_MODEL ** -0.5),
        "b_ada": nrm(ks[10], (DEPTH, 6 * D_MODEL), 0.02),
        "w_in": nrm(ks[11], (DEPTH, D_MODEL, IN_COLS), D_MODEL ** -0.5),
        "kv_norm": 1.0 + nrm(ks[12], (DEPTH, KV_LORA_RANK), 0.02),
        "w_ukv": nrm(ks[13], (DEPTH, KV_LORA_RANK, MLA_HEADS * (QK_NOPE_DIM + V_HEAD_DIM)), KV_LORA_RANK ** -0.5),
        "q_norm": 1.0 + nrm(ks[14], (DEPTH, QK_HEAD_DIM), 0.02),
        "k_norm": 1.0 + nrm(ks[15], (DEPTH, QK_HEAD_DIM), 0.02),
        "decay_logit": base_logit[None, None, :] + nrm(ks[16], (DEPTH, 2, RET_HEADS), 0.1),
        "w_out": nrm(ks[17], (DEPTH, MIX_WIDTH, D_MODEL), MIX_WIDTH ** -0.5),
        "w_ffn_gate": nrm(ks[18], (N_DENSE, D_MODEL, D_FF), D_MODEL ** -0.5),
        "w_ffn_up": nrm(ks[19], (N_DENSE, D_MODEL, D_FF), D_MODEL ** -0.5),
        "w_ffn_down": nrm(ks[20], (N_DENSE, D_FF, D_MODEL), D_FF ** -0.5),
        "w_router": nrm(ks[21], (N_MOE, D_MODEL, N_EXPERTS), D_MODEL ** -0.5),
        "w_exp_gate": nrm(ks[22], (N_MOE, N_EXPERTS, D_MODEL, EXPERT_FF), D_MODEL ** -0.5),
        "w_exp_up": nrm(ks[23], (N_MOE, N_EXPERTS, D_MODEL, EXPERT_FF), D_MODEL ** -0.5),
        "w_exp_down": nrm(ks[24], (N_MOE, N_EXPERTS, EXPERT_FF, D_MODEL), EXPERT_FF ** -0.5),
    }

def reference(x_prompt, x_sample, cache_ckv, cache_krope, state_ret, c, c_ctx,
              attn_norm, ffn_norm, w_ada, b_ada, w_in, kv_norm, w_ukv, q_norm, k_norm,
              decay_logit, w_out, w_ffn_gate, w_ffn_up, w_ffn_down,
              w_router, w_exp_gate, w_exp_up, w_exp_down):
    yp = x_prompt
    ys = x_sample
    ckv_list, krope_list, state_list = [], [], []
    for l in range(DEPTH):
        mix_w = (w_in[l], kv_norm[l], w_ukv[l], q_norm[l], k_norm[l], decay_logit[l], w_out[l])
        ffn_w = (w_ffn_gate, w_ffn_up, w_ffn_down, w_router, w_exp_gate, w_exp_up, w_exp_down)
        sh1, sc1, g1, sh2, sc2, g2 = adaln(c_ctx[None, :], w_ada[l], b_ada[l])
        h = modulate(rmsnorm(yp, attn_norm[l]), sh1, sc1)
        out, ckv_l, krope_l, st_l = mix_context(h, *mix_w)
        yp = yp + g1 * out
        h = modulate(rmsnorm(yp, ffn_norm[l]), sh2, sc2)
        yp = yp + g2 * channel_mixer(h, l, *ffn_w)
        ckv_list.append(ckv_l)
        krope_list.append(krope_l)
        state_list.append(st_l)
        sh1, sc1, g1, sh2, sc2, g2 = adaln(c, w_ada[l], b_ada[l])
        h = modulate(rmsnorm(ys, attn_norm[l]), sh1, sc1)
        out = mix_latent(h, cache_ckv[:, l], cache_krope[:, l], state_ret[:, l], *mix_w)
        ys = ys + g1 * out
        h = modulate(rmsnorm(ys, ffn_norm[l]), sh2, sc2)
        ys = ys + g2 * channel_mixer(h, l, *ffn_w)
    new_cache_ckv = jnp.stack(ckv_list, axis=1)
    new_cache_krope = jnp.stack(krope_list, axis=1)
    new_state_ret = jnp.stack(state_list, axis=1)
    return (yp, ys, new_cache_ckv, new_cache_krope, new_state_ret)


_drawn_inputs = setup_inputs


def setup_inputs(seed=0):
    import zlib

    import numpy as np

    out = dict(_drawn_inputs(seed))
    spreads = {}
    factors = {'cache_krope': 4.904, 'ffn_norm': 2.901, 'kv_norm': 2.873, 'q_norm': 8.0, 'k_norm': 8.0}
    for name, (base, spread) in spreads.items():
        noise = np.random.default_rng([zlib.crc32(name.encode()), seed]).standard_normal(out[name].shape)
        drawn = base * np.exp(spread * noise) if base else spread * noise
        out[name] = __import__('jax').numpy.asarray(drawn.astype(out[name].dtype))
    for name, factor in factors.items():
        out[name] = (out[name] * factor).astype(out[name].dtype)
    return out
```

```python
import concourse.bass as bass
from concourse import mybir
from contextlib import ExitStack

P = 128
D = 1024
DK = D // P
NT = 3
TOK = NT * P
KIND = (0, 1, 1)
DEPTH = 2
HEADS, NOPE, ROPE = 8, 64, 32
HD = NOPE + ROPE
VD = 64
LORA = 256
RH, RD = 4, 128
Q, CKV, KRP, QR, KR, VR, GG = 0, 768, 1024, 1056, 1568, 2080, 2592
IN_COLS = 3104
FF, EFF = 2816, 1408
EXPERTS = 8
EPS = 1e-6
SLOT = 2048
RING = 3
BLK = 256
ADA_COLS = 2048
ADA_UNITS = 6 * D // ADA_COLS
IN_ORDER = [3, 4, 5, 6, 7, 8, 9, 10, 11, 12, 0, 1, 2]
NB = len(IN_ORDER)
DENSE = FF // BLK
EG = (EFF + BLK - 1) // BLK
EF = EFF // P
EK = 3 * EG
MRING = 6
CHUNKS_OVER = TOK // P - 1

CONST = {}
_at = 0
for _n, _w in (("ident", 128), ("cosm", 64), ("sinm", 64), ("cosr", 256), ("sinr", 256), ("kexp", 2),
               ("qexp", 256), ("dexp", 256), ("tri", 256), ("upper", 128), ("iota", 128), ("ones", 128)):
    CONST[_n] = (_at, _at + _w)
    _at += _w
N_CONST = _at


def hybrid_step(nc, x_prompt, x_sample, cache_ckv, cache_krope, state_ret, c, c_ctx, attn_norm, ffn_norm,
                w_ada, b_ada, w_in, kv_norm, w_ukv, q_norm, k_norm, decay_logit, w_out, w_ffn_gate,
                w_ffn_up, w_ffn_down, w_router, w_exp_gate, w_exp_up, w_exp_down, const_tab,
                y_prompt, y_sample, new_ckv, new_krope, new_state):
    f32, f32r = mybir.dt.float32, mybir.dt.float32r
    i32, u32 = mybir.dt.int32, mybir.dt.uint32
    ACT, ALU, AX = mybir.ActivationFunctionType, mybir.AluOpType, mybir.AxisListType

    mod_rows = nc.dram_tensor("mod_rows", (DEPTH * ADA_UNITS, 2, ADA_COLS), f32, kind="Internal").ap()

    chunks = []
    n_split = 0

    def add(kind, src, size, shape, free=None):
        nonlocal n_split
        m = None
        if kind == "split":
            m = n_split
            n_split += 1
        chunks.append(dict(n=len(chunks), m=m, a=sum(q["m"] is None for q in chunks), src=src, size=size,
                           shape=shape, free=free))
        return chunks[-1]

    def cols(w, c0, wd):
        return w.rearrange("(k p) n -> p k n", p=P)[:, :, c0:c0 + wd]

    sems = ExitStack()

    def sem(name):
        return sems.enter_context(nc.semaphore(name))

    with sems:
        raw_full = [sem(f"raw_full{i}") for i in range(MRING)]
        ada_used, hi_made, lo_made = sem("ada_used"), sem("hi_made"), sem("lo_made")
        proj_psum, ukv_psum, out_psum = sem("proj_psum"), sem("ukv_psum"), sem("out_psum")
        gate_done, up_done, down_done = sem("gate_done"), sem("up_done"), sem("down_done")

        ada_extra = [2 if p % 3 == 0 else 1 for p in range(12)] + [0]
        IN, UKV, OUT = {}, {}, {}

        def add_ada(l, u, k):
            add("plain", w_ada[l, P * k:P * (k + 1), ADA_COLS * u:ADA_COLS * (u + 1)], ADA_COLS, None)

        for k in range(DK):
            add_ada(0, 0, k)
        for l in range(DEPTH):
            a = 0
            for p in range(NB):
                c0 = IN_ORDER[p] * BLK
                wd = min(BLK, IN_COLS - c0)
                IN[l, p] = add("split", cols(w_in[l], c0, wd), DK * wd, wd, (proj_psum, NB * NT * l + NT * (p + 1)))
                for _ in range(ada_extra[p]):
                    add_ada(l, 1 + a // DK, a % DK)
                    a += 1
            UKV[l] = add("split", w_ukv[l].rearrange("(k p) n -> p k n", p=P), SLOT, 1024, (ukv_psum, 8 * (l + 1)))
            if l == 0:
                for k in range(DK):
                    add_ada(1, 0, k)
            for j in range(4):
                OUT[l, j] = add("split", cols(w_out[l], BLK * j, BLK), SLOT, BLK, (out_psum, 12 * l + 3 * (j + 1)))
            if l == 0:
                DN, DM = len(chunks), n_split
                for s in range(3 * DENSE):
                    add("split", None, SLOT, None)
                chunks[DN]["free"] = (gate_done, 2)
                chunks[DN + 1]["free"] = (up_done, 2)
                chunks[-3]["free"] = (up_done, 2 * DENSE)
                chunks[-2]["free"] = (down_done, DENSE)
                chunks[-1]["free"] = (down_done, DENSE + 1)
        MN, MM = len(chunks), n_split
        assert MN % RING == 0 and MM % RING == 0
        splits = [q for q in chunks if q["m"] is not None]

        setup_dma, setup_dve, setup_act = sem("setup_dma"), sem("setup_dve"), sem("setup_act")
        x_loaded, decay_loaded = sem("x_loaded"), sem("decay_loaded")
        bias_loaded, modrow_made, mod_stored, mod_loaded = sem("bias_loaded"), sem("modrow_made"), sem("mod_stored"), sem("mod_loaded")
        gate_loaded, scale_made = sem("gate_loaded"), sem("scale_made")
        ss_made, rstd_made, htok_made, hT_psum, hT_hi_made, hT_made = (sem(n) for n in (
            "ss_made", "rstd_made", "htok_made", "hT_psum", "hT_hi_made", "hT_made"))
        proj_made = sem("proj_made")
        wrow_loaded, ckv_ss, ckv_rstd, ckv_made, cache_stored = (sem(n) for n in (
            "wrow_loaded", "ckv_ss", "ckv_rstd", "ckv_made", "cache_stored"))
        rope_made, silu_g, dec_arg, dec_exp, dec_made, s0_loaded = (sem(n) for n in (
            "rope_made", "silu_g", "dec_arg", "dec_exp", "dec_made", "s0_loaded"))
        rT_psum, rT_made, kd_made, qd_made = sem("rT_psum"), sem("rT_made"), sem("kd_made"), sem("qd_made")
        sc_psum, sc_masked, st_psum, st_made, state_stored = (sem(n) for n in (
            "sc_psum", "sc_masked", "st_psum", "st_made", "state_stored"))
        ro_psum, ro_sq, ro_ss, ro_rstd, ro_made = (sem(n) for n in ("ro_psum", "ro_sq", "ro_ss", "ro_rstd", "ro_made"))
        ckvc_loaded, ckvT_psum, ckvT_hi, ckvT_made, kv_made, kpe_made = (sem(n) for n in (
            "ckvc_loaded", "ckvT_psum", "ckvT_hi", "ckvT_made", "kv_made", "kpe_made"))
        qk_ss, qk_rstd, qk_made, qk_rope, hT2_psum, headT_lo = (sem(n) for n in (
            "qk_ss", "qk_rstd", "qk_made", "qk_rope", "hT2_psum", "headT_lo"))
        headT_hi = sem("headT_hi")
        s_psum, negmax, exp_made, pT_psum, pT_made, pv_psum, a_made = (sem(n) for n in (
            "s_psum", "negmax", "exp_made", "pT_psum", "pT_made", "pv_psum", "a_made"))
        mT_psum, mT_hi, mT_made, x1_made = sem("mT_psum"), sem("mT_hi"), sem("mT_made"), sem("x1_made")
        gate_silu, act_made, acth_made, actl_made, x2_made = (sem(n) for n in (
            "gate_silu", "act_made", "acth_made", "actl_made", "x2_made"))
        y_stored = sem("y_stored")
        dve_chain, pool_chain, act_chain = sem("dve_chain"), sem("pool_chain"), sem("act_chain")
        pe_phase, act_phase, dve_phase, pool_phase = (sem(n) for n in ("pe_phase", "act_phase", "dve_phase", "pool_phase"))
        hth_made, htl_made = sem("hth_made"), sem("htl_made")
        wr_loaded, wr_hi, wr_made, lg_psum, lg_exp, route_made, rank_psum, rank_made, flags_made = (sem(n) for n in (
            "wr_loaded", "wr_hi", "wr_made", "lg_psum", "lg_exp", "route_made", "rank_psum", "rank_made", "flags_made"))
        pick_made, pickT_psum, pickT_made, gath_psum, xe_hi, xe_made = (sem(n) for n in (
            "pick_made", "pickT_psum", "pickT_made", "gath_psum", "xe_hi", "xe_made"))
        eg_done, eu_done, esilu_made, eact_made, eT_psum, eT_hi, eT_made = (sem(n) for n in (
            "eg_done", "eu_done", "esilu_made", "eact_made", "eT_psum", "eT_hi", "eT_made"))
        ed_done, o_hi_made, o_made, sca_psum, y_added = (sem(n) for n in (
            "ed_done", "o_hi_made", "o_made", "sca_psum", "y_added"))

        mem = ExitStack()

        def sb(name, shape, dt=f32, where=None):
            return (where or mem).enter_context(nc.sbuf_tensor(name, shape, dt))

        with mem:
            raw = sb("raw", [P, RING, SLOT])
            whi = sb("whi", [P, RING, SLOT], f32r)
            wlo = sb("wlo", [P, RING, SLOT], f32r)
            x = sb("x", [P, NT, D])
            const = sb("const", [P, N_CONST])
            modsb = sb("modsb", [P, 2, 2, D])
            modg = sb("modg", [P, 2, D])
            nw = sb("nw", [P, D])
            brow = sb("brow", [P, 512])
            modrow = sb("modrow", [P, 512])
            cT = sb("cT", [P, DK, 32])
            craw = sb("craw", [P, 2, DK])
            stat = sb("stat", [P, 64])
            pstat = sb("pstat", [P, 128])
            half = sb("half", [P, 8])
            lg = sb("lg", [P, DEPTH, 8])
            lgt = sb("lgt", [P, 2, DEPTH * 8])
            dec = sb("dec", [P, 2, 8])
            wrow = sb("wrow", [P, LORA + 2 * HD])
            psum = [mem.enter_context(nc.psum_tensor(f"bank{i}", [P, 512], f32)) for i in range(8)]

            def cst(name):
                return const[:, CONST[name][0]:CONST[name][1]]

            ident = cst("ident")
            ones = cst("ones")
            sbflat = modsb[:].rearrange("p a b c -> p (a b c)")
            qdec = sbflat[:, 0:1024].rearrange("p (d h i) -> p d h i", d=2, h=RH)
            mtmp = sbflat[:, 1024:2048].rearrange("p (d h i) -> p d h i", d=2, h=RH)
            maskT = mtmp[:, 0]
            S0 = sbflat[:, 2048:3072].rearrange("p (d h e) -> p d h e", d=2, h=RH)
            S1 = sbflat[:, 3072:4096].rearrange("p (d h e) -> p d h e", d=2, h=RH)
            kT = sbflat[0:HD, 0:4096].rearrange("p (h t) -> p h t", h=HEADS)
            ysum = sbflat[:, 0:NT * D].rearrange("p (t d) -> p t d", t=NT)
            esg = sbflat[:, 3072:3584].rearrange("p (b n) -> p b n", b=2)
            eact = sbflat[:, 3584:4096].rearrange("p (b n) -> p b n", b=2)

            mix = {}
            for l in range(DEPTH):
                with ExitStack() as ph:
                    proj = sb(f"proj{l}", [P, NT, IN_COLS], f32, ph)
                    m = {"proj": proj}
                    with ExitStack() as a:
                        m["hTh"] = sb(f"hTh{l}", [P, DK, TOK], f32r, a)
                        m["hTl"] = sb(f"hTl{l}", [P, DK, TOK], f32r, a)
                        m["htok"] = sb(f"htok{l}", [P, 2, D], f32, a)
                        m["rt"] = sb(f"ropetmp{l}", [P, 2, 512], f32, a)
                        m["sq"] = sb(f"sqtmp{l}", [P, LORA], f32, a)
                    with ExitStack() as a:
                        m["qrT"] = sb(f"qrT{l}", [P, NT, RH, P], f32, a)
                        m["krT"] = sb(f"krT{l}", [P, NT, RH, P], f32, a)
                        m["kd"] = sb(f"kd{l}", [P, 4, RH, P], f32, a)
                        m["qd"] = sb(f"qd{l}", [P, 4, RH, P], f32, a)
                        m["at"] = sb(f"at{l}", [P, NT, RH, P], f32, a)
                        m["st"] = sb(f"st{l}", [P, 2, RH, P], f32, a)
                    with ExitStack() as a:
                        m["kcat"] = sb(f"kcat{l}", [P, 4, HEADS, HD], f32, a)
                        m["v"] = sb(f"v{l}", [P, 4, HEADS, VD], f32, a)
                        m["kpe"] = sb(f"kpe{l}", [P, ROPE], f32, a)
                        m["rt2"] = sb(f"ropetmp2{l}", [P, 2, HEADS * ROPE], f32, a)
                        with ExitStack() as b:
                            m["cTh"] = sb(f"cTh{l}", [P, 2, 512], f32r, b)
                            m["cTl"] = sb(f"cTl{l}", [P, 2, 512], f32r, b)
                            m["cc"] = sb(f"cc{l}", [P, LORA], f32, b)
                        with ExitStack() as b:
                            m["qT"] = sb(f"qT{l}", [HD, HEADS, TOK], f32, b)
                            m["pT"] = sb(f"pT{l}", [P, 2, TOK], f32, b)
                    with ExitStack() as a:
                        m["mTh"] = sb(f"mTh{l}", [P, DK, TOK], f32r, a)
                        m["mTl"] = sb(f"mTl{l}", [P, DK, TOK], f32r, a)
                        m["tmp"] = sb(f"outtmp{l}", [P, 2, BLK], f32, a)
                    mix[l] = m
            ffn = {}
            with ExitStack() as ph:
                ffn["hTh"] = sb("fhTh", [P, DK, TOK], f32r, ph)
                ffn["hTl"] = sb("fhTl", [P, DK, TOK], f32r, ph)
                ffn["htok"] = sb("fhtok", [P, 2, D], f32, ph)
                ffn["sg"] = sb("fsg", [P, 2, TOK], f32, ph)
                ffn["act"] = sb("fact", [P, 2, TOK], f32, ph)
                ffn["acth"] = sb("facth", [P, 2, 2, TOK], f32r, ph)
                ffn["actl"] = sb("factl", [P, 2, 2, TOK], f32r, ph)
                ffn["tmp"] = sb("ftmp", [P, 2, 512], f32, ph)
            moe = {}
            with ExitStack() as ph:
                moe["hth"] = sb("hth", [P, NT, D], f32r, ph)
                moe["htl"] = sb("htl", [P, NT, D], f32r, ph)
                moe["cmb"] = sb("cmb", [P, NT, 8], f32, ph)
                moe["posc"] = sb("posc", [P, NT, 8 * (1 + CHUNKS_OVER)], f32, ph)
                moe["flags"] = sb("flags", [1, 8 * CHUNKS_OVER], i32, ph)
                with ExitStack() as a:
                    moe["hTh"] = sb("ehTh", [P, DK, TOK], f32r, a)
                    moe["hTl"] = sb("ehTl", [P, DK, TOK], f32r, a)
                    moe["htok"] = sb("ehtok", [P, 2, D], f32, a)
                    moe["wr"] = sb("wr", [P, DK, 8], f32, a)
                    moe["wrh"] = sb("wrh", [P, DK, 8], f32r, a)
                    moe["wrl"] = sb("wrl", [P, DK, 8], f32r, a)
                    moe["r"] = sb("route", [P, 12, NT, 8], f32, a)
                    moe["ix"] = sb("ix", [P, NT, 8], u32, a)
                with ExitStack() as a:
                    moe["rawx"] = sb("rawx", [P, MRING - RING, SLOT], f32, a)
                    moe["xeh"] = sb("xeh", [P, DK, P], f32r, a)
                    moe["xel"] = sb("xel", [P, DK, P], f32r, a)
                    moe["pick"] = sb("pick", [P, NT, P], f32r, a)
                    moe["pickT"] = sb("pickT", [P, NT, P], f32r, a)
                    moe["eTh"] = sb("eTh", [P, EF, P], f32r, a)
                    moe["eTl"] = sb("eTl", [P, EF, P], f32r, a)
                    moe["oh"] = sb("oh", [P, D], f32r, a)
                    moe["ol"] = sb("ol", [P, D], f32r, a)
                    moe["gw"] = sb("gw", [P, 1], f32, a)
                with ExitStack() as a:
                    moe["tmp"] = sb("ytmp", [P, 2, D], f32, a)

            def bc(ap, shape):
                return ap.to_broadcast(shape)

            def raw_wait(eng, n0, it=0):
                eng.wait_ge(raw_full[n0 % RING], 16 * (n0 // RING + 1) + 16 * it)

            def mraw(k):
                return raw[:, k] if k < RING else moe["rawx"][:, k - RING]

            MUSES = [MN // RING] * RING + [0] * (MRING - RING)

            def e_size(k):
                if k < 2 * EG:
                    return DK * min(BLK, EFF - BLK * (k // 2))
                return D * min(2, EF - 2 * (k - 2 * EG))

            def pre_free(m):
                return splits[m - RING]["free"] if m >= RING else None

            def dense_free(off, it):
                if off == 2:
                    return gate_done, 2 * it + 2
                if off == 3:
                    return up_done, 2 * it + 2
                return down_done, it + (off - 3)

            def expert_wait(eng, r, k):
                eng.wait_ge(raw_full[k % MRING], 16 * (MUSES[k % MRING] + k // MRING + 1) + 16 * (EK // MRING) * r)

            def expert_hi(act, s, r, k, static=False):
                expert_wait(act, r, k)
                if static:
                    act.wait_ge(*splits[MM + k - RING]["free"])
                elif k < RING:
                    act.wait_ge(ed_done, EG * r + k + 1)
                else:
                    act.wait_ge(*expert_free(r, k - RING))
                z = e_size(k)
                s.activation(whi[:, k % RING, 0:z], mraw(k % MRING)[:, 0:z], ACT.Copy).then_inc(hi_made, 1)

            def expert_lo(dve, v, r, k):
                dve.wait_ge(hi_made, MM + EK * r + k + 1)
                z = e_size(k)
                v.tensor_tensor(wlo[:, k % RING, 0:z], mraw(k % MRING)[:, 0:z], whi[:, k % RING, 0:z].bitcast(f32),
                                ALU.subtract).then_inc(lo_made, 1)

            def expert_free(r, k):
                if k < 2 * EG:
                    return ((eg_done, eu_done)[k % 2], EG * r + k // 2 + 1)
                return (ed_done, EG * r + (k - 2 * EG) + 1 + RING)

            def act_gather(act, s, r):
                act.wait_ge(gath_psum, r + 1)
                for b in range(2):
                    s.activation(moe["xeh"][:, 4 * b:4 * b + 4, :],
                                 psum[2 * b][:].rearrange("p (c i) -> p c i", c=4), ACT.Copy).then_inc(xe_hi, 1)

            def make_act_expert(act, s):
                def eT(r, j):
                    act.wait_ge(eT_psum, EG * r + j + 1)
                    w = min(2, EF - 2 * j)
                    s.activation(moe["eTh"][:, 2 * j:2 * j + w, :],
                                 psum[4 + j % 2][:, 0:P * w].rearrange("p (c i) -> p c i", c=w), ACT.Copy).then_inc(eT_hi, 1)

                def body(r, more):
                    for j in range(EG):
                        w = min(BLK, EFF - BLK * j)
                        expert_hi(act, s, r, 2 * j + 2)
                        act.wait_ge(eg_done, EG * r + j + 1)
                        s.activation(esg[:, j % 2, 0:w], psum[j % 2][:, 0:w], ACT.Silu).then_inc(esilu_made, 1)
                        expert_hi(act, s, r, 2 * j + 3)
                        if j >= 1:
                            eT(r, j - 1)
                        if j == 3:
                            act.wait_ge(pickT_psum, r + 1)
                            s.activation(moe["pickT"][:], psum[6][:, 0:TOK].rearrange("p (t i) -> p t i", t=NT),
                                         ACT.Copy).then_inc(pickT_made, 1)
                            s.activation(moe["gw"][:], psum[6][:, TOK:TOK + 1], ACT.Copy).then_inc(pickT_made, 1)
                    if more:
                        act_gather(act, s, r + 1)
                    eT(r, EG - 1)
                    for k in range(2 * EG, EK):
                        if k + 2 < EK:
                            expert_hi(act, s, r, k + 2)
                        elif more:
                            expert_hi(act, s, r + 1, k + 2 - EK)
                    act.wait_ge(ed_done, EG * (r + 1) + RING)
                    act.wait_ge(pickT_made, 2 * r + 2)
                    for b in range(2):
                        s.activation(moe["oh"][:, 512 * b:512 * (b + 1)], psum[6 + b][:], ACT.Copy,
                                     scale=moe["gw"][:, 0:1]).then_inc(o_hi_made, 1)
                return body

            def overflow(eng, ns, item):
                count = ns.alloc_register("items_run")
                flag = ns.alloc_register("flag")
                ns.reg_mov(count, EXPERTS)
                eng.wait_ge(flags_made, 1)
                for cc in range(1, CHUNKS_OVER + 1):
                    with eng.Fori(0, EXPERTS) as e:
                        ns.reg_load(flag, moe["flags"][0:1, bass.ds(e + EXPERTS * (cc - 1), 1)])
                        with ns.If_ne(flag, 0):
                            r = ns.snap(count)
                            item(e, e + EXPERTS * cc, r)
                            ns.reg_add(count, count, 1)

            def dve_moe(dve, v, link, barrier):
                R = moe["r"]
                dve.wait_ge(wr_hi, 1)
                v.tensor_tensor(moe["wrl"][:], moe["wr"][:], moe["wrh"][:].bitcast(f32), ALU.subtract).then_inc(wr_made, 1)
                dve.wait_ge(lg_psum, 1)
                link(v.tensor_copy(R[:, 0], psum[0][:, 0:NT * 8].rearrange("p (t e) -> p t e", t=NT)))
                for t in range(NT):
                    last = v.max(R[:, 2, t, :], R[:, 0, t, :])
                link(last)
                for t in range(NT):
                    last = v.max_index(moe["ix"][:, t, :], R[:, 2, t, :], R[:, 0, t, :])
                link(last)
                v.tensor_copy(R[:, 3], moe["ix"][:])
                v.tensor_tensor(R[:, 1, :, 0:1], R[:, 2, :, 1:2], R[:, 2, :, 0:1], ALU.subtract).then_inc(route_made, 1)
                dve.wait_ge(lg_exp, 1)
                link(v.tensor_scalar(R[:, 4, :, 0:1], R[:, 1, :, 0:1], 1.0, None, ALU.add))
                link(v.reciprocal(R[:, 5, :, 0:1], R[:, 4, :, 0:1]))
                link(v.tensor_tensor(R[:, 5, :, 1:2], R[:, 5, :, 0:1], R[:, 1, :, 0:1], ALU.mult))
                io = cst("iota")[:, 0:8]
                for t in range(NT):
                    for c2 in range(2):
                        v.tensor_scalar(R[:, 6 + c2, t, :], io, R[:, 3, t, c2:c2 + 1], None, ALU.is_equal)
                        last = v.tensor_scalar(R[:, 8 + c2, t, :], io, R[:, 3, t, c2:c2 + 1], R[:, 5, t, c2:c2 + 1],
                                               ALU.is_equal, ALU.mult)
                link(last)
                v.tensor_tensor(moe["cmb"][:], R[:, 8], R[:, 9], ALU.add)
                v.tensor_tensor(R[:, 10], R[:, 6], R[:, 7], ALU.add).then_inc(route_made, 1)
                dve.wait_ge(rank_psum, 1)
                link(v.tensor_scalar(R[:, 11], psum[1][:, 0:NT * 8].rearrange("p (t e) -> p t e", t=NT), 1.0, None, ALU.add))
                link(v.tensor_tensor(R[:, 11], R[:, 11], R[:, 10], ALU.mult))
                for cc in range(1 + CHUNKS_OVER):
                    v.tensor_scalar(moe["posc"][:, :, 8 * cc:8 * cc + 8], R[:, 11], -1.0 - P * cc, None, ALU.add)
                for cc in range(1, 1 + CHUNKS_OVER):
                    last = v.tensor_scalar(moe["flags"][0:1, 8 * (cc - 1):8 * cc], psum[1][0:1, NT * 8:NT * 8 + 8],
                                           float(P * cc), None, ALU.is_gt)
                link(last)
                barrier()
                v.drain().then_inc(flags_made, 1)
                link(v.memset(ysum, 0.0))
                v.memset(moe["oh"][:].bitcast(f32), 0.0)
                v.memset(moe["ol"][:].bitcast(f32), 0.0)
                v.memset(moe["pickT"][:].bitcast(f32), 0.0).then_inc(o_made, 2)

                def pick(q, n):
                    for t in range(NT):
                        last = v.tensor_scalar(moe["pick"][:, t, :], cst("iota"), moe["posc"][:, t, bass.ds(q, 1)], None, ALU.is_equal)
                    last.then_inc(pick_made, 1)

                def gather(r):
                    for b in range(2):
                        dve.wait_ge(xe_hi, 2 * r + b + 1)
                        v.tensor_tensor(moe["xel"][:, 4 * b:4 * b + 4, :], psum[2 * b][:].rearrange("p (c i) -> p c i", c=4),
                                        moe["xeh"][:, 4 * b:4 * b + 4, :].bitcast(f32), ALU.subtract).then_inc(xe_made, 1)

                def eT(r, j):
                    dve.wait_ge(eT_hi, EG * r + j + 1)
                    w = min(2, EF - 2 * j)
                    v.tensor_tensor(moe["eTl"][:, 2 * j:2 * j + w, :], psum[4 + j % 2][:, 0:P * w].rearrange("p (c i) -> p c i", c=w),
                                    moe["eTh"][:, 2 * j:2 * j + w, :].bitcast(f32), ALU.subtract).then_inc(eT_made, 1)

                def add_y(s, u):
                    t, hf = divmod(u, 2)
                    dve.wait_ge(sca_psum, 2 * NT * s + u + 1)
                    ys = ysum[:, t, 512 * hf:512 * (hf + 1)]
                    v.tensor_tensor(ys, ys, psum[6 + u % 2][:], ALU.add).then_inc(y_added, 1)

                def body(r, more, scatter_first):
                    for j in range(EG):
                        w = min(BLK, EFF - BLK * j)
                        expert_lo(dve, v, r, 2 * j + 2)
                        expert_lo(dve, v, r, 2 * j + 3)
                        dve.wait_ge(eu_done, EG * r + j + 1)
                        dve.wait_ge(esilu_made, EG * r + j + 1)
                        v.tensor_tensor(eact[:, j % 2, 0:w], psum[2 + j % 2][:, 0:w], esg[:, j % 2, 0:w], ALU.mult).then_inc(eact_made, 1)
                        if j >= 1:
                            eT(r, j - 1)
                        if j < NT and scatter_first:
                            add_y(r, 2 * j)
                            add_y(r, 2 * j + 1)
                        if j == 4 and more:
                            dve.wait_ge(pickT_psum, r + 1)
                            pick(r + 1, r + 1)
                    if more:
                        gather(r + 1)
                    eT(r, EG - 1)
                    for k in range(2 * EG, EK):
                        if k + 2 < EK:
                            expert_lo(dve, v, r, k + 2)
                        elif more:
                            expert_lo(dve, v, r + 1, k + 2 - EK)
                    for b in range(2):
                        dve.wait_ge(o_hi_made, 2 * r + b + 1)
                        cs = slice(512 * b, 512 * (b + 1))
                        v.scalar_tensor_tensor(out=moe["ol"][:, cs], in0=psum[6 + b][:], scalar=moe["gw"][:, 0:1],
                                               in1=moe["oh"][:, cs].bitcast(f32), op0=ALU.mult, op1=ALU.subtract).then_inc(o_made, 1)

                pick(0, 0)
                gather(0)
                with dve.Fori(0, EXPERTS - 1) as e:
                    body(e, True, True)
                body(EXPERTS - 1, False, True)
                for u in range(2 * NT):
                    add_y(EXPERTS, u)

                def item(e, q, r):
                    dve.wait_ge(pickT_psum, r)
                    pick(q, r)
                    gather(r)
                    for k in range(2):
                        expert_lo(dve, v, r, k)
                    body(r, False, False)
                    for u in range(2 * NT):
                        add_y(r + 1, u)
                overflow(dve, v, item)
                link_done = v.drain()
                link_done.then_inc(route_made, 1)
                dve.wait_ge(route_made, 3)
                dve.wait_ge(gate_loaded, 128)
                for t in range(NT):
                    if t == 2:
                        dve.wait_ge(x2_made, NT + 1)
                    link(v.tensor_tensor(moe["tmp"][:, t % 2, :], ysum[:, t, :], modg[:, KIND[t], :], ALU.mult))
                    v.tensor_tensor(x[:, t, :], x[:, t, :], moe["tmp"][:, t % 2, :], ALU.add).then_inc(x2_made, 1)

            def pe_dense(pe, mm):
                nc.tensor.drain().then_inc(down_done, 1)
                pe.wait_ge(hT_made, 2 * NT * 2)

                def up_block(off, it, i):
                    for ft in range(2):
                        for w, (bank, done, freed) in enumerate(((6, gate_done, gate_silu), (7, up_done, act_made))):
                            m0 = DM + off + w
                            pe.wait_ge(lo_made, m0 + 1 + 3 * it)
                            if not (isinstance(i, int) and i == 0 and ft == 0):
                                pe.wait_ge(freed, 2 * i + ft)
                            wh = whi[:, m0 % RING, :].rearrange("p (k n) -> p k n", n=BLK)
                            wl = wlo[:, m0 % RING, :].rearrange("p (k n) -> p k n", n=BLK)
                            fs = slice(P * ft, P * (ft + 1))
                            for k in range(DK):
                                mm(psum[bank][:, 0:TOK], wh[:, k, fs], ffn["hTh"][:, k, :], start=(k == 0), stop=False)
                                mm(psum[bank][:, 0:TOK], wh[:, k, fs], ffn["hTl"][:, k, :], start=False, stop=False)
                                last = mm(psum[bank][:, 0:TOK], wl[:, k, fs], ffn["hTh"][:, k, :], start=False, stop=(k == DK - 1))
                            last.then_inc(done, 1)

                def down_block(off, it, i, par, first, final):
                    m0 = DM + off
                    pe.wait_ge(lo_made, m0 + 1 + 3 * it)
                    pe.wait_ge(actl_made, 2 * i + 2)
                    wh = whi[:, m0 % RING, :].rearrange("p (k n) -> p k n", n=D)
                    wl = wlo[:, m0 % RING, :].rearrange("p (k n) -> p k n", n=D)
                    for t in range(NT):
                        for ft in range(2):
                            ah = ffn["acth"][:, par, ft, P * t:P * (t + 1)]
                            al = ffn["actl"][:, par, ft, P * t:P * (t + 1)]
                            for a, w in ((ah, wh), (ah, wl), (al, wh)):
                                for hf in range(2):
                                    last = mm(psum[2 * t + hf][:], a, w[:, ft, 512 * hf:512 * (hf + 1)],
                                              start=(first and ft == 0 and a is ah and w is wh),
                                              stop=(final and ft == 1 and a is al))
                    last.then_inc(down_done, 1)

                up_block(0, 0, 0)
                up_block(2, 0, 1)
                down_block(4, 0, 0, 0, True, False)
                up_block(2, 1, 2)
                down_block(4, 1, 1, 1, False, False)
                with pe.Fori(1, (DENSE - 1) // 2) as b:
                    for h in range(2):
                        up_block(2, 2 * b + h, 2 * b + h + 1)
                        down_block(4, 2 * b + h, 2 * b + h, h, False, False)
                down_block(5, DENSE - 2, DENSE - 1, 0, False, True)

            def pe_moe(pe, mm, mm3, barrier):
                tr = nc.tensor.transpose
                pe.wait_ge(hT_made, 2 * NT * 4)
                pe.wait_ge(wr_made, 1)
                for t in range(NT):
                    ts = slice(P * t, P * (t + 1))
                    for k in range(DK):
                        last = mm3(psum[0][:, 8 * t:8 * t + 8], moe["hTh"][:, k, ts], moe["hTl"][:, k, ts],
                                   moe["wrh"][:, k, :], moe["wrl"][:, k, :], k == 0, k == DK - 1)
                last.then_inc(lg_psum, 1)
                pe.wait_ge(route_made, 2)
                one = moe["r"][:, 10]
                for t in range(NT):
                    for t2 in range(t + 1):
                        mm(psum[1][:, 8 * t:8 * t + 8], cst("upper") if t2 == t else ones, one[:, t2, :],
                           start=(t2 == 0), stop=(t2 == t))
                for t2 in range(NT):
                    last = mm(psum[1][:, 8 * NT:8 * NT + 8], ones, one[:, t2, :], start=(t2 == 0), stop=(t2 == NT - 1))
                last.then_inc(rank_psum, 1)
                barrier()
                nc.tensor.drain().then_inc(ed_done, RING)

                def gather(r):
                    pe.wait_ge(pick_made, r + 1)
                    for c_ in range(DK):
                        o = psum[2 * (c_ // 4)][:, P * (c_ % 4):P * (c_ % 4 + 1)]
                        for t in range(NT):
                            for z, h in enumerate((moe["hth"], moe["htl"])):
                                last = mm(o, h[:, t, P * c_:P * (c_ + 1)], moe["pick"][:, t, :],
                                          start=(t == 0 and z == 0), stop=(t == NT - 1 and z == 1))
                    last.then_inc(gath_psum, 1)

                def scatter(s, units):
                    for u in units:
                        t, hf = divmod(u, 2)
                        if u == 0:
                            pe.wait_ge(o_made, 2 * s + 2)
                        if u >= 2:
                            pe.wait_ge(y_added, 2 * NT * s + u - 1)
                        cs = slice(512 * hf, 512 * (hf + 1))
                        mm(psum[6 + u % 2][:], moe["pickT"][:, t, :], moe["oh"][:, cs], start=True, stop=False)
                        mm(psum[6 + u % 2][:], moe["pickT"][:, t, :], moe["ol"][:, cs], start=False, stop=True).then_inc(sca_psum, 1)

                def eT(r, j):
                    pe.wait_ge(eact_made, EG * r + j + 1)
                    if j >= 2:
                        pe.wait_ge(eT_made, EG * r + j - 1)
                    for i in range(min(2, EF - 2 * j)):
                        last = tr(psum[4 + j % 2][:, P * i:P * (i + 1)], eact[:, j % 2, P * i:P * (i + 1)], ident)
                    last.then_inc(eT_psum, 1)

                def body(r, e, more, scatter_first):
                    for j in range(EG):
                        w = min(BLK, EFF - BLK * j)
                        if j == 0:
                            pe.wait_ge(xe_made, 2 * (r + 1))
                        for z, (bank, done, freed) in enumerate(((0, eg_done, esilu_made), (2, eu_done, eact_made))):
                            k0 = 2 * j + z
                            pe.wait_ge(lo_made, MM + EK * r + k0 + 1)
                            if j >= 2:
                                pe.wait_ge(freed, EG * r + j - 1)
                            wh = whi[:, k0 % RING, 0:DK * w].rearrange("p (k n) -> p k n", n=w)
                            wl = wlo[:, k0 % RING, 0:DK * w].rearrange("p (k n) -> p k n", n=w)
                            for k in range(DK):
                                last = mm3(psum[bank + j % 2][:, 0:w], moe["xeh"][:, k, :], moe["xel"][:, k, :],
                                           wh[:, k, :], wl[:, k, :], k == 0, k == DK - 1)
                            last.then_inc(done, 1)
                        if j >= 1:
                            eT(r, j - 1)
                        if j < NT and scatter_first:
                            scatter(r, (2 * j, 2 * j + 1))
                        if j == 3:
                            pe.wait_ge(y_added, 2 * NT * (r + 1))
                            for t in range(NT):
                                tr(psum[6][:, P * t:P * (t + 1)], moe["pick"][:, t, :].bitcast(f32), ident)
                            for t in range(NT):
                                last = mm(psum[6][:, TOK:TOK + 1], moe["pick"][:, t, :].bitcast(f32), moe["cmb"][:, t, bass.ds(e, 1)],
                                          start=(t == 0), stop=(t == NT - 1))
                            last.then_inc(pickT_psum, 1)
                    if more:
                        gather(r + 1)
                    eT(r, EG - 1)
                    pe.wait_ge(pickT_made, 2 * (r + 1))
                    for i in range(EG):
                        k0 = 2 * EG + i
                        n = min(2, EF - 2 * i)
                        pe.wait_ge(lo_made, MM + EK * r + k0 + 1)
                        pe.wait_ge(eT_made, EG * r + i + 1)
                        wh = whi[:, k0 % RING, 0:D * n].rearrange("p (k n) -> p k n", n=D)
                        wl = wlo[:, k0 % RING, 0:D * n].rearrange("p (k n) -> p k n", n=D)
                        for f in range(n):
                            ah, al = moe["eTh"][:, 2 * i + f, :], moe["eTl"][:, 2 * i + f, :]
                            for z, (a, wt) in enumerate(((ah, wh), (ah, wl), (al, wh))):
                                for hf in range(2):
                                    last = mm(psum[6 + hf][:], a, wt[:, f, 512 * hf:512 * (hf + 1)],
                                              start=(i == 0 and f == 0 and z == 0), stop=(i == EG - 1 and f == n - 1 and z == 2))
                        last.then_inc(ed_done, 1)

                gather(0)
                with pe.Fori(0, EXPERTS - 1) as e:
                    body(e, e, True, True)
                body(EXPERTS - 1, EXPERTS - 1, False, True)
                scatter(EXPERTS, range(2 * NT))

                def item(e, q, r):
                    gather(r)
                    body(r, e, False, False)
                    scatter(r + 1, range(2 * NT))
                overflow(pe, nc.tensor, item)

            block = sems.enter_context(nc.Block())

            @block.sync
            def _(sp):
                def load(q, dst):
                    n = q["n"]
                    if n >= RING:
                        before = chunks[n - RING]
                        if before["m"] is None:
                            sp.wait_ge(ada_used, before["a"] + 1)
                        else:
                            sp.wait_ge(lo_made, before["m"] + 1)
                    sp.dma_start(dst, q["src"]).then_inc(raw_full[n % RING], 16)

                def slot(q):
                    r = raw[:, q["n"] % RING, 0:q["size"]]
                    return r if q["shape"] is None else r.rearrange("p (k n) -> p k n", n=q["shape"])

                for q in chunks[:DN]:
                    load(q, slot(q))

                def dense_load(off, it, src, shape):
                    n0, m0 = DN + off, DM + off
                    sp.wait_ge(lo_made, m0 - RING + 1 + 3 * it)
                    sp.dma_start(raw[:, n0 % RING, :].rearrange("p (k n) -> p k n", n=shape), src)\
                        .then_inc(raw_full[n0 % RING], 16)

                wg, wu = (w[0].rearrange("(k p) n -> p k n", p=P) for w in (w_ffn_gate, w_ffn_up))
                wd = w_ffn_down[0].rearrange("(i k p) n -> i p k n", p=P, k=2)
                dense_load(0, 0, wg[:, :, 0:BLK], BLK)
                dense_load(1, 0, wu[:, :, 0:BLK], BLK)
                with sp.Fori(0, DENSE - 1) as i:
                    dense_load(2, i, wg[:, :, bass.ds(i * BLK + BLK, BLK)], BLK)
                    dense_load(3, i, wu[:, :, bass.ds(i * BLK + BLK, BLK)], BLK)
                    dense_load(4, i, wd[i], D)
                dense_load(5, DENSE - 2, wd[DENSE - 1], D)

                for q in chunks[DN + 3 * DENSE:]:
                    load(q, slot(q))

                def expert_load(e, r, k):
                    s = k % MRING
                    sz = e_size(k)
                    if k < 2 * EG:
                        w = (w_exp_gate, w_exp_up)[k % 2]
                        wdt = sz // DK
                        src = w[0, e].rearrange("(k p) n -> p k n", p=P)[:, :, BLK * (k // 2):BLK * (k // 2) + wdt]
                        dst = mraw(s)[:, 0:sz].rearrange("p (k n) -> p k n", n=wdt)
                    else:
                        i = 2 * (k - 2 * EG)
                        src = w_exp_down[0, e].rearrange("(k p) n -> p k n", p=P)[:, i:i + sz // D, :]
                        dst = mraw(s)[:, 0:sz].rearrange("p (k n) -> p k n", n=D)
                    sp.wait_ge(lo_made, MM + EK * r + k - MRING + 1)
                    sp.dma_start(dst, src).then_inc(raw_full[s], 16)

                for k in range(EK):
                    if k < RING:
                        sp.wait_ge(lo_made, MM - RING + k + 1)
                    if k == RING:
                        sp.wait_ge(flags_made, 1)
                    expert_load(0, 0, k)
                with sp.Fori(1, EXPERTS) as e:
                    for k in range(EK):
                        expert_load(e, e, k)
                overflow(sp, nc.sync, lambda e, qi, r: [expert_load(e, r, k) for k in range(EK)])

            @block.gpsimd
            def _(pool):
                g = nc.gpsimd
                chain = [0]

                def link(ins):
                    chain[0] += 1
                    ins.then_inc(pool_chain, 1)
                    pool.wait_ge(pool_chain, chain[0])

                phase = [0]

                def barrier():
                    phase[0] += 1
                    g.drain().then_inc(pool_phase, 1)
                    for s in (pe_phase, act_phase, dve_phase):
                        pool.wait_ge(s, phase[0])

                g.dma_start(craw[:, 0, :], c_ctx.rearrange("(k p) -> p k", p=P), allow_slow_non_contiguous=True).then_inc(setup_dma, 16)
                g.dma_start(craw[:, 1, :], c.rearrange("a (k p) -> p (a k)", p=P), allow_slow_non_contiguous=True).then_inc(setup_dma, 16)
                g.dma_start(const[:], const_tab).then_inc(setup_dma, 16)
                g.dma_start(x[:, 0, :], x_prompt[0]).then_inc(x_loaded, 16)
                g.dma_start(x[:, 1:3, :], x_sample[0].rearrange("(t p) d -> p t d", p=P)).then_inc(x_loaded, 16)
                g.dma_start(lgt[:, 0, :], decay_logit.rearrange("(o l) a h -> o (l a h)", o=1).to_broadcast([P, 16]))\
                    .then_inc(decay_loaded, 16)
                g.memset(half[:], -0.5).then_inc(pool_chain, 1)
                chain[0] += 1
                pool.wait_ge(pool_chain, 1)

                pool.wait_ge(setup_dma, 48)

                def load_bias(u):
                    l, k = divmod(u, ADA_UNITS)
                    for j in range(4):
                        c0 = ADA_COLS * k + 512 * j
                        g.dma_start(brow[32 * j:32 * j + 2, :], b_ada[l:l + 1, c0:c0 + 512].to_broadcast([2, 512]))\
                            .then_inc(bias_loaded, 16)

                def store_mod(u):
                    pool.wait_ge(modrow_made, u + 1)
                    for j in range(4):
                        g.dma_start(mod_rows[u, :, 512 * j:512 * (j + 1)], modrow[32 * j:32 * j + 2, :])\
                            .then_inc(mod_stored, 16)
                    if u + 1 < DEPTH * ADA_UNITS:
                        load_bias(u + 1)
                    pool.wait_ge(mod_stored, 64 * (u + 1))

                def row(u, kind, h):
                    return mod_rows[u, kind:kind + 1, D * h:D * (h + 1)].to_broadcast([P, D])

                def load_sb(n):
                    l, s = divmod(n, 2)
                    base = ADA_UNITS * l
                    where = ((base, 0), (base, 1)) if s == 0 else ((base + 1, 1), (base + 2, 0))
                    for kind in range(2):
                        for b in range(2):
                            g.dma_start(modsb[:, kind, b, :], row(where[b][0], kind, where[b][1])).then_inc(mod_loaded, 16)
                    w = (attn_norm, ffn_norm)[s]
                    g.dma_start(nw[:], w[l:l + 1, :].to_broadcast([P, D])).then_inc(mod_loaded, 16)

                def load_gate(l, s):
                    u, h = ((ADA_UNITS * l + 1, 0), (ADA_UNITS * l + 2, 1))[s]
                    for kind in range(2):
                        g.dma_start(modg[:, kind, :], row(u, kind, h)).then_inc(gate_loaded, 16)

                def rstd(dst, src, scale, ready, val, out):
                    pool.wait_ge(ready, val)
                    link(g.tensor_scalar(src, src, scale, EPS, ALU.mult, ALU.add))
                    w = src.shape[-1]
                    g.tensor_tensor(dst, src, half[:, 0:w], ALU.pow).then_inc(out, 1)

                def norm_rstd(n):
                    for t in range(NT):
                        rstd(pstat[:, t:t + 1], stat[:, t:t + 1], 1.0 / D, ss_made, NT * n + t + 1, rstd_made)

                def rope(view, cosn, sinn, t, nh, dim, tmp, done):
                    w = dim // 4
                    cs = cst(cosn)[:, (t - 1) * dim:t * dim].unsqueeze(1).to_broadcast([P, nh, dim])
                    sn = cst(sinn)[:, (t - 1) * dim:t * dim].rearrange("p (g s w) -> p g s w", g=2, s=2)
                    t1 = tmp[:, 0, 0:nh * dim].rearrange("p (h d) -> p h d", h=nh)
                    t2 = tmp[:, 1, 0:nh * dim].rearrange("p (h g s w) -> p h g s w", h=nh, g=2, s=2)
                    v5 = view.rearrange("p h (g s w) -> p h g s w", g=2, s=2)
                    g.tensor_tensor(t1, view, cs, ALU.mult)
                    for gg in range(2):
                        for s in range(2):
                            last = g.tensor_tensor(t2[:, :, gg, s, :], v5[:, :, gg, 1 - s, :],
                                                   sn[:, gg, s, :].unsqueeze(1).to_broadcast([P, nh, w]), ALU.mult)
                    link(last)
                    done(g.tensor_tensor(view, t1, tmp[:, 1, 0:nh * dim].rearrange("p (h d) -> p h d", h=nh), ALU.add))

                pool.wait_ge(setup_dve, 2)
                load_bias(0)
                store_mod(0)
                load_sb(0)
                for l in range(DEPTH):
                    m = mix[l]
                    proj = m["proj"]
                    if l == 1:
                        load_sb(2)
                    g.dma_start(wrow[:, 0:LORA], kv_norm[l:l + 1, :].to_broadcast([P, LORA])).then_inc(wrow_loaded, 16)
                    g.dma_start(wrow[:, LORA:LORA + HD], q_norm[l:l + 1, :].to_broadcast([P, HD])).then_inc(wrow_loaded, 16)
                    g.dma_start(wrow[:, LORA + HD:], k_norm[l:l + 1, :].to_broadcast([P, HD])).then_inc(wrow_loaded, 16)
                    norm_rstd(2 * l)
                    pool.wait_ge(htok_made, NT * 2 * l + NT)
                    g.dma_start(S0, state_ret[0, l].rearrange("a h d e -> d a h e")).then_inc(s0_loaded, 16)
                    for t in range(NT):
                        rstd(pstat[:, 8 + t:9 + t], stat[:, 8 + t:9 + t], 1.0 / LORA, ckv_ss, NT * l + t + 1, ckv_rstd)
                    pool.wait_ge(ckv_made, NT * l + 1)
                    g.dma_start(new_ckv[0, l], proj[:, 0, CKV:CKV + LORA]).then_inc(cache_stored, 16)
                    pool.wait_ge(proj_made, NB * NT * l + NT * 2)
                    g.dma_start(new_krope[0, l], proj[:, 0, KRP:KRP + ROPE]).then_inc(cache_stored, 16)
                    for part, pos in ((QR, 4), (KR, 6)):
                        pool.wait_ge(proj_made, NB * NT * l + NT * pos)
                        for t in (1, 2):
                            v = proj[:, t, part:part + RH * RD].rearrange("p (h d) -> p h d", h=RH)
                            rope(v, "cosr", "sinr", t, RH, RD, m["rt"], lambda i: (link(i)))
                    store_mod(ADA_UNITS * l + 1)
                    load_gate(l, 0)
                    store_mod(ADA_UNITS * l + 2)
                    barrier()
                    for t in range(NT):
                        rstd(pstat[:, 16 + 4 * t:20 + 4 * t], stat[:, 16 + 4 * t:20 + 4 * t], 1.0 / RD, ro_ss,
                             NT * l + t + 1, ro_rstd)
                    pool.wait_ge(st_made, 4 * l + 2)
                    for d in range(2):
                        g.dma_start(new_state[0, l, d].rearrange("h d e -> d h e"), m["st"][:, d]).then_inc(state_stored, 16)
                    pool.wait_ge(state_stored, 32 * (l + 1))
                    barrier()
                    g.dma_start(m["cc"][:], cache_ckv[0, l]).then_inc(ckvc_loaded, 16)
                    g.dma_start(m["kpe"][:], cache_krope[0, l]).then_inc(ckvc_loaded, 16)
                    pool.wait_ge(ckvc_loaded, 32 * (l + 1))
                    for kt in range(4):
                        src = m["kpe"][:, :] if kt == 1 else proj[:, (0, 1, 1, 2)[kt], KRP:KRP + ROPE]
                        g.tensor_copy(m["kcat"][:, kt, :, NOPE:HD], src.unsqueeze(1).to_broadcast([P, HEADS, ROPE]))\
                            .then_inc(kpe_made, 1)
                    for i in range(7):
                        o = 32 + 8 * i
                        rstd(pstat[:, o:o + 8], pstat[:, o:o + 8], 1.0 / HD, qk_ss, 7 * l + i + 1, qk_rstd)
                    for i in (1, 2, 5, 6):
                        pool.wait_ge(qk_made, 7 * l + i + 1)
                        if i < 3:
                            v = proj[:, i, Q:Q + HEADS * HD].rearrange("p (h d) -> p h d", h=HEADS)[:, :, NOPE:HD]
                            t = i
                        else:
                            v = m["kcat"][:, i - 3, :, NOPE:HD]
                            t = i - 4
                        rope(v, "cosm", "sinm", t, HEADS, ROPE, m["rt2"], lambda ins: ins.then_inc(qk_rope, 1))
                        pool.wait_ge(qk_rope, 4 * l + (1, 2, 5, 6).index(i) + 1)
                    if l == 0:
                        store_mod(ADA_UNITS)
                    barrier()
                    load_sb(2 * l + 1)
                    barrier()
                    load_gate(l, 1)
                    if l == 1:
                        g.dma_start(moe["wr"][:], w_router[0].rearrange("(k p) n -> p k n", p=P)).then_inc(wr_loaded, 16)
                    norm_rstd(2 * l + 1)
                    barrier()
                for t in range(NT):
                    pool.wait_ge(x2_made, NT + t + 1)
                    dst = y_prompt[0] if t == 0 else y_sample[0, P * (t - 1):P * t, :]
                    g.dma_start(dst, x[:, t, :]).then_inc(y_stored, 16)
                pool.wait_ge(y_stored, 16 * NT)
                pool.wait_ge(cache_stored, 32 * DEPTH)
                pool.wait_ge(state_stored, 32 * DEPTH)

            @block.scalar
            def _(act):
                s = nc.scalar
                phase = [0]
                nxt = [0]

                def barrier():
                    phase[0] += 1
                    s.drain().then_inc(act_phase, 1)
                    for q in (pe_phase, pool_phase, dve_phase):
                        act.wait_ge(q, phase[0])

                def split_to(m):
                    while nxt[0] <= m and nxt[0] < len(splits):
                        q = splits[nxt[0]]
                        raw_wait(act, q["n"])
                        if pre_free(q["m"]):
                            act.wait_ge(*pre_free(q["m"]))
                        z = q["size"]
                        s.activation(whi[:, q["m"] % RING, 0:z], raw[:, q["n"] % RING, 0:z], ACT.Copy).then_inc(hi_made, 1)
                        nxt[0] += 1

                act.wait_ge(setup_dma, 48)
                act.wait_ge(setup_dve, 1)
                for v in range(2):
                    s.activation(cT[:, :, v:v + 1].rearrange("p k o -> p (k o)"), craw[:, v, :], ACT.Silu).then_inc(setup_act, 1)
                act.wait_ge(decay_loaded, 16)
                s.activation(lgt[:, 1, :], lgt[:, 0, :], ACT.Abs).then_inc(act_chain, 1)
                act.wait_ge(act_chain, 1)
                s.activation(lgt[:, 1, :], lgt[:, 1, :], ACT.Exp, scale=-1.0).then_inc(act_chain, 1)
                act.wait_ge(act_chain, 2)
                s.activation(lgt[:, 1, :], lgt[:, 1, :], ACT.Ln, bias=1.0).then_inc(setup_act, 1)

                def norm(n, m):
                    def square(t):
                        if t == 0 and n == 0:
                            act.wait_ge(x_loaded, 32)
                        if t >= 2:
                            act.wait_ge(hT_psum, NT * n + t - 1)
                            if n == 3:
                                act.wait_ge(htl_made, t - 1)
                        s.activation(m["htok"][:, t % 2, :], x[:, t, :], ACT.Square,
                                     accum_out=stat[:, t:t + 1]).then_inc(ss_made, 1)
                    square(0)
                    square(1)
                    for t in range(NT):
                        if n == 3:
                            act.wait_ge(htok_made, NT * n + t + 1)
                            s.activation(moe["hth"][:, t, :], m["htok"][:, t % 2, :], ACT.Copy).then_inc(hth_made, 1)
                        act.wait_ge(hT_psum, NT * n + t + 1)
                        for b in range(2):
                            s.activation(m["hTh"][:, 4 * b:4 * b + 4, P * t:P * (t + 1)],
                                         psum[2 * t + b][:].rearrange("p (c i) -> p c i", c=4), ACT.Copy)\
                                .then_inc(hT_hi_made, 1)
                        if t == 0:
                            square(2)

                for l in range(DEPTH):
                    m = mix[l]
                    proj = m["proj"]
                    norm(2 * l, m)
                    for p in range(NB):
                        split_to(min(IN[l, p]["m"] + 2, UKV[l]["m"]))
                        c0 = IN_ORDER[p] * BLK
                        wd = min(BLK, IN_COLS - c0)
                        for t in range(NT):
                            act.wait_ge(proj_psum, NB * NT * l + NT * p + t + 1)
                            s.activation(proj[:, t, c0:c0 + wd], psum[3 * (p % 2) + t][:, 0:wd], ACT.Copy).then_inc(proj_made, 1)
                        if p == 1:
                            act.wait_ge(proj_made, NB * NT * l + NT * 2)
                            for t in range(NT):
                                if t:
                                    act.wait_ge(ckv_ss, NT * l + t)
                                s.activation(m["sq"][:], proj[:, t, CKV:CKV + LORA], ACT.Square,
                                             accum_out=stat[:, 8 + t:9 + t]).then_inc(ckv_ss, 1)
                        if p == 2:
                            act.wait_ge(dec_arg, l + 1)
                            s.activation(sbflat[:, 0:1024], sbflat[:, 0:1024], ACT.Exp).then_inc(dec_exp, 1)
                            s.activation(sbflat[:, 1024:2048], sbflat[:, 1024:2048], ACT.Exp).then_inc(dec_exp, 1)
                            s.activation(dec[:], dec[:], ACT.Exp).then_inc(dec_exp, 1)
                        if p == 10:
                            act.wait_ge(proj_made, NB * NT * l + NT * 10)
                            for t in range(NT):
                                s.activation(proj[:, t, GG:GG + 512], proj[:, t, GG:GG + 512], ACT.Silu).then_inc(silu_g, 1)
                    split_to(UKV[l]["m"])
                    barrier()
                    for t in range(NT):
                        act.wait_ge(rT_psum, 2 * NT * l + 2 * t + 1)
                        s.activation(m["qrT"][:, t], psum[2 * t][:].rearrange("p (h i) -> p h i", h=RH), ACT.Copy).then_inc(rT_made, 1)
                    for t in range(NT):
                        act.wait_ge(ro_psum, NT * l + t + 1)
                        s.activation(m["at"][:, t].rearrange("p h i -> p (h i)"), psum[t][:], ACT.Square).then_inc(ro_sq, 1)
                    barrier()
                    for b in range(2):
                        act.wait_ge(ckvT_psum, 2 * l + b + 1)
                        s.activation(m["cTh"][:, :, 256 * b:256 * (b + 1)],
                                     psum[b][:].rearrange("p (k i) -> p k i", k=2), ACT.Copy).then_inc(ckvT_hi, 1)
                    for kt in range(4):
                        for hb in range(2):
                            act.wait_ge(ukv_psum, 8 * l + 2 * kt + hb + 1)
                            src = psum[2 + 2 * (kt % 2) + hb][:].rearrange("p (h e) -> p h e", h=4)
                            s.activation(m["kcat"][:, kt, 4 * hb:4 * hb + 4, 0:NOPE], src[:, :, 0:NOPE], ACT.Copy).then_inc(kv_made, 1)
                            s.activation(m["v"][:, kt, 4 * hb:4 * hb + 4, :], src[:, :, NOPE:NOPE + VD], ACT.Copy).then_inc(kv_made, 1)
                    if l == 1:
                        split_to(OUT[l, 0]["m"] + 1)
                    for i in range(7):
                        act.wait_ge(hT2_psum, 14 * l + 2 * i + 1)
                        dst = m["qT"][:, 0:4, P * (i - 4):P * (i - 3)] if i >= 4 else kT[:, 0:4, P * i:P * (i + 1)]
                        s.activation(dst, psum[2 * (i % 3)][0:HD, :].rearrange("p (h i) -> p h i", h=4), ACT.Copy).then_inc(headT_lo, 1)
                    for v in range(24):
                        t = v // HEADS
                        nk = P if t == 0 else 3 * P
                        act.wait_ge(negmax, 24 * l + v + 1)
                        if v >= 2:
                            act.wait_ge(pT_psum, 24 * l + v - 1)
                        s.activation(proj[:, v % 2, KR:KR + nk], psum[v % 2][:, 0:nk], ACT.Exp,
                                     bias=stat[:, 32 + v:33 + v], accum_out=pstat[:, 96 + v:97 + v]).then_inc(exp_made, 1)
                    split_to(OUT[l, 0]["m"] + 1)
                    barrier()
                    for t in range(NT):
                        act.wait_ge(mT_psum, NT * l + t + 1)
                        for b in range(2):
                            s.activation(m["mTh"][:, 4 * b:4 * b + 4, P * t:P * (t + 1)],
                                         psum[2 * t + b][:].rearrange("p (c i) -> p c i", c=4), ACT.Copy).then_inc(mT_hi, 1)
                    split_to(OUT[l, 3]["m"] + (2 if l == 0 else 0))
                    if l == 1:
                        for k in range(2):
                            expert_hi(act, s, 0, k, static=True)
                    barrier()
                    norm(2 * l + 1, (ffn, moe)[l])
                    if l == 0:
                        def dense_split(off, it):
                            n0, m0 = DN + off, DM + off
                            raw_wait(act, n0, it)
                            act.wait_ge(*dense_free(off, it))
                            s.activation(whi[:, m0 % RING, :], raw[:, n0 % RING, :], ACT.Copy).then_inc(hi_made, 1)

                        def dense_evac(i, par):
                            for ft in range(2):
                                act.wait_ge(gate_done, 2 * i + ft + 1)
                                s.activation(ffn["sg"][:, ft, :], psum[6][:, 0:TOK], ACT.Silu).then_inc(gate_silu, 1)
                                act.wait_ge(act_made, 2 * i + ft + 1)
                                s.activation(ffn["acth"][:, par, ft, :], ffn["act"][:, ft, :], ACT.Copy).then_inc(acth_made, 1)

                        dense_evac(0, 0)
                        with act.Fori(0, (DENSE - 1) // 2) as b:
                            for h in range(2):
                                i = 2 * b + h
                                dense_split(2, i)
                                dense_split(3, i)
                                dense_split(4, i)
                                dense_evac(2 * b + (h + 1), (h + 1) % 2)
                        dense_split(5, DENSE - 2)
                        nxt[0] = DM + 3 * DENSE
                        split_to(IN[1, 0]["m"] + 1)
                        barrier()
                    else:
                        act.wait_ge(wr_loaded, 16)
                        s.activation(moe["wrh"][:], moe["wr"][:], ACT.Copy).then_inc(wr_hi, 1)
                        act.wait_ge(route_made, 1)
                        s.activation(moe["r"][:, 1, :, 0:1], moe["r"][:, 1, :, 0:1], ACT.Exp).then_inc(lg_exp, 1)
                        barrier()
                        act_expert = make_act_expert(act, s)
                        act_gather(act, s, 0)
                        with act.Fori(0, EXPERTS - 1) as e:
                            act_expert(e, True)
                        act_expert(EXPERTS - 1, False)

                        def item(e, qi, r):
                            act_gather(act, s, r)
                            for k in range(2):
                                expert_hi(act, s, r, k)
                            act_expert(r, False)
                        overflow(act, s, item)

            @block.vector
            def _(dve):
                v = nc.vector
                phase = [0]
                nxt = [0]
                chain = [0]

                def link(ins):
                    chain[0] += 1
                    ins.then_inc(dve_chain, 1)
                    dve.wait_ge(dve_chain, chain[0])

                def barrier():
                    phase[0] += 1
                    v.drain().then_inc(dve_phase, 1)
                    for q in (pe_phase, pool_phase, act_phase):
                        dve.wait_ge(q, phase[0])

                def split_to(m):
                    while nxt[0] <= m and nxt[0] < len(splits):
                        q = splits[nxt[0]]
                        dve.wait_ge(hi_made, q["m"] + 1)
                        z = q["size"]
                        v.tensor_tensor(wlo[:, q["m"] % RING, 0:z], raw[:, q["n"] % RING, 0:z],
                                        whi[:, q["m"] % RING, 0:z].bitcast(f32), ALU.subtract).then_inc(lo_made, 1)
                        nxt[0] += 1

                v.memset(cT[:], 0.0).then_inc(setup_dve, 1)
                v.memset(brow[:], 0.0).then_inc(setup_dve, 1)
                dve.wait_ge(setup_act, 3)
                link(v.tensor_scalar(lg[:].rearrange("p l d -> p (l d)"), lgt[:, 0, :], 0.0, None, ALU.min))
                link(v.tensor_tensor(lg[:].rearrange("p l d -> p (l d)"), lg[:].rearrange("p l d -> p (l d)"), lgt[:, 1, :],
                                     ALU.subtract))

                def make_modrow(u):
                    dve.wait_ge(ada_used, DK * (u + 1))
                    dve.wait_ge(bias_loaded, 64 * (u + 1))
                    if u:
                        dve.wait_ge(mod_stored, 64 * u)
                    v.tensor_tensor(modrow[:], psum[6 + u % 2][:], brow[:], ALU.add).then_inc(modrow_made, 1)

                def make_scale(n):
                    dve.wait_ge(mod_loaded, 80 * (n + 1))
                    for kind in range(2):
                        last = v.scalar_tensor_tensor(out=modsb[:, kind, 1, :], in0=modsb[:, kind, 1, :], scalar=1.0,
                                                      in1=nw[:], op0=ALU.add, op1=ALU.mult)
                    link(last)

                def norm(n, m, after0=None):
                    for t in range(NT):
                        h = m["htok"][:, t % 2, :]
                        dve.wait_ge(rstd_made, NT * n + t + 1)
                        link(v.scalar_tensor_tensor(out=h, in0=x[:, t, :], scalar=pstat[:, t:t + 1],
                                                    in1=modsb[:, KIND[t], 1, :], op0=ALU.mult, op1=ALU.mult))
                        v.tensor_tensor(h, h, modsb[:, KIND[t], 0, :], ALU.add).then_inc(htok_made, 1)
                        if n == 3:
                            dve.wait_ge(hth_made, t + 1)
                            v.tensor_tensor(moe["htl"][:, t, :], h, moe["hth"][:, t, :].bitcast(f32),
                                            ALU.subtract).then_inc(htl_made, 1)
                        if t == 0 and after0:
                            after0()
                        for b in range(2):
                            dve.wait_ge(hT_hi_made, 2 * NT * n + 2 * t + b + 1)
                            c = slice(4 * b, 4 * b + 4)
                            v.tensor_tensor(m["hTl"][:, c, P * t:P * (t + 1)],
                                            psum[2 * t + b][:].rearrange("p (c i) -> p c i", c=4),
                                            m["hTh"][:, c, P * t:P * (t + 1)].bitcast(f32), ALU.subtract).then_inc(hT_made, 1)

                make_modrow(0)
                for l in range(DEPTH):
                    m = mix[l]
                    proj = m["proj"]
                    make_scale(2 * l)
                    norm(2 * l, m)
                    dve.wait_ge(htok_made, NT * (2 * l + 1))
                    lgl = lg[:, l, :]
                    lgb = lgl.rearrange("p (d h) -> p d h", d=2).unsqueeze(3).to_broadcast([P, 2, RH, P])

                    def rows(name):
                        return cst(name).rearrange("p (d i) -> p d i", d=2).unsqueeze(2).to_broadcast([P, 2, RH, P])
                    v.tensor_scalar(dec[:, 1, :], lgl, float(P), None, ALU.mult)
                    v.tensor_tensor(dec[:, 0, :].rearrange("p (d h) -> p d h", d=2), lgl.rearrange("p (d h) -> p d h", d=2),
                                    cst("kexp").unsqueeze(2).to_broadcast([P, 2, RH]), ALU.mult)
                    for d in range(2):
                        lb = lgl[:, RH * d:RH * (d + 1)].unsqueeze(2).to_broadcast([P, RH, P])
                        v.tensor_tensor(qdec[:, d], cst("qexp")[:, P * d:P * (d + 1)].unsqueeze(1).to_broadcast([P, RH, P]), lb, ALU.mult)
                        last = v.tensor_tensor(mtmp[:, d], cst("dexp")[:, P * d:P * (d + 1)].unsqueeze(1).to_broadcast([P, RH, P]), lb, ALU.mult)
                    last.then_inc(dec_arg, 1)
                    for p in range(NB):
                        split_to(min(IN[l, p]["m"] + 2, UKV[l]["m"]))
                        if p == 3:
                            dve.wait_ge(wrow_loaded, 48 * (l + 1))
                            for t in range(NT):
                                dve.wait_ge(ckv_rstd, NT * l + t + 1)
                                ck = proj[:, t, CKV:CKV + LORA]
                                v.scalar_tensor_tensor(out=ck, in0=ck, scalar=pstat[:, 8 + t:9 + t], in1=wrow[:, 0:LORA],
                                                       op0=ALU.mult, op1=ALU.mult).then_inc(ckv_made, 1)
                        if p == 4:
                            dve.wait_ge(dec_exp, 3 * (l + 1))
                            for d in range(2):
                                last = v.tensor_tensor(mtmp[:, d], mtmp[:, d],
                                                       cst("tri")[:, P * d:P * (d + 1)].unsqueeze(1).to_broadcast([P, RH, P]), ALU.mult)
                            v.tensor_scalar(dec[:, 0, :], dec[:, 0, :], RD ** -0.5, None, ALU.mult)
                            link(last)
                            link(v.tensor_tensor(maskT, maskT, mtmp[:, 1], ALU.add))
                        if p == 7:
                            make_modrow(ADA_UNITS * l + 1)
                    make_modrow(ADA_UNITS * l + 2)
                    split_to(UKV[l]["m"])
                    barrier()
                    for i, (t, d) in enumerate(((0, 0), (0, 1), (1, 0), (2, 1))):
                        kr = proj[:, t, KR:KR + RH * RD].rearrange("p (h e) -> p h e", h=RH)
                        v.tensor_tensor(m["kd"][:, i], kr, dec[:, 0, RH * d:RH * (d + 1)].unsqueeze(2).to_broadcast([P, RH, RD]),
                                        ALU.mult).then_inc(kd_made, 1)
                    for t in range(NT):
                        dve.wait_ge(rT_psum, 2 * NT * l + 2 * t + 2)
                        v.tensor_scalar(m["krT"][:, t], psum[2 * t + 1][:].rearrange("p (h i) -> p h i", h=RH), RD ** -0.5, None,
                                        ALU.mult).then_inc(qd_made, 1)
                        if t:
                            dve.wait_ge(rT_made, NT * l + t + 1)
                            for d in range(2):
                                v.tensor_tensor(m["qd"][:, 2 * (t - 1) + d], m["qrT"][:, t], qdec[:, d], ALU.mult).then_inc(qd_made, 1)
                    for t in range(NT):
                        dve.wait_ge(sc_psum, NT * l + t + 1)
                        v.tensor_tensor(m["at"][:, t], psum[t][:].rearrange("p (h i) -> p h i", h=RH), maskT, ALU.mult).then_inc(sc_masked, 1)
                    dve.wait_ge(s0_loaded, 16 * (l + 1))
                    for i in range(4):
                        dve.wait_ge(st_psum, 4 * l + i + 1)
                        up = psum[3 + i % 3][:].rearrange("p (h e) -> p h e", h=RH)
                        if i < 2:
                            v.tensor_copy(m["st"][:, i], up).then_inc(st_made, 1)
                        else:
                            d = i - 2
                            link(v.tensor_tensor(S1[:, d], S0[:, d], dec[:, 1, RH * d:RH * (d + 1)].unsqueeze(2).to_broadcast([P, RH, RD]), ALU.mult))
                            v.tensor_tensor(S1[:, d], S1[:, d], up, ALU.add).then_inc(st_made, 1)
                    for t in range(NT):
                        dve.wait_ge(ro_sq, NT * l + t + 1)
                        v.tensor_reduce(stat[:, 16 + 4 * t:20 + 4 * t], m["at"][:, t], axis=AX.X, op=ALU.add).then_inc(ro_ss, 1)
                    for t in range(NT):
                        dve.wait_ge(ro_rstd, NT * l + t + 1)
                        dst = proj[:, t, QR:QR + RH * RD].rearrange("p (h e) -> p h e", h=RH)
                        link(v.tensor_tensor(dst, psum[t][:].rearrange("p (h e) -> p h e", h=RH),
                                             pstat[:, 16 + 4 * t:20 + 4 * t].unsqueeze(2).to_broadcast([P, RH, RD]), ALU.mult))
                        dve.wait_ge(silu_g, NT * l + t + 1)
                        v.tensor_tensor(proj[:, t, QR:QR + 512], proj[:, t, QR:QR + 512], proj[:, t, GG:GG + 512],
                                        ALU.mult).then_inc(ro_made, 1)
                    barrier()
                    def head_norm(i):
                        if i < 3:
                            src = proj[:, i, Q:Q + HEADS * HD].rearrange("p (h d) -> p h d", h=HEADS)
                            w = wrow[:, LORA:LORA + HD]
                        else:
                            src = m["kcat"][:, i - 3]
                            w = wrow[:, LORA + HD:]
                        return src, w

                    def head_ss(i):
                        src, _ = head_norm(i)
                        tmp = proj[:, i % 3, KR:KR + HEADS * HD].rearrange("p (h d) -> p h d", h=HEADS)
                        link(v.tensor_tensor(tmp, src, src, ALU.mult))
                        v.tensor_reduce(pstat[:, 32 + 8 * i:40 + 8 * i], tmp, axis=AX.X, op=ALU.add).then_inc(qk_ss, 1)

                    def head_scale(i):
                        src, w = head_norm(i)
                        dve.wait_ge(qk_rstd, 7 * l + i + 1)
                        link(v.tensor_tensor(src, src, pstat[:, 32 + 8 * i:40 + 8 * i].unsqueeze(2).to_broadcast([P, HEADS, HD]), ALU.mult))
                        v.tensor_tensor(src, src, w.unsqueeze(1).to_broadcast([P, HEADS, HD]), ALU.mult).then_inc(qk_made, 1)

                    for b in range(2):
                        dve.wait_ge(ckvT_hi, 2 * l + b + 1)
                        v.tensor_tensor(m["cTl"][:, :, 256 * b:256 * (b + 1)], psum[b][:].rearrange("p (k i) -> p k i", k=2),
                                        m["cTh"][:, :, 256 * b:256 * (b + 1)].bitcast(f32), ALU.subtract).then_inc(ckvT_made, 1)
                    link(v.tensor_scalar(wrow[:, LORA:LORA + HD], wrow[:, LORA:LORA + HD], HD ** -0.5, None, ALU.mult))
                    for i in range(3):
                        head_ss(i)
                    for i in range(3):
                        head_scale(i)
                    for i in range(3, 7):
                        dve.wait_ge(kv_made, 16 * l + 4 * (i - 2))
                        dve.wait_ge(kpe_made, 4 * l + i - 2)
                        head_ss(i)
                    for i in range(3, 7):
                        head_scale(i)
                    if l == 1:
                        split_to(OUT[l, 0]["m"] + 1)
                    for i in range(7):
                        dve.wait_ge(hT2_psum, 14 * l + 2 * i + 2)
                        dst = m["qT"][:, 4:8, P * (i - 4):P * (i - 3)] if i >= 4 else kT[:, 4:8, P * i:P * (i + 1)]
                        v.tensor_copy(dst, psum[2 * (i % 3) + 1][0:HD, :].rearrange("p (h i) -> p h i", h=4)).then_inc(headT_hi, 1)

                    def row_max(u):
                        nk = P if u < HEADS else 3 * P
                        dve.wait_ge(s_psum, 24 * l + u + 1)
                        v.tensor_reduce(stat[:, 32 + u:33 + u], psum[u % 2][:, 0:nk], axis=AX.X, op=ALU.max, negate=True)\
                            .then_inc(negmax, 1)

                    row_max(0)
                    row_max(1)
                    for u in range(24):
                        t, h = divmod(u, HEADS)
                        nk = P if t == 0 else 3 * P
                        dve.wait_ge(pT_psum, 24 * l + u + 1)
                        if u >= 2:
                            dve.wait_ge(pv_psum, 24 * l + u - 1)
                        v.tensor_copy(m["pT"][:, u % 2, 0:nk], psum[2 + u % 2][:, 0:nk]).then_inc(pT_made, 1)
                        if u + 2 < 24:
                            row_max(u + 2)
                        if h == HEADS - 1:
                            o = 96 + HEADS * t
                            dve.wait_ge(exp_made, 24 * l + u + 1)
                            link(v.reciprocal(pstat[:, o:o + 8], pstat[:, o:o + 8]))
                            dve.wait_ge(pv_psum, 24 * l + u + 1)
                            v.tensor_tensor(proj[:, t, Q:Q + 512].rearrange("p (h e) -> p h e", h=HEADS),
                                            psum[4 + t % 2][:].rearrange("p (h e) -> p h e", h=HEADS),
                                            pstat[:, o:o + 8].unsqueeze(2).to_broadcast([P, HEADS, VD]), ALU.mult).then_inc(a_made, 1)
                    if l == 0:
                        make_modrow(ADA_UNITS)
                    split_to(OUT[l, 0]["m"] + 1)
                    barrier()
                    for t in range(NT):
                        for b in range(2):
                            dve.wait_ge(mT_hi, 2 * NT * l + 2 * t + b + 1)
                            c = slice(4 * b, 4 * b + 4)
                            v.tensor_tensor(m["mTl"][:, c, P * t:P * (t + 1)], psum[2 * t + b][:].rearrange("p (c i) -> p c i", c=4),
                                            m["mTh"][:, c, P * t:P * (t + 1)].bitcast(f32), ALU.subtract).then_inc(mT_made, 1)
                    make_scale(2 * l + 1)
                    dve.wait_ge(gate_loaded, 32 * (2 * l + 1))
                    for j in range(4):
                        split_to(OUT[l, j]["m"] + 2 if l == 0 else min(OUT[l, j]["m"] + 2, MM - 1))
                        for t in range(NT):
                            dve.wait_ge(out_psum, 12 * l + 3 * j + t + 1)
                            cs = slice(BLK * j, BLK * (j + 1))
                            n = 3 * j + t
                            if n >= 2:
                                dve.wait_ge(x1_made, 12 * l + n - 1)
                            link(v.tensor_tensor(m["tmp"][:, n % 2, :], psum[3 * (j % 2) + t][:, 0:BLK], modg[:, KIND[t], cs], ALU.mult))
                            v.tensor_tensor(x[:, t, cs], x[:, t, cs], m["tmp"][:, n % 2, :], ALU.add).then_inc(x1_made, 1)
                    if l == 1:
                        for k in range(2):
                            expert_lo(dve, v, 0, k)
                    barrier()
                    norm(2 * l + 1, (ffn, moe)[l])
                    if l == 0:
                        def dense_split(off, it):
                            n0, m0 = DN + off, DM + off
                            dve.wait_ge(hi_made, m0 + 1 + 3 * it)
                            v.tensor_tensor(wlo[:, m0 % RING, :], raw[:, n0 % RING, :], whi[:, m0 % RING, :].bitcast(f32),
                                            ALU.subtract).then_inc(lo_made, 1)

                        def dense_evac(i, par):
                            for ft in range(2):
                                dve.wait_ge(gate_silu, 2 * i + ft + 1)
                                dve.wait_ge(up_done, 2 * i + ft + 1)
                                v.tensor_tensor(ffn["act"][:, ft, :], psum[7][:, 0:TOK], ffn["sg"][:, ft, :], ALU.mult).then_inc(act_made, 1)
                                dve.wait_ge(acth_made, 2 * i + ft + 1)
                                v.tensor_tensor(ffn["actl"][:, par, ft, :], ffn["act"][:, ft, :],
                                                ffn["acth"][:, par, ft, :].bitcast(f32), ALU.subtract).then_inc(actl_made, 1)

                        dense_evac(0, 0)
                        with dve.Fori(0, (DENSE - 1) // 2) as b:
                            for h in range(2):
                                i = 2 * b + h
                                dense_split(2, i)
                                dense_split(3, i)
                                dense_split(4, i)
                                dense_evac(2 * b + (h + 1), (h + 1) % 2)
                        dense_split(5, DENSE - 2)
                        nxt[0] = DM + 3 * DENSE
                        split_to(IN[1, 0]["m"] + 1)
                        dve.wait_ge(gate_loaded, 64)
                        for t in range(NT):
                            if t:
                                dve.wait_ge(x2_made, t)
                            for hf in range(2):
                                dve.wait_ge(down_done, DENSE + 1)
                                cs = slice(512 * hf, 512 * (hf + 1))
                                link(v.tensor_tensor(ffn["tmp"][:, hf, :], psum[2 * t + hf][:], modg[:, KIND[t], cs], ALU.mult))
                                last = v.tensor_tensor(x[:, t, cs], x[:, t, cs], ffn["tmp"][:, hf, :], ALU.add)
                            last.then_inc(x2_made, 1)
                        barrier()
                    else:
                        dve_moe(dve, v, link, barrier)

            @block.tensor
            def _(pe):
                mm = nc.tensor.matmul
                phase = [0]
                ada = [0]

                def barrier():
                    phase[0] += 1
                    nc.tensor.drain().then_inc(pe_phase, 1)
                    for q in (act_phase, pool_phase, dve_phase):
                        pe.wait_ge(q, phase[0])

                def mm3(out, ah, al, bh, bl, first, last):
                    mm(out, ah, bh, start=first, stop=False)
                    mm(out, ah, bl, start=False, stop=False)
                    return mm(out, al, bh, start=False, stop=last)

                def ada_chunk():
                    a = ada[0]
                    q = [z for z in chunks if z["m"] is None][a]
                    u, k = divmod(a, DK)
                    raw_wait(pe, q["n"])
                    if k == 0 and u >= 2:
                        pe.wait_ge(modrow_made, u - 1)
                    for j in range(4):
                        last = mm(psum[6 + u % 2][32 * j:32 * j + 32, :], cT[:, k, :], raw[:, q["n"] % RING, 512 * j:512 * (j + 1)],
                                  start=(k == 0), stop=(k == DK - 1))
                    last.then_inc(ada_used, 1)
                    ada[0] += 1

                def norm(n, m):
                    for t in range(NT):
                        pe.wait_ge(htok_made, NT * n + t + 1)
                        for c_ in range(DK):
                            last = nc.tensor.transpose(psum[2 * t + c_ // 4][:, P * (c_ % 4):P * (c_ % 4 + 1)],
                                                       m["htok"][:, t % 2, P * c_:P * (c_ + 1)], ident)
                        last.then_inc(hT_psum, 1)

                pe.wait_ge(setup_act, 2)
                pe.wait_ge(setup_dve, 2)
                for k in range(DK):
                    ada_chunk()
                for l in range(DEPTH):
                    m = mix[l]
                    proj = m["proj"]
                    norm(2 * l, m)
                    for p in range(NB):
                        q = IN[l, p]
                        wd = q["shape"]
                        pe.wait_ge(lo_made, q["m"] + 1)
                        wh = whi[:, q["m"] % RING, 0:q["size"]].rearrange("p (k n) -> p k n", n=wd)
                        wl = wlo[:, q["m"] % RING, 0:q["size"]].rearrange("p (k n) -> p k n", n=wd)
                        for t in range(NT):
                            if p == 0:
                                pe.wait_ge(hT_made, 2 * NT * 2 * l + 2 * (t + 1))
                            if p >= 2:
                                pe.wait_ge(proj_made, NB * NT * l + NT * (p - 2) + t + 1)
                            ts = slice(P * t, P * (t + 1))
                            for k in range(DK):
                                last = mm3(psum[3 * (p % 2) + t][:, 0:wd], m["hTh"][:, k, ts], m["hTl"][:, k, ts],
                                           wh[:, k, :], wl[:, k, :], k == 0, k == DK - 1)
                            last.then_inc(proj_psum, 1)
                        for _ in range(ada_extra[p]):
                            ada_chunk()
                    barrier()
                    for t in range(NT):
                        for b, part in enumerate((QR, KR)):
                            for h in range(RH):
                                last = nc.tensor.transpose(psum[2 * t + b][:, P * h:P * (h + 1)],
                                                           proj[:, t, part + RD * h:part + RD * (h + 1)], ident)
                            last.then_inc(rT_psum, 1)
                    for t in range(NT):
                        pe.wait_ge(rT_made, NT * (l + 1))
                        pe.wait_ge(qd_made, 7 * l + (1, 4, 7)[t])
                        for h in range(RH):
                            last = mm(psum[t][:, P * h:P * (h + 1)], m["krT"][:, t, h, :], m["qrT"][:, t, h, :], start=True, stop=True)
                        last.then_inc(sc_psum, 1)
                    pe.wait_ge(qd_made, 7 * (l + 1))
                    for i, t in enumerate((0, 0, 1, 2)):
                        pe.wait_ge(kd_made, 4 * l + i + 1)
                        if i == 3:
                            pe.wait_ge(st_made, 4 * l + 1)
                        for h in range(RH):
                            last = mm(psum[3 + i % 3][:, P * h:P * (h + 1)], m["kd"][:, i, h, :],
                                      proj[:, t, VR + RD * h:VR + RD * (h + 1)], start=True, stop=True)
                        last.then_inc(st_psum, 1)
                    pe.wait_ge(s0_loaded, 16 * (l + 1))
                    for t in range(NT):
                        pe.wait_ge(sc_masked, NT * l + t + 1)
                        if t == 1:
                            pe.wait_ge(st_made, 4 * (l + 1))
                        for h in range(RH):
                            o = psum[t][:, P * h:P * (h + 1)]
                            last = mm(o, m["at"][:, t, h, :], proj[:, t, VR + RD * h:VR + RD * (h + 1)], start=True, stop=(t == 0))
                            if t:
                                sf, sb_ = (S0, S1) if t == 1 else (S1, S0)
                                mm(o, m["qd"][:, 2 * (t - 1), h, :], sf[:, 0, h, :], start=False, stop=False)
                                last = mm(o, m["qd"][:, 2 * (t - 1) + 1, h, :], sb_[:, 1, h, :], start=False, stop=True)
                        last.then_inc(ro_psum, 1)
                    barrier()
                    pe.wait_ge(ckvc_loaded, 32 * (l + 1))
                    for b in range(2):
                        for i in range(2):
                            kt = 2 * b + i
                            src = m["cc"][:, :] if kt == 1 else proj[:, (0, 1, 1, 2)[kt], CKV:CKV + LORA]
                            for k in range(2):
                                last = nc.tensor.transpose(psum[b][:, 256 * k + P * i:256 * k + P * (i + 1)], src[:, P * k:P * (k + 1)], ident)
                        last.then_inc(ckvT_psum, 1)
                    q = UKV[l]
                    pe.wait_ge(lo_made, q["m"] + 1)
                    wh = whi[:, q["m"] % RING, :].rearrange("p (k n) -> p k n", n=1024)
                    wl = wlo[:, q["m"] % RING, :].rearrange("p (k n) -> p k n", n=1024)
                    for kt in range(4):
                        pe.wait_ge(ckvT_made, 2 * l + kt // 2 + 1)
                        ts = slice(P * kt, P * (kt + 1))
                        for hb in range(2):
                            if kt >= 2:
                                pe.wait_ge(kv_made, 16 * l + 4 * (kt - 2) + 2 * hb + 2)
                            for k in range(2):
                                cs = slice(512 * hb, 512 * (hb + 1))
                                last = mm3(psum[2 + 2 * (kt % 2) + hb][:], m["cTh"][:, k, ts], m["cTl"][:, k, ts],
                                           wh[:, k, cs], wl[:, k, cs], k == 0, k == 1)
                            last.then_inc(ukv_psum, 1)
                    pe.wait_ge(kv_made, 16 * (l + 1))
                    for i in range(7):
                        if i < 4:
                            pe.wait_ge(qk_made, 7 * l + 3 + i + 1)
                            if i >= 2:
                                pe.wait_ge(qk_rope, 4 * l + i + 1)
                        elif i > 4:
                            pe.wait_ge(qk_rope, 4 * l + i - 4)
                        for hb in range(2):
                            if i >= 3:
                                pe.wait_ge((headT_lo, headT_hi)[hb], 7 * l + i - 2)
                            for h in range(4):
                                hh = 4 * hb + h
                                src = m["kcat"][:, i, hh, :] if i < 4 else proj[:, i - 4, Q + HD * hh:Q + HD * (hh + 1)]
                                last = nc.tensor.transpose(psum[2 * (i % 3) + hb][0:HD, P * h:P * (h + 1)], src, ident)
                            last.then_inc(hT2_psum, 1)
                    pe.wait_ge(headT_lo, 7 * (l + 1))
                    pe.wait_ge(headT_hi, 7 * (l + 1))

                    def scores(u):
                        t, h = divmod(u, HEADS)
                        if u >= 2:
                            pe.wait_ge(exp_made, 24 * l + u - 1)
                        k0, nk = (0, P) if t == 0 else (P, 3 * P)
                        mm(psum[u % 2][:, 0:nk], m["qT"][:, h, P * t:P * (t + 1)], kT[:, h, k0:k0 + nk], start=True, stop=True)\
                            .then_inc(s_psum, 1)

                    scores(0)
                    scores(1)
                    for u in range(24):
                        t, h = divmod(u, HEADS)
                        n = 1 if t == 0 else 3
                        pe.wait_ge(exp_made, 24 * l + u + 1)
                        if u >= 2:
                            pe.wait_ge(pT_made, 24 * l + u - 1)
                        for i in range(n):
                            last = nc.tensor.transpose(psum[2 + u % 2][:, P * i:P * (i + 1)], proj[:, u % 2, KR + P * i:KR + P * (i + 1)], ident)
                        last.then_inc(pT_psum, 1)
                        if u + 2 < 24:
                            scores(u + 2)
                        if l == 0 and u % 3 == 2:
                            ada_chunk()
                        pe.wait_ge(pT_made, 24 * l + u + 1)
                        if h == 0 and t == 2:
                            pe.wait_ge(a_made, 3 * l + 1)
                        for i in range(n):
                            kt = i + (0 if t == 0 else 1)
                            last = mm(psum[4 + t % 2][:, VD * h:VD * (h + 1)], m["pT"][:, u % 2, P * i:P * (i + 1)],
                                      m["v"][:, kt, h, :], start=(i == 0), stop=(i == n - 1))
                        last.then_inc(pv_psum, 1)
                    barrier()
                    for t in range(NT):
                        for c_ in range(DK):
                            o = Q + P * c_ if c_ < 4 else QR + P * (c_ - 4)
                            last = nc.tensor.transpose(psum[2 * t + c_ // 4][:, P * (c_ % 4):P * (c_ % 4 + 1)], proj[:, t, o:o + P], ident)
                        last.then_inc(mT_psum, 1)
                    for j in range(4):
                        q = OUT[l, j]
                        pe.wait_ge(lo_made, q["m"] + 1)
                        wh = whi[:, q["m"] % RING, :].rearrange("p (k n) -> p k n", n=BLK)
                        wl = wlo[:, q["m"] % RING, :].rearrange("p (k n) -> p k n", n=BLK)
                        for t in range(NT):
                            if j == 0:
                                pe.wait_ge(mT_made, 2 * NT * l + 2 * (t + 1))
                            if j >= 2:
                                pe.wait_ge(x1_made, 12 * l + 3 * (j - 2) + t + 1)
                            ts = slice(P * t, P * (t + 1))
                            for k in range(DK):
                                last = mm3(psum[3 * (j % 2) + t][:, 0:BLK], m["mTh"][:, k, ts], m["mTl"][:, k, ts],
                                           wh[:, k, :], wl[:, k, :], k == 0, k == DK - 1)
                            last.then_inc(out_psum, 1)
                    barrier()
                    norm(2 * l + 1, (ffn, moe)[l])
                    if l == 0:
                        pe_dense(pe, mm)
                        barrier()
                    else:
                        pe_moe(pe, mm, mm3, barrier)



_INS = ["x_prompt", "x_sample", "cache_ckv", "cache_krope", "state_ret", "c", "c_ctx", "attn_norm", "ffn_norm", "w_ada",
        "b_ada", "w_in", "kv_norm", "w_ukv", "q_norm", "k_norm", "decay_logit", "w_out", "w_ffn_gate", "w_ffn_up",
        "w_ffn_down", "w_router", "w_exp_gate", "w_exp_up", "w_exp_down"]
_OUTS = [(1, 128, 1024), (1, 256, 1024), (1, 2, 128, 256), (1, 2, 128, 32), (1, 2, 2, 4, 128, 128)]
GRID_W = 64
ROPE_BASE = 10000.0


def shape_constants():
    import numpy as np

    tab = np.zeros((P, N_CONST), np.float32)

    def put(name, a):
        lo, hi = CONST[name]
        tab[:, lo:hi] = np.asarray(a, np.float32).reshape(P, hi - lo)

    def rotary(dim):
        n = (NT - 1) * P
        half = dim // 2
        freqs = (np.float32(ROPE_BASE) ** (-np.arange(0, half, 2, dtype=np.float32) / np.float32(half))).astype(np.float32)
        tok = np.arange(n)

        def ang(p):
            a = p.astype(np.float32)[:, None] * freqs[None, :]
            return np.concatenate([a, a], -1)
        a = np.concatenate([ang(tok // GRID_W), ang(tok % GRID_W)], -1)
        cos, sin = np.cos(a).astype(np.float32), np.sin(a).astype(np.float32)
        sin = sin.reshape(n, 2, 2, dim // 4).copy()
        sin[:, :, 0] *= -1
        lay = lambda z: z.reshape(NT - 1, P, dim).transpose(1, 0, 2)
        return lay(cos), lay(sin.reshape(n, dim))

    i = np.arange(P)
    put("ident", np.eye(P))
    for tag, dim in (("m", ROPE), ("r", RD)):
        cos, sin = rotary(dim)
        put("cos" + tag, cos)
        put("sin" + tag, sin)
    put("kexp", np.stack([P - 1 - i, i], 1))
    put("qexp", np.broadcast_to(np.stack([i + 1, P - i]), (P, 2, P)))
    d = i[None, :] - i[:, None]
    put("dexp", np.stack([np.maximum(d, 0), np.maximum(-d, 0)], 1))
    put("tri", np.stack([d >= 0, d <= 0], 1))
    put("upper", d > 0)
    put("ones", np.ones((P, P)))
    put("iota", np.broadcast_to(i, (P, P)))
    return tab


def kernel(**inputs):
    import numpy as _np
    import concourse.bacc as _bacc
    from concourse import mybir as _mybir
    from concourse.bass_utils import run_bass_kernel_spmd as _run

    nc = _bacc.Bacc("TRN2", target_bir_lowering=False, num_devices=1)
    arrays, args = {}, []
    for name in _INS:
        a = _np.ascontiguousarray(inputs[name])
        arrays[f"in_{name}"] = a
        args.append(nc.dram_tensor(f"in_{name}", a.shape, _mybir.dt.from_np(a.dtype), kind="ExternalInput").ap())
    tab = shape_constants()
    arrays["in_const"] = tab
    args.append(nc.dram_tensor("in_const", tab.shape, _mybir.dt.float32, kind="ExternalInput").ap())
    for i, shape in enumerate(_OUTS):
        args.append(nc.dram_tensor(f"out_{i}", shape, _mybir.dt.float32, kind="ExternalOutput").ap())
    hybrid_step(nc, *args)
    r = _run(nc, [arrays], core_ids=[0])
    return tuple(r.results[0][f"out_{i}"] for i in range(len(_OUTS)))
```

```python
import concourse.bass as bass
from concourse import mybir
from contextlib import ExitStack

P = 128
D = 1024
DK = D // P
NT = 3
TOK = NT * P
KIND = (0, 1, 1)
DEPTH = 2
HEADS, NOPE, ROPE = 8, 64, 32
HD = NOPE + ROPE
VD = 64
LORA = 256
RH, RD = 4, 128
Q, CKV, KRP, QR, KR, VR, GG = 0, 768, 1024, 1056, 1568, 2080, 2592
IN_COLS = 3104
FF, EFF = 2816, 1408
EXPERTS = 8
EPS = 1e-6
SLOT = 2048
RING = 3
BLK = 256
ADA_COLS = 2048
ADA_UNITS = 6 * D // ADA_COLS
IN_ORDER = [3, 4, 0, 1, 2, 5, 6, 7, 8, 9, 10, 11, 12]
NB = len(IN_ORDER)
DENSE = FF // BLK
EG = EFF // BLK
EREM = EFF - EG * BLK
EJ = EG + 1
EF = EFF // P
KD = 2 * EG + 1
DROWS = (2, 2, 1, 1, 1, 2, 2)
ED = len(DROWS)
EK = KD + ED
assert sum(DROWS) == EF and 2 * EREM == BLK
MRING = 6
CHUNKS_OVER = TOK // P - 1
MAX_EXTRA = (2 * TOK - 1) // P
GATHER_AT, TURN_AT = 4, 5

CONST = {}
_at = 0
for _n, _w in (("ident", 128), ("cosm", 64), ("sinm", 64), ("cosr", 256), ("sinr", 256), ("kexp", 2),
               ("qexp", 256), ("dexp", 256), ("tri", 256), ("upper", 128), ("iota", 128), ("ones", 128),
               ("number", EXPERTS * CHUNKS_OVER)):
    CONST[_n] = (_at, _at + _w)
    _at += _w
N_CONST = _at


def hybrid_step(nc, x_prompt, x_sample, cache_ckv, cache_krope, state_ret, c, c_ctx, attn_norm, ffn_norm,
                w_ada, b_ada, w_in, kv_norm, w_ukv, q_norm, k_norm, decay_logit, w_out, w_ffn_gate,
                w_ffn_up, w_ffn_down, w_router, w_exp_gate, w_exp_up, w_exp_down, const_tab,
                y_prompt, y_sample, new_ckv, new_krope, new_state):
    f32, f32r = mybir.dt.float32, mybir.dt.float32r
    i32, u32 = mybir.dt.int32, mybir.dt.uint32
    ACT, ALU, AX = mybir.ActivationFunctionType, mybir.AluOpType, mybir.AxisListType

    mod_rows = nc.dram_tensor("mod_rows", (DEPTH * ADA_UNITS, P, 512), f32, kind="Internal").ap()

    chunks = []
    n_split = 0

    def add(kind, src, size, shape, free=None):
        nonlocal n_split
        m = None
        if kind == "split":
            m = n_split
            n_split += 1
        chunks.append(dict(n=len(chunks), m=m, a=sum(q["m"] is None for q in chunks), src=src, size=size,
                           shape=shape, free=free))
        return chunks[-1]

    def cols(w, c0, wd):
        return w.rearrange("(k p) n -> p k n", p=P)[:, :, c0:c0 + wd]

    sems = ExitStack()

    def sem(name):
        return sems.enter_context(nc.semaphore(name))

    with sems:
        raw_full = [sem(f"raw_full{i}") for i in range(MRING)]
        ada_used, hi_made, lo_made = sem("ada_used"), sem("hi_made"), sem("lo_made")
        proj_psum, ukv_psum, out_psum = sem("proj_psum"), sem("ukv_psum"), sem("out_psum")
        gate_done, up_done, down_done = sem("gate_done"), sem("up_done"), sem("down_done")

        ada_extra = [0] + [1] * (NB - 1)
        ADA_RET = 2 * DK - sum(ada_extra)
        assert ADA_RET == NT + 1
        IN, UKV, OUT = {}, {}, {}

        def add_ada(l, u, k):
            add("plain", w_ada[l, P * k:P * (k + 1), ADA_COLS * u:ADA_COLS * (u + 1)], ADA_COLS, None)

        for k in range(DK):
            add_ada(0, 0, k)
        for l in range(DEPTH):
            a = 0
            for p in range(NB):
                c0 = IN_ORDER[p] * BLK
                wd = min(BLK, IN_COLS - c0)
                IN[l, p] = add("split", cols(w_in[l], c0, wd), DK * wd, wd, (proj_psum, NB * NT * l + NT * (p + 1)))
                for _ in range(ada_extra[p]):
                    add_ada(l, 1 + a // DK, a % DK)
                    a += 1
            UKV[l] = add("split", w_ukv[l].rearrange("(k p) n -> p k n", p=P), SLOT, 1024, (ukv_psum, 8 * (l + 1)))
            for k in range(DK - ADA_RET, DK):
                add_ada(l, 2, k)
            if l == 0:
                for k in range(DK):
                    add_ada(1, 0, k)
            for j in range(4):
                OUT[l, j] = add("split", cols(w_out[l], BLK * j, BLK), SLOT, BLK, (out_psum, 12 * l + 3 * (j + 1)))
            if l == 0:
                DN, DM = len(chunks), n_split
                for s in range(3 * DENSE):
                    add("split", None, SLOT, None)
                chunks[DN]["free"] = (gate_done, 2)
                chunks[DN + 1]["free"] = (up_done, 2)
                chunks[-3]["free"] = (up_done, 2 * DENSE)
                chunks[-2]["free"] = (down_done, DENSE)
                chunks[-1]["free"] = (down_done, DENSE + 1)
        MN, MM = len(chunks), n_split
        assert MN % RING == 0 and MM % RING == 0
        splits = [q for q in chunks if q["m"] is not None]

        c_loaded, ident_loaded, const_loaded = sem("c_loaded"), sem("ident_loaded"), sem("const_loaded")
        c_silu, cT_psum, cT_made, sigmoid_made = sem("c_silu"), sem("cT_psum"), sem("cT_made"), sem("sigmoid_made")
        spread_psum, shift_made = sem("spread_psum"), sem("shift_made")
        x_loaded, decay_loaded = sem("x_loaded"), sem("decay_loaded")
        bias_loaded, modrow_made, mod_stored, mod_loaded = sem("bias_loaded"), sem("modrow_made"), sem("mod_stored"), sem("mod_loaded")
        gate_loaded = sem("gate_loaded")
        ss_made, rstd_made, htok_made, hT_psum, hT_hi_made, hT_made = (sem(n) for n in (
            "ss_made", "rstd_made", "htok_made", "hT_psum", "hT_hi_made", "hT_made"))
        proj_made = sem("proj_made")
        wrow_loaded, ckv_ss, ckv_rstd, ckv_made, cache_stored = (sem(n) for n in (
            "wrow_loaded", "ckv_ss", "ckv_rstd", "ckv_made", "cache_stored"))
        silu_g, dec_arg, dec_exp, s0_loaded = (sem(n) for n in ("silu_g", "dec_arg", "dec_exp", "s0_loaded"))
        kr_roped, x_rest, down_tile = sem("kr_roped"), sem("x_rest"), sem("down_tile")
        rT_psum, rT_made, kd_made, qd_made = sem("rT_psum"), sem("rT_made"), sem("kd_made"), sem("qd_made")
        sc_psum, sc_masked, st_psum, st_made, state_stored = (sem(n) for n in (
            "sc_psum", "sc_masked", "st_psum", "st_made", "state_stored"))
        ro_psum, ro_sq, ro_ss, ro_rstd, ro_made = (sem(n) for n in ("ro_psum", "ro_sq", "ro_ss", "ro_rstd", "ro_made"))
        ckvc_loaded, tail_ss, tail_eps, v_made, sqk_made, ckvT_psum, ckvT_hi, ckvT_made = (sem(n) for n in (
            "ckvc_loaded", "tail_ss", "tail_eps", "v_made", "sqk_made", "ckvT_psum", "ckvT_hi", "ckvT_made"))
        q_sq, qk_ss, qk_rstd, qk_made, qk_rope, hT2_psum, headT_lo = (sem(n) for n in (
            "q_sq", "qk_ss", "qk_rstd", "qk_made", "qk_rope", "hT2_psum", "headT_lo"))
        headT_hi = sem("headT_hi")
        s_psum, negmax, exp_made, pT_psum, pT_made, pv_psum, a_made = (sem(n) for n in (
            "s_psum", "negmax", "exp_made", "pT_psum", "pT_made", "pv_psum", "a_made"))
        mT_psum, mT_hi, mT_made, x1_made = sem("mT_psum"), sem("mT_hi"), sem("mT_made"), sem("x1_made")
        gate_silu, act_made, acth_made, actl_made, x2_made = (sem(n) for n in (
            "gate_silu", "act_made", "acth_made", "actl_made", "x2_made"))
        y_stored = sem("y_stored")
        dve_chain, pool_chain, act_chain = sem("dve_chain"), sem("pool_chain"), sem("act_chain")
        pe_phase, act_phase, dve_phase, pool_phase = (sem(n) for n in ("pe_phase", "act_phase", "dve_phase", "pool_phase"))
        hth_made, htl_made = sem("hth_made"), sem("htl_made")
        wr_loaded, wr_hi, wr_made, lgT_psum, lgT_made, lg_psum, lg_exp, route_made, rank_psum, extra_listed = (sem(n) for n in (
            "wr_loaded", "wr_hi", "wr_made", "lgT_psum", "lgT_made", "lg_psum", "lg_exp", "route_made", "rank_psum", "extra_listed"))
        pick_made, xtok_made, xT_psum, sums_zeroed, sums_made, pickT_psum, pickT_made, gath_psum, xe_hi, xe_made = (sem(n) for n in (
            "pick_made", "xtok_made", "xT_psum", "sums_zeroed", "sums_made", "pickT_psum", "pickT_made", "gath_psum", "xe_hi", "xe_made"))
        eg_done, eu_done, esilu_made, eact_made, eT_psum, eT_hi, eT_made = (sem(n) for n in (
            "eg_done", "eu_done", "esilu_made", "eact_made", "eT_psum", "eT_hi", "eT_made"))
        ed_done, o_hi_made, o_made, sca_psum, y_added = (sem(n) for n in (
            "ed_done", "o_hi_made", "o_made", "sca_psum", "y_added"))

        mem = ExitStack()

        def sb(name, shape, dt=f32, where=None):
            return (where or mem).enter_context(nc.sbuf_tensor(name, shape, dt))

        with mem:
            raw = sb("raw", [P, RING, SLOT])
            whi = sb("whi", [P, RING, SLOT], f32r)
            wlo = sb("wlo", [P, RING, SLOT], f32r)
            x = sb("x", [P, NT, D])
            const = sb("const", [P, N_CONST])
            modsb = sb("modsb", [P, 2, 2, D])
            modg = sb("modg", [P, 2, D])
            nw = sb("nw", [P, D])
            brow = sb("brow", [P, 512])
            modrow = sb("modrow", [P, 512])
            cT = sb("cT", [P, DK, 32])
            craw = modg[0:2 * DK, 0, 0:P]
            stat = sb("stat", [P, 64])
            pstat = sb("pstat", [P, 128])
            half = sb("half", [P, 8])
            lg = sb("lg", [P, DEPTH, 8])
            lgt = sb("lgt", [P, 2, DEPTH * 8])
            dec = sb("dec", [P, 2, 8])
            wrow = sb("wrow", [P, LORA + 2 * HD])
            cc = sb("cc", [P, LORA])
            kpe = sb("kpe", [P, ROPE])
            ktail = sb("ktail", [P, 4, ROPE])
            psum = [mem.enter_context(nc.psum_tensor(f"bank{i}", [P, 512], f32)) for i in range(8)]

            def cst(name):
                return const[:, CONST[name][0]:CONST[name][1]]

            ident = cst("ident")
            ones = cst("ones")
            sbflat = modsb[:].rearrange("p a b c -> p (a b c)")
            qdec = sbflat[:, 0:1024].rearrange("p (d h i) -> p d h i", d=2, h=RH)
            mtmp = sbflat[:, 1024:2048].rearrange("p (d h i) -> p d h i", d=2, h=RH)
            maskT = mtmp[:, 0]
            S0 = sbflat[:, 2048:3072].rearrange("p (d h e) -> p d h e", d=2, h=RH)
            S1 = sbflat[:, 3072:4096].rearrange("p (d h e) -> p d h e", d=2, h=RH)
            kT = sbflat[0:HD, 0:4096].rearrange("p (h t) -> p h t", h=HEADS)
            ysum = sbflat[:, 0:NT * D].rearrange("p (t d) -> p t d", t=NT)
            esg = sbflat[:, 3072:3584].rearrange("p (b n) -> p b n", b=2)
            eact = sbflat[:, 3584:4096].rearrange("p (b n) -> p b n", b=2)

            mix = {}
            for l in range(DEPTH):
                with ExitStack() as ph:
                    proj = sb(f"proj{l}", [P, NT, IN_COLS], f32, ph)
                    m = {"proj": proj, "sqk": nw[:].rearrange("p (b h e) -> p b h e", b=2, h=HEADS)}
                    with ExitStack() as a:
                        m["hTh"] = sb(f"hTh{l}", [P, DK, TOK], f32r, a)
                        m["hTl"] = sb(f"hTl{l}", [P, DK, TOK], f32r, a)
                        m["htok"] = sb(f"htok{l}", [P, NT, D], f32, a)
                        m["rt"] = m["htok"][:, 1, :].rearrange("p (b n) -> p b n", b=2)
                        m["sq"] = m["htok"][:, 2, 0:HEADS * HD]
                    with ExitStack() as a:
                        m["at"] = sb(f"at{l}", [P, NT, RH, P], f32, a)
                        m["qrT"] = sb(f"qrT{l}", [P, NT, RH, P], f32, a)
                        m["krT"] = sb(f"krT{l}", [P, NT, RH, P], f32, a)
                        m["kd"] = sb(f"kd{l}", [P, 4, RH, P], f32, a)
                        m["qd"] = sb(f"qd{l}", [P, 4, RH, P], f32, a)
                        m["st"] = sb(f"st{l}", [P, 2, RH, P], f32, a)
                    with ExitStack() as a:
                        m["k3"] = sb(f"keys3{l}", [P, HEADS, HD], f32, a)
                        m["v"] = sb(f"v{l}", [P, 4, HEADS, VD], f32, a)
                        m["qT"] = sb(f"qT{l}", [HD, HEADS, TOK], f32, a)
                        with ExitStack() as b:
                            m["cTh"] = sb(f"cTh{l}", [P, 2, 512], f32r, b)
                            m["cTl"] = sb(f"cTl{l}", [P, 2, 512], f32r, b)
                        with ExitStack() as b:
                            m["pT"] = sb(f"pT{l}", [P, 3, TOK], f32, b)
                    with ExitStack() as a:
                        m["mTh"] = sb(f"mTh{l}", [P, DK, TOK], f32r, a)
                        m["mTl"] = sb(f"mTl{l}", [P, DK, TOK], f32r, a)
                        m["tmp"] = sb(f"outtmp{l}", [P, 2, BLK], f32, a)
                    m["kcat"] = [proj[:, kt, VR:VR + HEADS * HD].rearrange("p (h d) -> p h d", h=HEADS) for kt in range(3)] + [m["k3"][:]]
                    mix[l] = m
            ffn = {}
            with ExitStack() as ph:
                ffn["hTh"] = sb("fhTh", [P, DK, TOK], f32r, ph)
                ffn["hTl"] = sb("fhTl", [P, DK, TOK], f32r, ph)
                ffn["htok"] = sb("fhtok", [P, NT, D], f32, ph)
                ffn["sg"] = sb("fsg", [P, 2, TOK], f32, ph)
                ffn["act"] = sb("fact", [P, 2, TOK], f32, ph)
                ffn["acth"] = sb("facth", [P, 2, 2, TOK], f32r, ph)
                ffn["actl"] = sb("factl", [P, 2, 2, TOK], f32r, ph)
                ffn["tmp"] = sb("ftmp", [P, 2, 512], f32, ph)
            moe = {}
            with ExitStack() as ph:
                moe["hth"] = sb("hth", [P, NT, D], f32r, ph)
                moe["htl"] = sb("htl", [P, NT, D], f32r, ph)
                moe["cmb"] = sb("cmb", [P, NT, 8], f32, ph)
                moe["posc"] = sb("posc", [P, NT, 8 * (1 + CHUNKS_OVER)], f32, ph)
                moe["over"] = sb("over", [1, 8 * CHUNKS_OVER], f32, ph)
                moe["sorted"] = sb("sorted", [1, 8], f32, ph)
                moe["extra"] = sb("extra", [1, 8], i32, ph)
                with ExitStack() as a:
                    moe["htok"] = sb("ehtok", [P, NT, D], f32, a)
                    moe["hTh"] = sb("ehTh", [P, DK, TOK], f32r, a)
                    moe["hTl"] = sb("ehTl", [P, DK, TOK], f32r, a)
                    moe["wr"] = sb("wr", [P, DK, 8], f32, a)
                    moe["wrh"] = sb("wrh", [P, DK, 8], f32r, a)
                    moe["wrl"] = sb("wrl", [P, DK, 8], f32r, a)
                    moe["r"] = sb("route", [P, 12, NT, 8], f32, a)
                    moe["lgT"] = sb("lgT", [8, TOK], f32, a)
                    moe["ix"] = sb("ix", [P, NT, 8], u32, a)
                with ExitStack() as a:
                    moe["rawx"] = sb("rawx", [P, MRING - RING, SLOT], f32, a)
                    moe["xtok"] = nw
                    moe["xeh"] = sb("xeh", [P, DK, P], f32r, a)
                    moe["xel"] = sb("xel", [P, DK, P], f32r, a)
                    moe["pick"] = sb("pick", [P, NT, P], f32r, a)
                    moe["pickT"] = sb("pickT", [P, NT, P], f32r, a)
                    moe["eTh"] = sb("eTh", [P, EF, P], f32r, a)
                    moe["eTl"] = sb("eTl", [P, EF, P], f32r, a)
                    moe["oh"] = sb("oh", [P, D], f32r, a)
                    moe["ol"] = sb("ol", [P, D], f32r, a)
                    moe["gw"] = sb("gw", [P, 1], f32, a)
                    moe["warm"] = sb("warm", [P, 1], f32, a)

            def bc(ap, shape):
                return ap.to_broadcast(shape)

            def raw_wait(eng, n0, it=0):
                eng.wait_ge(raw_full[n0 % RING], 16 * (n0 // RING + 1) + 16 * it)

            def mraw(k):
                return raw[:, k] if k < RING else moe["rawx"][:, k - RING]

            MUSES = [MN // RING] * RING + [0] * (MRING - RING)

            def e_size(k):
                return SLOT if k < KD else D * DROWS[k - KD]

            def e_loads(k):
                return 2 if k == KD - 1 else 1

            def pre_free(m):
                return splits[m - RING]["free"] if m >= RING else None

            def dense_free(off, it):
                if off == 5:
                    return gate_done, 2 * it + 4
                if off == 3:
                    return up_done, 2 * it + 2
                return down_done, it + 1

            def expert_wait(eng, r, k):
                ring = [q for q in range(EK) if q % MRING == k % MRING]
                before = MUSES[k % MRING] + sum(e_loads(q) for q in ring if q <= k)
                eng.wait_ge(raw_full[k % MRING], 16 * before + 16 * sum(e_loads(q) for q in ring) * r)

            def expert_hi(act, s, r, k, static=False):
                expert_wait(act, r, k)
                if static:
                    act.wait_ge(*splits[MM + k - RING]["free"])
                elif k < RING:
                    act.wait_ge(ed_done, ED * r + k + 1)
                else:
                    act.wait_ge(*expert_free(r, k - RING))
                z = e_size(k)
                s.activation(whi[:, k % RING, 0:z], mraw(k % MRING)[:, 0:z], ACT.Copy).then_inc(hi_made, 1)

            def expert_lo(dve, v, r, k):
                dve.wait_ge(hi_made, MM + EK * r + k + 1)
                z = e_size(k)
                v.tensor_tensor(wlo[:, k % RING, 0:z], mraw(k % MRING)[:, 0:z], whi[:, k % RING, 0:z].bitcast(f32),
                                ALU.subtract).then_inc(lo_made, 1)

            def expert_free(r, k):
                if k < KD - 1:
                    return (eu_done, EG * r + k // 2 + 1) if k % 2 else (eg_done, EJ * r + k // 2 + 1)
                if k == KD - 1:
                    return (eg_done, EJ * (r + 1))
                return (ed_done, ED * r + (k - KD) + 1 + RING)

            SPREAD_BANK = (0, 1, 2, 3, 4, 5, 7, 6)

            HEAD_BANK = (0, 0, 0, 0, 2, 0, 4)
            UKV_BANK = (4, 2, 6, 4)
            CKV_BANK = (6, 7)
            ADA_AT = tuple(range(1, 2 * DK, 2))
            OUT_AT = {19: 0, 21: 1}
            SCORE_BANK = (0, 1, 6)

            LAST_BANK = (6, 7, 0, 1, 2, 3)
            SCATTER_AT = ((0,), (1,), (2,), (3,), (4, 5), ())

            def act_gather(act, s, r):
                for b in range(2):
                    act.wait_ge(gath_psum, 2 * r + b + 1)
                    s.activation(moe["xtok"][:, 512 * b:512 * (b + 1)], psum[2 * b][:], ACT.Copy).then_inc(xtok_made, 1)

            def act_turn(act, s, r):
                for b in range(2):
                    act.wait_ge(xT_psum, 2 * r + b + 1)
                    s.activation(moe["xeh"][:, 4 * b:4 * b + 4, :],
                                 psum[1 + 2 * b][:].rearrange("p (c i) -> p c i", c=4), ACT.Copy).then_inc(xe_hi, 1)

            def make_act_expert(act, s):
                def eT(r, j):
                    act.wait_ge(eT_psum, EJ * r + j + 1)
                    w = min(2, EF - 2 * j)
                    s.activation(moe["eTh"][:, 2 * j:2 * j + w, :],
                                 psum[4 + j % 2][:, 0:P * w].rearrange("p (c i) -> p c i", c=w), ACT.Copy).then_inc(eT_hi, 1)

                def body(r, more):
                    s.activation(moe["warm"][:], half[:, 0:1], ACT.Silu)
                    for j in range(EJ):
                        w = BLK if j < EG else EREM
                        if j >= 1:
                            expert_hi(act, s, r, 2 * j + 2)
                        act.wait_ge(eg_done, EJ * r + j + 1)
                        s.activation(esg[:, j % 2, 0:w], psum[j % 2][:, 0:w], ACT.Silu).then_inc(esilu_made, 1)
                        if j < EG:
                            expert_hi(act, s, r, 2 * j + 3)
                        if j >= 1:
                            eT(r, j - 1)
                        if j == EG - 1:
                            act.wait_ge(pickT_psum, r + 1)
                            s.activation(moe["pickT"][:], psum[3][:, 0:TOK].rearrange("p (t i) -> p t i", t=NT),
                                         ACT.Copy).then_inc(pickT_made, 1)
                            s.activation(moe["gw"][:], psum[3][:, TOK:TOK + 1], ACT.Copy).then_inc(pickT_made, 1)
                    for k in range(KD, EK):
                        if more and k == KD + TURN_AT:
                            act_turn(act, s, r + 1)
                        if k + 2 < EK:
                            expert_hi(act, s, r, k + 2)
                        elif more:
                            expert_hi(act, s, r + 1, k + 2 - EK)
                        if k == KD + 1:
                            eT(r, EJ - 1)
                        if more and k == KD + GATHER_AT:
                            act_gather(act, s, r + 1)
                    act.wait_ge(ed_done, ED * (r + 1) + RING)
                    act.wait_ge(pickT_made, 2 * r + 2)
                    for b in range(2):
                        s.activation(moe["oh"][:, 512 * b:512 * (b + 1)], psum[6 + b][:], ACT.Copy,
                                     scale=moe["gw"][:, 0:1]).then_inc(o_hi_made, 1)
                    if more:
                        expert_hi(act, s, r + 1, 2)
                return body

            def extra_items(eng, ns, item):
                count = ns.alloc_register("last_item")
                cur = ns.alloc_register("its_expert")
                entry, expert, column = (ns.alloc_register(n) for n in ("entry", "expert", "column"))
                ns.reg_mov(count, EXPERTS - 1)
                ns.reg_mov(cur, EXPERTS - 1)
                eng.wait_ge(extra_listed, 1)
                with eng.Fori(0, MAX_EXTRA) as i:
                    ns.reg_load(entry, moe["extra"][0:1, bass.ds(i, 1)])
                    with ns.If_ne(entry, 0):
                        ns.reg_mov(expert, (ns.snap(entry) - 1) & (EXPERTS - 1))
                        ns.reg_mov(column, ns.snap(entry) + (EXPERTS - 1))
                        e1 = ns.snap(expert, min_val=0, max_val=EXPERTS - 1)
                        q1 = ns.snap(column, min_val=EXPERTS, max_val=EXPERTS * (1 + CHUNKS_OVER) - 1)
                        item(ns.snap(count), ns.snap(cur, min_val=0, max_val=EXPERTS - 1), e1, q1)
                        ns.reg_add(count, count, 1)
                        ns.reg_mov(cur, expert)
                return ns.snap(count), ns.snap(cur, min_val=0, max_val=EXPERTS - 1)

            def dve_moe(dve, v, link, barrier):
                R = moe["r"]
                dve.wait_ge(wr_hi, 1)
                v.tensor_tensor(moe["wrl"][:], moe["wr"][:], moe["wrh"][:].bitcast(f32), ALU.subtract).then_inc(wr_made, 1)
                for k in range(2):
                    expert_lo(dve, v, 0, k)
                dve.wait_ge(lg_psum, 1)
                link(v.tensor_copy(R[:, 0], psum[2][:, 0:NT * 8].rearrange("p (t e) -> p t e", t=NT)))
                for t in range(NT):
                    last = v.max(R[:, 2, t, :], R[:, 0, t, :])
                link(last)
                for t in range(NT):
                    last = v.max_index(moe["ix"][:, t, :], R[:, 2, t, :], R[:, 0, t, :])
                link(last)
                v.tensor_tensor(R[:, 1, :, 0:1], R[:, 2, :, 1:2], R[:, 2, :, 0:1], ALU.subtract).then_inc(route_made, 1)
                link(v.tensor_copy(R[:, 3], moe["ix"][:]))
                io = cst("iota")[:, 0:8]
                for t in range(NT):
                    for c2 in range(2):
                        last = v.tensor_scalar(R[:, 6 + c2, t, :], io, R[:, 3, t, c2:c2 + 1], None, ALU.is_equal)
                link(last)
                v.tensor_tensor(R[:, 10], R[:, 6], R[:, 7], ALU.add).then_inc(route_made, 1)
                dve.wait_ge(lg_exp, 1)
                link(v.tensor_scalar(R[:, 4, :, 0:1], R[:, 1, :, 0:1], 1.0, None, ALU.add))
                link(v.reciprocal(R[:, 5, :, 0:1], R[:, 4, :, 0:1]))
                link(v.tensor_tensor(R[:, 5, :, 1:2], R[:, 5, :, 0:1], R[:, 1, :, 0:1], ALU.mult))
                for t in range(NT):
                    for c2 in range(2):
                        last = v.tensor_scalar(R[:, 8 + c2, t, :], R[:, 6 + c2, t, :], R[:, 5, t, c2:c2 + 1], None, ALU.mult)
                link(last)
                v.tensor_tensor(moe["cmb"][:], R[:, 8], R[:, 9], ALU.add)
                expert_lo(dve, v, 0, 2)
                dve.wait_ge(rank_psum, 1)
                link(v.tensor_scalar(R[:, 11], psum[1][:, 0:NT * 8].rearrange("p (t e) -> p t e", t=NT), 1.0, None, ALU.add))
                link(v.tensor_tensor(R[:, 11], R[:, 11], R[:, 10], ALU.mult))
                for cc in range(1 + CHUNKS_OVER):
                    last = v.tensor_scalar(moe["posc"][:, :, 8 * cc:8 * cc + 8], R[:, 11], -1.0 - P * cc, None, ALU.add)
                link(last)
                barrier(pool_too=True)

                def pick(q, n):
                    for t in range(NT):
                        last = v.tensor_scalar(moe["pick"][:, t, :], cst("iota"), moe["posc"][:, t, bass.ds(q, 1)], None, ALU.is_equal)
                    last.then_inc(pick_made, 1)

                def gather(r):
                    for b in range(2):
                        dve.wait_ge(xe_hi, 2 * r + b + 1)
                        v.tensor_tensor(moe["xel"][:, 4 * b:4 * b + 4, :], psum[1 + 2 * b][:].rearrange("p (c i) -> p c i", c=4),
                                        moe["xeh"][:, 4 * b:4 * b + 4, :].bitcast(f32), ALU.subtract).then_inc(xe_made, 1)

                def eT(r, j):
                    dve.wait_ge(eT_hi, EJ * r + j + 1)
                    w = min(2, EF - 2 * j)
                    v.tensor_tensor(moe["eTl"][:, 2 * j:2 * j + w, :], psum[4 + j % 2][:, 0:P * w].rearrange("p (c i) -> p c i", c=w),
                                    moe["eTh"][:, 2 * j:2 * j + w, :].bitcast(f32), ALU.subtract).then_inc(eT_made, 1)

                def add_y(s, u):
                    t, hf = divmod(u, 2)
                    dve.wait_ge(sca_psum, 2 * NT * s + u + 1)
                    ys = ysum[:, t, 512 * hf:512 * (hf + 1)]
                    v.tensor_tensor(ys, ys, psum[6 + u % 2][:], ALU.add).then_inc(y_added, 1)

                def join(r, t):
                    dve.wait_ge(y_added, 2 * NT * (r + 1))
                    link(v.tensor_tensor(ysum[:, t, :], ysum[:, t, :], modg[:, KIND[t], :], ALU.mult))
                    v.tensor_tensor(x[:, t, :], x[:, t, :], ysum[:, t, :], ALU.add).then_inc(sums_made, 1)

                def body(r, q):
                    for j in range(EJ):
                        w = BLK if j < EG else EREM
                        if j >= 1:
                            expert_lo(dve, v, r, 2 * j + 2)
                        if j < EG:
                            expert_lo(dve, v, r, 2 * j + 3)
                            dve.wait_ge(eu_done, EG * r + j + 1)
                            up = psum[2 + j % 2][:, 0:w]
                        else:
                            dve.wait_ge(eg_done, EJ * r + j + 1)
                            up = psum[j % 2][:, EREM:2 * EREM]
                        dve.wait_ge(esilu_made, EJ * r + j + 1)
                        v.tensor_tensor(eact[:, j % 2, 0:w], up, esg[:, j % 2, 0:w], ALU.mult).then_inc(eact_made, 1)
                        if j >= 1:
                            eT(r, j - 1)
                        for u in SCATTER_AT[j]:
                            add_y(r, u)
                    if q is not None:
                        dve.wait_ge(pickT_psum, r + 1)
                        pick(q, r + 1)
                    for k in range(KD, EK):
                        if q is not None and k == KD + TURN_AT:
                            gather(r + 1)
                        if k + 2 < EK:
                            expert_lo(dve, v, r, k + 2)
                        elif q is not None:
                            expert_lo(dve, v, r + 1, k + 2 - EK)
                        if k == KD + 1:
                            eT(r, EJ - 1)
                        if q is None and k >= EK - 2:
                            join(r, k - (EK - 2))
                    for b in range(2):
                        dve.wait_ge(o_hi_made, 2 * r + b + 1)
                        cs = slice(512 * b, 512 * (b + 1))
                        v.scalar_tensor_tensor(out=moe["ol"][:, cs], in0=psum[6 + b][:], scalar=moe["gw"][:, 0:1],
                                               in1=moe["oh"][:, cs].bitcast(f32), op0=ALU.mult, op1=ALU.subtract).then_inc(o_made, 1)
                    if q is not None:
                        expert_lo(dve, v, r + 1, 2)

                pick(0, 0)
                for cc in range(1, 1 + CHUNKS_OVER):
                    last = v.tensor_scalar(moe["over"][0:1, 8 * (cc - 1):8 * cc], psum[1][0:1, NT * 8:NT * 8 + 8],
                                           float(P * cc), None, ALU.is_gt)
                link(last)
                link(v.tensor_tensor(moe["over"][:], moe["over"][:], cst("number")[0:1, :], ALU.mult))
                link(v.max(moe["sorted"][:], moe["over"][:]))
                v.tensor_copy(moe["extra"][:], moe["sorted"][:]).then_inc(extra_listed, 1)
                v.memset(moe["oh"][:].bitcast(f32), 0.0)
                v.memset(moe["ol"][:].bitcast(f32), 0.0)
                v.memset(moe["pickT"][:].bitcast(f32), 0.0).then_inc(o_made, 2)
                gather(0)
                dve.wait_ge(sums_zeroed, 1)
                with dve.Fori(0, EXPERTS - 1) as e:
                    body(e, e + 1)
                r, _ = extra_items(dve, v, lambda r, e, e1, q: body(r, q))
                dve.wait_ge(gate_loaded, 128)
                body(r, None)
                join(r, NT - 1)
                dve.wait_ge(sums_made, NT)
                for t in range(NT):
                    for hf in range(2):
                        u = 2 * t + hf
                        cs = slice(512 * hf, 512 * (hf + 1))
                        dve.wait_ge(sca_psum, 2 * NT * (r + 1) + u + 1)
                        link(v.tensor_tensor(ysum[:, t, cs], psum[LAST_BANK[u]][:], modg[:, KIND[t], cs], ALU.mult))
                        last = v.tensor_tensor(x[:, t, cs], x[:, t, cs], ysum[:, t, cs], ALU.add)
                    last.then_inc(x2_made, 1)

            def pe_dense(pe, mm):
                nc.tensor.drain().then_inc(down_done, 1)
                pe.wait_ge(hT_made, 2 * NT * 2)

                def up_block(off, it, i):
                    for ft in range(2):
                        for w, (bank, done, freed) in enumerate(((6, gate_done, gate_silu), (7, up_done, act_made))):
                            m0 = DM + off + w
                            pe.wait_ge(lo_made, m0 + 1 + 3 * it)
                            if not (isinstance(i, int) and i == 0 and ft == 0):
                                pe.wait_ge(freed, 2 * i + ft)
                            wh = whi[:, m0 % RING, :].rearrange("p (k n) -> p k n", n=BLK)
                            wl = wlo[:, m0 % RING, :].rearrange("p (k n) -> p k n", n=BLK)
                            fs = slice(P * ft, P * (ft + 1))
                            for k in range(DK):
                                mm(psum[bank][:, 0:TOK], wh[:, k, fs], ffn["hTh"][:, k, :], start=(k == 0), stop=False)
                                mm(psum[bank][:, 0:TOK], wh[:, k, fs], ffn["hTl"][:, k, :], start=False, stop=False)
                                last = mm(psum[bank][:, 0:TOK], wl[:, k, fs], ffn["hTh"][:, k, :], start=False, stop=(k == DK - 1))
                            last.then_inc(done, 1)

                def down_block(off, it, i, par, first, final):
                    m0 = DM + off
                    pe.wait_ge(lo_made, m0 + 1 + 3 * it)
                    pe.wait_ge(actl_made, 2 * i + 2)
                    wh = whi[:, m0 % RING, :].rearrange("p (k n) -> p k n", n=D)
                    wl = wlo[:, m0 % RING, :].rearrange("p (k n) -> p k n", n=D)
                    for t in range(NT):
                        for ft in range(2):
                            ah = ffn["acth"][:, par, ft, P * t:P * (t + 1)]
                            al = ffn["actl"][:, par, ft, P * t:P * (t + 1)]
                            for a, w in ((ah, wh), (ah, wl), (al, wh)):
                                for hf in range(2):
                                    last = mm(psum[2 * t + hf][:], a, w[:, ft, 512 * hf:512 * (hf + 1)],
                                              start=(first and ft == 0 and a is ah and w is wh),
                                              stop=(final and ft == 1 and a is al))
                        if final:
                            last.then_inc(down_tile, 1)
                    if final:
                        last = nc.tensor.drain()
                    last.then_inc(down_done, 1)

                up_block(0, 0, 0)
                up_block(2, 0, 1)
                down_block(4, 0, 0, 0, True, False)
                up_block(2, 1, 2)
                down_block(4, 1, 1, 1, False, False)
                with pe.Fori(1, (DENSE - 1) // 2) as b:
                    for h in range(2):
                        up_block(2, 2 * b + h, 2 * b + h + 1)
                        down_block(4, 2 * b + h, 2 * b + h, h, False, False)
                down_block(5, DENSE - 2, DENSE - 1, 0, False, True)

            def pe_moe(pe, mm, mm3, barrier):
                tr = nc.tensor.transpose
                pe.wait_ge(hT_made, 2 * NT * 4)
                pe.wait_ge(wr_made, 1)
                for k in range(DK):
                    last = mm3(psum[0][0:8, 0:TOK], moe["wrh"][:, k, :], moe["wrl"][:, k, :],
                               moe["hTh"][:, k, :], moe["hTl"][:, k, :], k == 0, k == DK - 1)
                last.then_inc(lgT_psum, 1)
                pe.wait_ge(lgT_made, 1)
                for t in range(NT):
                    last = tr(psum[2][:, 8 * t:8 * t + 8], moe["lgT"][:, P * t:P * (t + 1)], ident[0:8, 0:8])
                last.then_inc(lg_psum, 1)
                pe.wait_ge(route_made, 2)
                one = moe["r"][:, 10]
                for t in range(NT):
                    for t2 in range(t + 1):
                        mm(psum[1][:, 8 * t:8 * t + 8], cst("upper") if t2 == t else ones, one[:, t2, :],
                           start=(t2 == 0), stop=(t2 == t))
                for t2 in range(NT):
                    last = mm(psum[1][:, 8 * NT:8 * NT + 8], ones, one[:, t2, :], start=(t2 == 0), stop=(t2 == NT - 1))
                last.then_inc(rank_psum, 1)
                barrier(pool_too=True)
                nc.tensor.drain().then_inc(ed_done, RING)

                def gather(r):
                    pe.wait_ge(pick_made, r + 1)
                    for hf in range(2):
                        for t in range(NT):
                            for z, h in enumerate((moe["hth"], moe["htl"])):
                                last = mm(psum[2 * hf][:], moe["pick"][:, t, :], h[:, t, 512 * hf:512 * (hf + 1)],
                                          start=(t == 0 and z == 0), stop=(t == NT - 1 and z == 1))
                        last.then_inc(gath_psum, 1)

                def turn(r):
                    for hf in range(2):
                        pe.wait_ge(xtok_made, 2 * r + hf + 1)
                        for c_ in range(4):
                            last = tr(psum[1 + 2 * hf][:, P * c_:P * (c_ + 1)], moe["xtok"][:, 512 * hf + P * c_:512 * hf + P * (c_ + 1)], ident)
                        last.then_inc(xT_psum, 1)

                def scatter(s, units, banks=None):
                    for u in units:
                        t, hf = divmod(u, 2)
                        if u == 0:
                            pe.wait_ge(o_made, 2 * s + 2)
                        if u >= 2 and not banks:
                            pe.wait_ge(y_added, 2 * NT * s + u - 1)
                        cs = slice(512 * hf, 512 * (hf + 1))
                        bank = banks[u] if banks else 6 + u % 2
                        mm(psum[bank][:], moe["pickT"][:, t, :], moe["oh"][:, cs], start=True, stop=False)
                        mm(psum[bank][:], moe["pickT"][:, t, :], moe["ol"][:, cs], start=False, stop=True).then_inc(sca_psum, 1)

                def eT(r, j):
                    pe.wait_ge(eact_made, EJ * r + j + 1)
                    if j >= 2:
                        pe.wait_ge(eT_made, EJ * r + j - 1)
                    for i in range(min(2, EF - 2 * j)):
                        last = tr(psum[4 + j % 2][:, P * i:P * (i + 1)], eact[:, j % 2, P * i:P * (i + 1)], ident)
                    last.then_inc(eT_psum, 1)

                def product(r, k, bank, done):
                    pe.wait_ge(lo_made, MM + EK * r + k + 1)
                    wh = whi[:, k % RING, :].rearrange("p (k n) -> p k n", n=BLK)
                    wl = wlo[:, k % RING, :].rearrange("p (k n) -> p k n", n=BLK)
                    for c_ in range(DK):
                        last = mm3(psum[bank][:, 0:BLK], moe["xeh"][:, c_, :], moe["xel"][:, c_, :],
                                   wh[:, c_, :], wl[:, c_, :], c_ == 0, c_ == DK - 1)
                    last.then_inc(done, 1)

                def body(r, e, more):
                    pe.wait_ge(xe_made, 2 * (r + 1))
                    for j in range(EG):
                        if j >= 2:
                            pe.wait_ge(esilu_made, EJ * r + j - 1)
                        product(r, 2 * j, j % 2, eg_done)
                        if j >= 2:
                            pe.wait_ge(eact_made, EJ * r + j - 1)
                        product(r, 2 * j + 1, 2 + j % 2, eu_done)
                        if j >= 1:
                            eT(r, j - 1)
                        scatter(r, SCATTER_AT[j])
                    for t in range(NT):
                        tr(psum[3][:, P * t:P * (t + 1)], moe["pick"][:, t, :].bitcast(f32), ident)
                    for t in range(NT):
                        last = mm(psum[3][:, TOK:TOK + 1], moe["pick"][:, t, :].bitcast(f32), moe["cmb"][:, t, bass.ds(e, 1)],
                                  start=(t == 0), stop=(t == NT - 1))
                    last.then_inc(pickT_psum, 1)
                    product(r, KD - 1, EG % 2, eg_done)
                    eT(r, EJ - 2)
                    pe.wait_ge(y_added, 2 * NT * (r + 1))
                    pe.wait_ge(pickT_made, 2 * (r + 1))
                    f0 = 0
                    for i, n in enumerate(DROWS):
                        if more and i == GATHER_AT:
                            gather(r + 1)
                        if more and i == TURN_AT:
                            turn(r + 1)
                        k0 = KD + i
                        pe.wait_ge(lo_made, MM + EK * r + k0 + 1)
                        pe.wait_ge(eT_made, EJ * r + (f0 + n - 1) // 2 + 1)
                        wh = whi[:, k0 % RING, 0:D * n].rearrange("p (k n) -> p k n", n=D)
                        wl = wlo[:, k0 % RING, 0:D * n].rearrange("p (k n) -> p k n", n=D)
                        for f in range(n):
                            ah, al = moe["eTh"][:, f0 + f, :], moe["eTl"][:, f0 + f, :]
                            for z, (a, wt) in enumerate(((ah, wh), (ah, wl), (al, wh))):
                                for hf in range(2):
                                    last = mm(psum[6 + hf][:], a, wt[:, f, 512 * hf:512 * (hf + 1)],
                                              start=(i == 0 and f == 0 and z == 0), stop=(i == ED - 1 and f == n - 1 and z == 2))
                        last.then_inc(ed_done, 1)
                        f0 += n
                        if i == 0:
                            eT(r, EJ - 1)

                gather(0)
                pe.wait_ge(extra_listed, 1)
                turn(0)
                with pe.Fori(0, EXPERTS - 1) as e:
                    body(e, e, True)
                r, e = extra_items(pe, nc.tensor, lambda r, e, e1, q: body(r, e, True))
                body(r, e, False)
                scatter(r + 1, range(2 * NT), LAST_BANK)

            block = sems.enter_context(nc.Block())

            @block.sync
            def _(sp):
                def load(q, dst):
                    n = q["n"]
                    if n >= RING:
                        before = chunks[n - RING]
                        if before["m"] is None:
                            sp.wait_ge(ada_used, before["a"] + 1)
                        else:
                            sp.wait_ge(lo_made, before["m"] + 1)
                    sp.dma_start(dst, q["src"]).then_inc(raw_full[n % RING], 16)

                def slot(q):
                    r = raw[:, q["n"] % RING, 0:q["size"]]
                    return r if q["shape"] is None else r.rearrange("p (k n) -> p k n", n=q["shape"])

                sp.dma_start(craw[0:DK, :], c_ctx.rearrange("(k p) -> k p", p=P)).then_inc(c_loaded, 16)
                sp.dma_start(craw[DK:, :], c.rearrange("a (k p) -> (a k) p", p=P)).then_inc(c_loaded, 16)
                sp.dma_start(ident, const_tab[:, 0:P]).then_inc(ident_loaded, 16)
                for q in chunks[:DK]:
                    load(q, slot(q))
                sp.dma_start(x[:, 0, :], x_prompt[0]).then_inc(x_loaded, 16)
                sp.dma_start(x[:, 1:3, :], x_sample[0].rearrange("(t p) d -> p t d", p=P)).then_inc(x_rest, 16)
                load(chunks[DK], slot(chunks[DK]))
                sp.dma_start(const[:, P:], const_tab[:, P:]).then_inc(const_loaded, 16)
                for q in chunks[DK + 1:DN]:
                    load(q, slot(q))

                def dense_load(off, it, src, shape):
                    n0, m0 = DN + off, DM + off
                    sp.wait_ge(lo_made, m0 - RING + 1 + 3 * it)
                    sp.dma_start(raw[:, n0 % RING, :].rearrange("p (k n) -> p k n", n=shape), src)\
                        .then_inc(raw_full[n0 % RING], 16)

                wg, wu = (w[0].rearrange("(k p) n -> p k n", p=P) for w in (w_ffn_gate, w_ffn_up))
                wd = w_ffn_down[0].rearrange("(i k p) n -> i p k n", p=P, k=2)
                dense_load(0, 0, wg[:, :, 0:BLK], BLK)
                dense_load(1, 0, wu[:, :, 0:BLK], BLK)
                with sp.Fori(0, DENSE - 1) as i:
                    dense_load(2, i, wg[:, :, bass.ds(i * BLK + BLK, BLK)], BLK)
                    dense_load(3, i, wu[:, :, bass.ds(i * BLK + BLK, BLK)], BLK)
                    dense_load(4, i, wd[i], D)
                dense_load(5, DENSE - 2, wd[DENSE - 1], D)

                for q in chunks[DN + 3 * DENSE:]:
                    load(q, slot(q))

                def expert_load(e, r, k):
                    s = k % MRING
                    gate, up = (w[0, e].rearrange("(k p) n -> p k n", p=P) for w in (w_exp_gate, w_exp_up))
                    if k < KD:
                        dst = mraw(s).rearrange("p (k n) -> p k n", n=BLK)
                    if k < KD - 1:
                        pieces = ((dst, (gate, up)[k % 2][:, :, BLK * (k // 2):BLK * (k // 2 + 1)]),)
                    elif k == KD - 1:
                        pieces = ((dst[:, :, 0:EREM], gate[:, :, BLK * EG:]), (dst[:, :, EREM:], up[:, :, BLK * EG:]))
                    else:
                        i = k - KD
                        f0 = sum(DROWS[:i])
                        pieces = ((mraw(s)[:, 0:e_size(k)].rearrange("p (k n) -> p k n", n=D),
                                   w_exp_down[0, e].rearrange("(k p) n -> p k n", p=P)[:, f0:f0 + DROWS[i], :]),)
                    sp.wait_ge(lo_made, MM + EK * r + k - MRING + 1)
                    for out, src in pieces:
                        sp.dma_start(out, src).then_inc(raw_full[s], 16)

                for k in range(EK):
                    if k < RING:
                        sp.wait_ge(lo_made, MM - RING + k + 1)
                    if k == RING:
                        sp.wait_ge(pick_made, 1)
                    expert_load(0, 0, k)
                with sp.Fori(1, EXPERTS) as e:
                    for k in range(EK):
                        expert_load(e, e, k)
                extra_items(sp, nc.sync, lambda r, e, e1, q: [expert_load(e1, r + 1, k) for k in range(EK)])

            @block.gpsimd
            def _(pool):
                g = nc.gpsimd
                chain = [0]

                def link(ins):
                    chain[0] += 1
                    ins.then_inc(pool_chain, 1)
                    pool.wait_ge(pool_chain, chain[0])

                g.dma_start(lgt[:, 0, :], decay_logit.rearrange("(o l) a h -> o (l a h)", o=1).to_broadcast([P, 16]))\
                    .then_inc(decay_loaded, 16)
                g.memset(half[:], -0.5).then_inc(pool_chain, 1)
                chain[0] += 1
                pool.wait_ge(pool_chain, 1)

                def load_bias(u):
                    l, k = divmod(u, ADA_UNITS)
                    src = b_ada[l, ADA_COLS * k:ADA_COLS * (k + 1)].rearrange("(j c) -> j c", j=4)
                    for j in range(4):
                        g.dma_start(brow[32 * j:32 * j + 32, :], src[j:j + 1, :].to_broadcast([32, 512])).then_inc(bias_loaded, 16)

                def store_mod(u):
                    pool.wait_ge(modrow_made, u + 1)
                    g.dma_start(mod_rows[u], modrow[:]).then_inc(mod_stored, 16)
                    if u + 1 < DEPTH * ADA_UNITS:
                        load_bias(u + 1)
                    pool.wait_ge(mod_stored, 16 * u)

                def row(u, kind, h):
                    return mod_rows[u].rearrange("(j q) c -> q j c", q=32)[kind:kind + 1, 2 * h:2 * h + 2, :].to_broadcast([P, 2, 512])

                def halves(ap):
                    return ap.rearrange("p (f c) -> p f c", f=2)

                def load_sb(n):
                    l, s = divmod(n, 2)
                    base = ADA_UNITS * l
                    where = ((base, 0), (base, 1)) if s == 0 else ((base + 1, 1), (base + 2, 0))
                    for kind in range(2):
                        for b in range(2):
                            g.dma_start(halves(modsb[:, kind, b, :]), row(where[b][0], kind, where[b][1])).then_inc(mod_loaded, 16)
                    w = (attn_norm, ffn_norm)[s]
                    g.dma_start(nw[:], w[l:l + 1, :].to_broadcast([P, D])).then_inc(mod_loaded, 16)

                def load_gate(l, s):
                    u, h = ((ADA_UNITS * l + 1, 0), (ADA_UNITS * l + 2, 1))[s]
                    for kind in range(2):
                        g.dma_start(halves(modg[:, kind, :]), row(u, kind, h)).then_inc(gate_loaded, 16)

                def rstd(dst, src, scale, ready, val, out):
                    pool.wait_ge(ready, val)
                    link(g.tensor_scalar(src, src, scale, EPS, ALU.mult, ALU.add))
                    w = src.shape[-1]
                    g.tensor_tensor(dst, src, half[:, 0:w], ALU.pow).then_inc(out, 1)

                def norm_rstd(n):
                    for t in range(NT):
                        rstd(pstat[:, t:t + 1], stat[:, t:t + 1], 1.0 / D, ss_made, NT * n + t + 1, rstd_made)

                def rope(view, cosn, sinn, t, nh, dim, tmp, done):
                    w = dim // 4
                    cs = cst(cosn)[:, (t - 1) * dim:t * dim].unsqueeze(1).to_broadcast([P, nh, dim])
                    sn = cst(sinn)[:, (t - 1) * dim:t * dim].rearrange("p (g s w) -> p g s w", g=2, s=2)
                    t1 = tmp[:, 0, 0:nh * dim].rearrange("p (h d) -> p h d", h=nh)
                    t2 = tmp[:, 1, 0:nh * dim].rearrange("p (h g s w) -> p h g s w", h=nh, g=2, s=2)
                    v5 = view.rearrange("p h (g s w) -> p h g s w", g=2, s=2)
                    g.tensor_tensor(t1, view, cs, ALU.mult)
                    for gg in range(2):
                        for s in range(2):
                            last = g.tensor_tensor(t2[:, :, gg, s, :], v5[:, :, gg, 1 - s, :],
                                                   sn[:, gg, s, :].unsqueeze(1).to_broadcast([P, nh, w]), ALU.mult)
                    link(last)
                    done(g.tensor_tensor(view, t1, tmp[:, 1, 0:nh * dim].rearrange("p (h d) -> p h d", h=nh), ALU.add))

                load_bias(0)
                g.dma_start(nw[:], attn_norm[0:1, :].to_broadcast([P, D])).then_inc(mod_loaded, 16)
                norm_rstd(0)
                pool.wait_ge(modrow_made, 1)
                load_bias(1)
                pool.wait_ge(const_loaded, 16)
                for l in range(DEPTH):
                    m = mix[l]
                    proj = m["proj"]
                    g.dma_start(wrow[:, 0:LORA], kv_norm[l:l + 1, :].to_broadcast([P, LORA])).then_inc(wrow_loaded, 16)
                    g.dma_start(wrow[:, LORA:LORA + HD], q_norm[l:l + 1, :].to_broadcast([P, HD])).then_inc(wrow_loaded, 16)
                    g.dma_start(wrow[:, LORA + HD:], k_norm[l:l + 1, :].to_broadcast([P, HD])).then_inc(wrow_loaded, 16)
                    if l:
                        pool.wait_ge(qk_rope, 2 * l)
                        pool.wait_ge(qk_made, 7 * l)
                    g.dma_start(cc[:], cache_ckv[0, l]).then_inc(ckvc_loaded, 16)
                    g.dma_start(kpe[:], cache_krope[0, l]).then_inc(ckvc_loaded, 16)
                    pool.wait_ge(htok_made, NT * 2 * l + NT)
                    g.dma_start(S0, state_ret[0, l].rearrange("a h d e -> d a h e")).then_inc(s0_loaded, 16)
                    for t in range(NT):
                        rstd(pstat[:, 8 + t:9 + t], stat[:, 8 + t:9 + t], 1.0 / LORA, ckv_ss, NT * l + t + 1, ckv_rstd)
                    pool.wait_ge(ckv_made, NT * l + 1)
                    g.dma_start(new_ckv[0, l], proj[:, 0, CKV:CKV + LORA]).then_inc(cache_stored, 16)
                    pool.wait_ge(proj_made, NB * NT * l + NT * 2)
                    g.dma_start(new_krope[0, l], proj[:, 0, KRP:KRP + ROPE]).then_inc(cache_stored, 16)
                    pool.wait_ge(ckvc_loaded, 32 * (l + 1))
                    pool.wait_ge(proj_made, NB * NT * l + NT * 2)
                    pool.wait_ge(wrow_loaded, 48 * (l + 1))
                    for kt in range(4):
                        src = kpe[:] if kt == 1 else proj[:, (0, 1, 1, 2)[kt], KRP:KRP + ROPE]
                        last = g.tensor_tensor(ktail[:, kt, :], src, wrow[:, LORA + HD + NOPE:], ALU.mult)
                    link(last)
                    for kt in (2, 3):
                        rope(ktail[:, kt:kt + 1, :], "cosm", "sinm", kt - 1, 1, ROPE, m["rt"], link)
                    pool.wait_ge(tail_ss, l + 1)
                    g.tensor_scalar(pstat[:, 28:32], stat[:, 56:60], 1.0 / HD, EPS, ALU.mult, ALU.add).then_inc(tail_eps, 1)
                    for t in range(NT):
                        o = 32 + 8 * t
                        rstd(pstat[:, o:o + 8], pstat[:, o:o + 8], 1.0 / HD, qk_ss, 7 * l + t + 1, qk_rstd)
                    for t in (1, 2):
                        pool.wait_ge(qk_made, 7 * l + t + 1)
                        v = proj[:, t, Q:Q + HEADS * HD].rearrange("p (h d) -> p h d", h=HEADS)[:, :, NOPE:HD]
                        rope(v, "cosm", "sinm", t, HEADS, ROPE, m["rt"], lambda ins: ins.then_inc(qk_rope, 1))
                        pool.wait_ge(qk_rope, 2 * l + t)
                    for part, pos in ((QR, 7), (KR, 9)):
                        pool.wait_ge(proj_made, NB * NT * l + NT * pos)
                        for t in (1, 2):
                            v = proj[:, t, part:part + RH * RD].rearrange("p (h d) -> p h d", h=RH)
                            rope(v, "cosr", "sinr", t, RH, RD, m["rt"], link)
                            if part == KR:
                                g.drain().then_inc(kr_roped, 1)
                    store_mod(ADA_UNITS * l + 1)
                    for t in range(NT):
                        rstd(pstat[:, 16 + 4 * t:20 + 4 * t], stat[:, 16 + 4 * t:20 + 4 * t], 1.0 / RD, ro_ss,
                             NT * l + t + 1, ro_rstd)
                    pool.wait_ge(st_made, 4 * l + 2)
                    for d in range(2):
                        g.dma_start(new_state[0, l, d].rearrange("h d e -> d h e"), m["st"][:, d]).then_inc(state_stored, 16)
                    load_gate(l, 0)
                    store_mod(ADA_UNITS * l + 2)
                    for kt in range(4):
                        o = 56 + 8 * kt
                        pool.wait_ge(qk_ss, 7 * l + 3 + kt + 1)
                        link(g.tensor_scalar(pstat[:, o:o + 8], pstat[:, o:o + 8], 1.0 / HD, pstat[:, 28 + kt:29 + kt], ALU.mult, ALU.add))
                        g.tensor_tensor(pstat[:, o:o + 8], pstat[:, o:o + 8], half[:], ALU.pow).then_inc(qk_rstd, 1)
                    pool.wait_ge(state_stored, 32 * (l + 1))
                    pool.wait_ge(s_psum, 24 * (l + 1))
                    load_sb(2 * l + 1)
                    if l == 0:
                        store_mod(ADA_UNITS)
                    norm_rstd(2 * l + 1)
                    load_gate(l, 1)
                    if l == 1:
                        pool.wait_ge(x1_made, 24)
                        g.dma_start(moe["wr"][:], w_router[0].rearrange("(k p) n -> p k n", p=P)).then_inc(wr_loaded, 16)
                    if l == 0:
                        pool.wait_ge(htok_made, NT * 2)
                        load_sb(2)
                        norm_rstd(2)
                    else:
                        pool.wait_ge(htok_made, NT * 4)
                        g.memset(ysum, 0.0).then_inc(sums_zeroed, 1)
                        g.drain().then_inc(pool_phase, 1)
                for t in range(NT):
                    pool.wait_ge(x2_made, NT + t + 1)
                    dst = y_prompt[0] if t == 0 else y_sample[0, P * (t - 1):P * t, :]
                    g.dma_start(dst, x[:, t, :]).then_inc(y_stored, 16)
                pool.wait_ge(y_stored, 16 * NT)
                pool.wait_ge(cache_stored, 32 * DEPTH)
                pool.wait_ge(state_stored, 32 * DEPTH)

            @block.scalar
            def _(act):
                s = nc.scalar
                phase = [0]
                nxt = [0]

                def barrier(pool_too=False):
                    phase[0] += 1
                    s.drain().then_inc(act_phase, 1)
                    for q in (pe_phase, dve_phase):
                        act.wait_ge(q, phase[0])
                    if pool_too:
                        act.wait_ge(pool_phase, 1)

                def split_to(m):
                    while nxt[0] <= m and nxt[0] < len(splits):
                        q = splits[nxt[0]]
                        raw_wait(act, q["n"])
                        if pre_free(q["m"]):
                            act.wait_ge(*pre_free(q["m"]))
                        z = q["size"]
                        s.activation(whi[:, q["m"] % RING, 0:z], raw[:, q["n"] % RING, 0:z], ACT.Copy).then_inc(hi_made, 1)
                        nxt[0] += 1

                act.wait_ge(c_loaded, 32)
                s.activation(craw, craw, ACT.Silu).then_inc(c_silu, 1)
                act.wait_ge(decay_loaded, 16)
                s.activation(lgt[:, 1, :], lgt[:, 0, :], ACT.Abs).then_inc(act_chain, 1)
                act.wait_ge(act_chain, 1)
                s.activation(lgt[:, 1, :], lgt[:, 1, :], ACT.Exp, scale=-1.0).then_inc(act_chain, 1)
                act.wait_ge(act_chain, 2)
                s.activation(lgt[:, 1, :], lgt[:, 1, :], ACT.Ln, bias=1.0).then_inc(sigmoid_made, 1)

                def squares(n, m, ready):
                    for t in range(NT):
                        act.wait_ge(*ready(t))
                        s.activation(m["htok"][:, t, :], x[:, t, :], ACT.Square, accum_out=stat[:, t:t + 1]).then_inc(ss_made, 1)

                def norm(n, m):
                    for t in range(NT):
                        if n == 3:
                            act.wait_ge(htok_made, NT * n + t + 1)
                            s.activation(moe["hth"][:, t, :], m["htok"][:, t, :], ACT.Copy).then_inc(hth_made, 1)
                        act.wait_ge(hT_psum, NT * n + t + 1)
                        for b in range(2):
                            s.activation(m["hTh"][:, 4 * b:4 * b + 4, P * t:P * (t + 1)],
                                         psum[2 * t + b][:].rearrange("p (c i) -> p c i", c=4), ACT.Copy)\
                                .then_inc(hT_hi_made, 1)

                squares(0, mix[0], lambda t: (x_rest if t else x_loaded, 16))
                for i in range(4):
                    kind, hf = divmod(i, 2)
                    act.wait_ge(spread_psum, 4 * kind + 3 + hf)
                    s.activation(modsb[:, kind, 0, 512 * hf:512 * (hf + 1)], psum[SPREAD_BANK[4 * kind + 2 + hf]][:], ACT.Copy)\
                        .then_inc(shift_made, 1)
                    if i == 1:
                        split_to(IN[0, 0]["m"])
                split_to(IN[0, 0]["m"] + 1)
                for l in range(DEPTH):
                    m = mix[l]
                    proj = m["proj"]
                    norm(2 * l, m)
                    for p in range(NB):
                        split_to(min(IN[l, p]["m"] + 2, UKV[l]["m"]))
                        c0 = IN_ORDER[p] * BLK
                        wd = min(BLK, IN_COLS - c0)
                        for t in range(NT):
                            act.wait_ge(proj_psum, NB * NT * l + NT * p + t + 1)
                            s.activation(proj[:, t, c0:c0 + wd], psum[3 * (p % 2) + t][:, 0:wd], ACT.Copy).then_inc(proj_made, 1)
                        if p == 1:
                            act.wait_ge(proj_made, NB * NT * l + NT * 2)
                            for t in range(NT):
                                if t:
                                    act.wait_ge(ckv_ss, NT * l + t)
                                s.activation(m["sq"][:, 0:LORA], proj[:, t, CKV:CKV + LORA], ACT.Square,
                                             accum_out=stat[:, 8 + t:9 + t]).then_inc(ckv_ss, 1)
                        if p == 2:
                            act.wait_ge(dec_arg, l + 1)
                            s.activation(sbflat[:, 0:1024], sbflat[:, 0:1024], ACT.Exp).then_inc(dec_exp, 1)
                            s.activation(sbflat[:, 1024:2048], sbflat[:, 1024:2048], ACT.Exp).then_inc(dec_exp, 1)
                            s.activation(dec[:], dec[:], ACT.Exp).then_inc(dec_exp, 1)
                        if p == 2:
                            act.wait_ge(ckvc_loaded, 32 * (l + 1))
                            for kt in range(4):
                                src = kpe[:] if kt == 1 else proj[:, (0, 1, 1, 2)[kt], KRP:KRP + ROPE]
                                act.wait_ge(ckv_ss, NT * (l + 1))
                                last = s.activation(m["sq"][:, ROPE * kt:ROPE * (kt + 1)], src, ACT.Square, accum_out=stat[:, 56 + kt:57 + kt])
                            last.then_inc(tail_ss, 1)
                        if 5 <= p < 5 + NT:
                            t = p - 5
                            act.wait_ge(proj_made, NB * NT * l + NT * 5)
                            act.wait_ge(tail_ss, l + 1)
                            if t:
                                act.wait_ge(qk_ss, 7 * l + t)
                            s.activation(m["sq"], proj[:, t, Q:Q + HEADS * HD], ACT.Square).then_inc(q_sq, 1)
                    split_to(UKV[l]["m"])
                    barrier()
                    for t in range(NT):
                        act.wait_ge(rT_psum, 2 * NT * l + 2 * t + 1)
                        s.activation(m["qrT"][:, t], psum[2 * t][:].rearrange("p (h i) -> p h i", h=RH), ACT.Copy).then_inc(rT_made, 1)
                    for t in range(NT):
                        s.activation(proj[:, t, GG:GG + 512], proj[:, t, GG:GG + 512], ACT.Silu).then_inc(silu_g, 1)
                    for t in range(NT):
                        act.wait_ge(ro_psum, NT * l + t + 1)
                        s.activation(m["at"][:, t].rearrange("p h i -> p (h i)"), psum[t][:], ACT.Square).then_inc(ro_sq, 1)
                    for b in range(2):
                        act.wait_ge(ckvT_psum, 2 * l + b + 1)
                        s.activation(m["cTh"][:, :, 256 * b:256 * (b + 1)],
                                     psum[CKV_BANK[b]][:].rearrange("p (k i) -> p k i", k=2), ACT.Copy).then_inc(ckvT_hi, 1)

                    def head_evac(i):
                        act.wait_ge(hT2_psum, 14 * l + 2 * i + 1)
                        dst = m["qT"][:, 0:4, P * i:P * (i + 1)] if i < NT else kT[:, 0:4, P * (i - NT):P * (i - NT + 1)]
                        s.activation(dst, psum[HEAD_BANK[i]][0:HD, :].rearrange("p (h i) -> p h i", h=4), ACT.Copy).then_inc(headT_lo, 1)

                    act.wait_ge(ro_ss, NT * (l + 1))
                    for kt in range(4):
                        if kt >= 2:
                            act.wait_ge(qk_ss, 7 * l + 3 + kt - 1)
                        for hb in range(2):
                            act.wait_ge(ukv_psum, 8 * l + 2 * kt + hb + 1)
                            src = psum[UKV_BANK[kt] + hb][:].rearrange("p (h e) -> p h e", h=4)
                            s.activation(m["sqk"][:, kt % 2, 4 * hb:4 * hb + 4, :], src[:, :, 0:NOPE], ACT.Square).then_inc(sqk_made, 1)
                            s.activation(m["v"][:, kt, 4 * hb:4 * hb + 4, :], src[:, :, NOPE:NOPE + VD], ACT.Copy).then_inc(v_made, 1)
                        if kt < NT:
                            head_evac(kt)
                    for i in range(NT, 7):
                        head_evac(i)
                    for u in range(24):
                        nk = P if u < HEADS else 3 * P
                        act.wait_ge(negmax, 24 * l + u + 1)
                        if u >= 3:
                            act.wait_ge(pT_psum, 24 * l + u - 2)
                        s.activation(proj[:, u % 3, KR:KR + nk], psum[SCORE_BANK[u % 3]][:, 0:nk], ACT.Exp,
                                     bias=stat[:, 32 + u:33 + u], accum_out=pstat[:, 96 + u:97 + u]).then_inc(exp_made, 1)
                        if u in OUT_AT:
                            split_to(OUT[l, OUT_AT[u]]["m"])
                    split_to(OUT[l, 0]["m"] + 1)
                    for t in range(NT):
                        act.wait_ge(mT_psum, NT * l + t + 1)
                        for b in range(2):
                            s.activation(m["mTh"][:, 4 * b:4 * b + 4, P * t:P * (t + 1)],
                                         psum[2 * t + b][:].rearrange("p (c i) -> p c i", c=4), ACT.Copy).then_inc(mT_hi, 1)
                    split_to(OUT[l, 3]["m"] + (2 if l == 0 else 0))
                    squares(2 * l + 1, (ffn, moe)[l], lambda t: (x1_made, 12 * l + 9 + t + 1))
                    if l == 0:
                        split_to(DM + 2)
                    norm(2 * l + 1, (ffn, moe)[l])
                    if l == 0:
                        def dense_split(off, it):
                            n0, m0 = DN + off, DM + off
                            raw_wait(act, n0, it)
                            act.wait_ge(*dense_free(off, it))
                            s.activation(whi[:, m0 % RING, :], raw[:, n0 % RING, :], ACT.Copy).then_inc(hi_made, 1)

                        def dense_evac(i, par):
                            for ft in range(2):
                                act.wait_ge(gate_done, 2 * i + ft + 1)
                                s.activation(ffn["sg"][:, ft, :], psum[6][:, 0:TOK], ACT.Silu).then_inc(gate_silu, 1)
                                act.wait_ge(act_made, 2 * i + ft + 1)
                                s.activation(ffn["acth"][:, par, ft, :], ffn["act"][:, ft, :], ACT.Copy).then_inc(acth_made, 1)

                        dense_evac(0, 0)
                        with act.Fori(0, (DENSE - 1) // 2) as b:
                            for h in range(2):
                                i = 2 * b + h
                                dense_split(3, i)
                                dense_split(4, i)
                                dense_evac(2 * b + (h + 1), (h + 1) % 2)
                                dense_split(5, i)
                        nxt[0] = DM + 3 * DENSE
                        split_to(IN[1, 0]["m"] + 1)
                        act.wait_ge(state_stored, 32)
                        squares(2, mix[1], lambda t: (x2_made, t + 1))
                        split_to(IN[1, 0]["m"] + 2)
                    else:
                        act.wait_ge(wr_loaded, 16)
                        s.activation(moe["wrh"][:], moe["wr"][:], ACT.Copy).then_inc(wr_hi, 1)
                        for k in range(2):
                            expert_hi(act, s, 0, k, static=True)
                        act.wait_ge(lgT_psum, 1)
                        s.activation(moe["lgT"][:], psum[0][0:8, 0:TOK], ACT.Copy).then_inc(lgT_made, 1)
                        act.wait_ge(route_made, 1)
                        s.activation(moe["r"][:, 1, :, 0:1], moe["r"][:, 1, :, 0:1], ACT.Exp).then_inc(lg_exp, 1)
                        expert_hi(act, s, 0, 2, static=True)
                        barrier(pool_too=True)
                        act_expert = make_act_expert(act, s)
                        act_gather(act, s, 0)
                        act_turn(act, s, 0)
                        with act.Fori(0, EXPERTS - 1) as e:
                            act_expert(e, True)
                        r, _ = extra_items(act, s, lambda r, e, e1, q: act_expert(r, True))
                        act_expert(r, False)

            @block.vector
            def _(dve):
                v = nc.vector
                phase = [0]
                nxt = [0]
                chain = [0]

                def link(ins):
                    chain[0] += 1
                    ins.then_inc(dve_chain, 1)
                    dve.wait_ge(dve_chain, chain[0])

                def barrier(pool_too=False):
                    phase[0] += 1
                    v.drain().then_inc(dve_phase, 1)
                    for q in (pe_phase, act_phase):
                        dve.wait_ge(q, phase[0])
                    if pool_too:
                        dve.wait_ge(pool_phase, 1)

                def split_to(m):
                    while nxt[0] <= m and nxt[0] < len(splits):
                        q = splits[nxt[0]]
                        dve.wait_ge(hi_made, q["m"] + 1)
                        z = q["size"]
                        v.tensor_tensor(wlo[:, q["m"] % RING, 0:z], raw[:, q["n"] % RING, 0:z],
                                        whi[:, q["m"] % RING, 0:z].bitcast(f32), ALU.subtract).then_inc(lo_made, 1)
                        nxt[0] += 1

                link(v.memset(cT[:], 0.0))
                dve.wait_ge(cT_psum, 1)
                v.tensor_copy(cT[:, :, 0:2], psum[5][:, 0:2 * DK].rearrange("p (v k) -> p k v", v=2)).then_inc(cT_made, 1)
                dve.wait_ge(sigmoid_made, 1)
                link(v.tensor_scalar(lg[:].rearrange("p l d -> p (l d)"), lgt[:, 0, :], 0.0, None, ALU.min))
                link(v.tensor_tensor(lg[:].rearrange("p l d -> p (l d)"), lg[:].rearrange("p l d -> p (l d)"), lgt[:, 1, :],
                                     ALU.subtract))

                def make_modrow(u):
                    dve.wait_ge(ada_used, DK * (u + 1))
                    dve.wait_ge(bias_loaded, 64 * (u + 1))
                    if u > 1:
                        dve.wait_ge(mod_stored, 16 * (u - 1))
                    elif u == 1:
                        dve.wait_ge(spread_psum, 8)
                    v.tensor_tensor(modrow[:], psum[6 + u % 2][:], brow[:], ALU.add).then_inc(modrow_made, 1)

                def make_scale(n):
                    dve.wait_ge(mod_loaded, 16 + 80 * n)
                    for kind in range(2):
                        last = v.scalar_tensor_tensor(out=modsb[:, kind, 1, :], in0=modsb[:, kind, 1, :], scalar=1.0,
                                                      in1=nw[:], op0=ALU.add, op1=ALU.mult)
                    link(last)

                def first_scale(kind):
                    for hf in range(2):
                        dve.wait_ge(spread_psum, 4 * kind + hf + 1)
                        cs = slice(512 * hf, 512 * (hf + 1))
                        last = v.scalar_tensor_tensor(out=modsb[:, kind, 1, cs], in0=psum[SPREAD_BANK[4 * kind + hf]][:], scalar=1.0,
                                                      in1=nw[:, cs], op0=ALU.add, op1=ALU.mult)
                    link(last)

                def norm(n, m, between=None, after0=None):
                    def scale(t):
                        h = m["htok"][:, t, :]
                        if n == 0 and t < 2:
                            first_scale(KIND[t])
                        dve.wait_ge(rstd_made, NT * n + t + 1)
                        link(v.scalar_tensor_tensor(out=h, in0=x[:, t, :], scalar=pstat[:, t:t + 1],
                                                    in1=modsb[:, KIND[t], 1, :], op0=ALU.mult, op1=ALU.mult))
                        if n == 0:
                            dve.wait_ge(shift_made, 4 if t else 2)
                        v.tensor_tensor(h, h, modsb[:, KIND[t], 0, :], ALU.add).then_inc(htok_made, 1)

                    def low(t):
                        if n == 3:
                            dve.wait_ge(hth_made, t + 1)
                            v.tensor_tensor(moe["htl"][:, t, :], m["htok"][:, t, :], moe["hth"][:, t, :].bitcast(f32),
                                            ALU.subtract).then_inc(htl_made, 1)
                        for b in range(2):
                            dve.wait_ge(hT_hi_made, 2 * NT * n + 2 * t + b + 1)
                            c = slice(4 * b, 4 * b + 4)
                            v.tensor_tensor(m["hTl"][:, c, P * t:P * (t + 1)],
                                            psum[2 * t + b][:].rearrange("p (c i) -> p c i", c=4),
                                            m["hTh"][:, c, P * t:P * (t + 1)].bitcast(f32), ALU.subtract).then_inc(hT_made, 1)

                    scale(0)
                    if after0:
                        after0()
                    scale(1)
                    low(0)
                    scale(2)
                    if between:
                        between()
                    low(1)
                    low(2)

                make_modrow(0)
                dve.wait_ge(mod_loaded, 16)
                def residual(t):
                    if t:
                        dve.wait_ge(x2_made, t)
                    for hf in range(2):
                        dve.wait_ge(down_tile, t + 1)
                        cs = slice(512 * hf, 512 * (hf + 1))
                        link(v.tensor_tensor(ffn["tmp"][:, hf, :], psum[2 * t + hf][:], modg[:, KIND[t], cs], ALU.mult))
                        last = v.tensor_tensor(x[:, t, cs], x[:, t, cs], ffn["tmp"][:, hf, :], ALU.add)
                    last.then_inc(x2_made, 1)

                for l in range(DEPTH):
                    m = mix[l]
                    proj = m["proj"]
                    norm(2 * l, m, lambda: split_to(IN[l, 0]["m"] + (1, 2)[l]), (lambda: residual(2)) if l else (lambda: split_to(IN[0, 0]["m"])))
                    if l == 0:
                        dve.wait_ge(const_loaded, 16)
                    dve.wait_ge(htok_made, NT * (2 * l + 1))
                    lgl = lg[:, l, :]
                    lgb = lgl.rearrange("p (d h) -> p d h", d=2).unsqueeze(3).to_broadcast([P, 2, RH, P])

                    def rows(name):
                        return cst(name).rearrange("p (d i) -> p d i", d=2).unsqueeze(2).to_broadcast([P, 2, RH, P])
                    v.tensor_scalar(dec[:, 1, :], lgl, float(P), None, ALU.mult)
                    v.tensor_tensor(dec[:, 0, :].rearrange("p (d h) -> p d h", d=2), lgl.rearrange("p (d h) -> p d h", d=2),
                                    cst("kexp").unsqueeze(2).to_broadcast([P, 2, RH]), ALU.mult)
                    for d in range(2):
                        lb = lgl[:, RH * d:RH * (d + 1)].unsqueeze(2).to_broadcast([P, RH, P])
                        v.tensor_tensor(qdec[:, d], cst("qexp")[:, P * d:P * (d + 1)].unsqueeze(1).to_broadcast([P, RH, P]), lb, ALU.mult)
                        last = v.tensor_tensor(mtmp[:, d], cst("dexp")[:, P * d:P * (d + 1)].unsqueeze(1).to_broadcast([P, RH, P]), lb, ALU.mult)
                    last.then_inc(dec_arg, 1)
                    for p in range(NB):
                        split_to(min(IN[l, p]["m"] + 2, UKV[l]["m"]))
                        if p == 3:
                            dve.wait_ge(wrow_loaded, 48 * (l + 1))
                            for t in range(NT):
                                dve.wait_ge(ckv_rstd, NT * l + t + 1)
                                ck = proj[:, t, CKV:CKV + LORA]
                                v.scalar_tensor_tensor(out=ck, in0=ck, scalar=pstat[:, 8 + t:9 + t], in1=wrow[:, 0:LORA],
                                                       op0=ALU.mult, op1=ALU.mult).then_inc(ckv_made, 1)
                            link(v.tensor_scalar(wrow[:, LORA:LORA + HD], wrow[:, LORA:LORA + HD], HD ** -0.5, None, ALU.mult))
                            link(v.tensor_tensor(wrow[:, LORA:LORA + NOPE], wrow[:, LORA:LORA + NOPE],
                                                 wrow[:, LORA + HD:LORA + HD + NOPE], ALU.mult))
                        if p == 4:
                            dve.wait_ge(dec_exp, 3 * (l + 1))
                            for d in range(2):
                                last = v.tensor_tensor(mtmp[:, d], mtmp[:, d],
                                                       cst("tri")[:, P * d:P * (d + 1)].unsqueeze(1).to_broadcast([P, RH, P]), ALU.mult)
                            v.tensor_scalar(dec[:, 0, :], dec[:, 0, :], RD ** -0.5, None, ALU.mult)
                            link(last)
                            link(v.tensor_tensor(maskT, maskT, mtmp[:, 1], ALU.add))
                        if 6 <= p < 6 + NT:
                            t = p - 6
                            dve.wait_ge(q_sq, NT * l + t + 1)
                            v.tensor_reduce(pstat[:, 32 + 8 * t:40 + 8 * t], m["sq"].rearrange("p (h d) -> p h d", h=HEADS),
                                            axis=AX.X, op=ALU.add).then_inc(qk_ss, 1)
                        if 8 <= p < 8 + NT:
                            t = p - 8
                            src = proj[:, t, Q:Q + HEADS * HD].rearrange("p (h d) -> p h d", h=HEADS)
                            dve.wait_ge(qk_rstd, 7 * l + t + 1)
                            link(v.tensor_tensor(src, src, pstat[:, 32 + 8 * t:40 + 8 * t].unsqueeze(2).to_broadcast([P, HEADS, HD]), ALU.mult))
                            v.tensor_tensor(src, src, wrow[:, LORA:LORA + HD].unsqueeze(1).to_broadcast([P, HEADS, HD]),
                                            ALU.mult).then_inc(qk_made, 1)
                        if p == 9:
                            make_modrow(ADA_UNITS * l + 1)
                    split_to(UKV[l]["m"])
                    barrier()
                    for i, (t, d) in enumerate(((0, 0), (0, 1), (1, 0), (2, 1))):
                        if t:
                            dve.wait_ge(kr_roped, 2 * l + t)
                        kr = proj[:, t, KR:KR + RH * RD].rearrange("p (h e) -> p h e", h=RH)
                        v.tensor_tensor(m["kd"][:, i], kr, dec[:, 0, RH * d:RH * (d + 1)].unsqueeze(2).to_broadcast([P, RH, RD]),
                                        ALU.mult).then_inc(kd_made, 1)
                    for t in range(NT):
                        dve.wait_ge(rT_psum, 2 * NT * l + 2 * t + 2)
                        v.tensor_scalar(m["krT"][:, t], psum[2 * t + 1][:].rearrange("p (h i) -> p h i", h=RH), RD ** -0.5, None,
                                        ALU.mult).then_inc(qd_made, 1)
                        if t:
                            dve.wait_ge(rT_made, NT * l + t + 1)
                            for d in range(2):
                                v.tensor_tensor(m["qd"][:, 2 * (t - 1) + d], m["qrT"][:, t], qdec[:, d], ALU.mult).then_inc(qd_made, 1)
                    for t in range(NT):
                        dve.wait_ge(sc_psum, NT * l + t + 1)
                        v.tensor_tensor(m["at"][:, t], psum[t][:].rearrange("p (h i) -> p h i", h=RH), maskT, ALU.mult).then_inc(sc_masked, 1)
                    make_modrow(ADA_UNITS * l + 2)
                    dve.wait_ge(s0_loaded, 16 * (l + 1))
                    for i in range(4):
                        dve.wait_ge(st_psum, 4 * l + i + 1)
                        up = psum[3 + i % 3][:].rearrange("p (h e) -> p h e", h=RH)
                        if i < 2:
                            v.tensor_copy(m["st"][:, i], up).then_inc(st_made, 1)
                        else:
                            d = i - 2
                            link(v.tensor_tensor(S1[:, d], S0[:, d], dec[:, 1, RH * d:RH * (d + 1)].unsqueeze(2).to_broadcast([P, RH, RD]), ALU.mult))
                            v.tensor_tensor(S1[:, d], S1[:, d], up, ALU.add).then_inc(st_made, 1)
                    for t in range(NT):
                        dve.wait_ge(ro_sq, NT * l + t + 1)
                        v.tensor_reduce(stat[:, 16 + 4 * t:20 + 4 * t], m["at"][:, t], axis=AX.X, op=ALU.add).then_inc(ro_ss, 1)
                    for b in range(2):
                        dve.wait_ge(ckvT_hi, 2 * l + b + 1)
                        v.tensor_tensor(m["cTl"][:, :, 256 * b:256 * (b + 1)], psum[CKV_BANK[b]][:].rearrange("p (k i) -> p k i", k=2),
                                        m["cTh"][:, :, 256 * b:256 * (b + 1)].bitcast(f32), ALU.subtract).then_inc(ckvT_made, 1)
                    for t in range(NT):
                        dve.wait_ge(ro_rstd, NT * l + t + 1)
                        dst = proj[:, t, QR:QR + RH * RD].rearrange("p (h e) -> p h e", h=RH)
                        link(v.tensor_tensor(dst, psum[t][:].rearrange("p (h e) -> p h e", h=RH),
                                             pstat[:, 16 + 4 * t:20 + 4 * t].unsqueeze(2).to_broadcast([P, RH, RD]), ALU.mult))
                        dve.wait_ge(silu_g, NT * l + t + 1)
                        v.tensor_tensor(proj[:, t, QR:QR + 512], proj[:, t, QR:QR + 512], proj[:, t, GG:GG + 512],
                                        ALU.mult).then_inc(ro_made, 1)
                    def key_ss(kt):
                        dve.wait_ge(sqk_made, 8 * l + 2 * kt + 2)
                        v.tensor_reduce(pstat[:, 56 + 8 * kt:64 + 8 * kt], m["sqk"][:, kt % 2], axis=AX.X, op=ALU.add).then_inc(qk_ss, 1)

                    def key_scale(kt):
                        dve.wait_ge(qk_rstd, 7 * l + NT + kt + 1)
                        r = pstat[:, 56 + 8 * kt:64 + 8 * kt]
                        for hb in range(2):
                            v.tensor_tensor(m["kcat"][kt][:, 4 * hb:4 * hb + 4, 0:NOPE],
                                            psum[UKV_BANK[kt] + hb][:].rearrange("p (h e) -> p h e", h=4)[:, :, 0:NOPE],
                                            r[:, 4 * hb:4 * hb + 4].unsqueeze(2).to_broadcast([P, 4, NOPE]), ALU.mult)
                        v.tensor_tensor(m["kcat"][kt][:, :, NOPE:HD], ktail[:, kt, :].unsqueeze(1).to_broadcast([P, HEADS, ROPE]),
                                        r.unsqueeze(2).to_broadcast([P, HEADS, ROPE]), ALU.mult).then_inc(qk_made, 1)

                    def head_evac(i):
                        dve.wait_ge(hT2_psum, 14 * l + 2 * i + 2)
                        dst = m["qT"][:, 4:8, P * i:P * (i + 1)] if i < NT else kT[:, 4:8, P * (i - NT):P * (i - NT + 1)]
                        v.tensor_copy(dst, psum[HEAD_BANK[i] + 1][0:HD, :].rearrange("p (h i) -> p h i", h=4)).then_inc(headT_hi, 1)

                    for kt in range(4):
                        key_ss(kt)
                        if kt < NT:
                            head_evac(kt)
                        if kt:
                            key_scale(kt - 1)
                    head_evac(NT)
                    key_scale(3)
                    for i in range(NT + 1, 7):
                        head_evac(i)

                    def row_max(u):
                        nk = P if u < HEADS else 3 * P
                        dve.wait_ge(s_psum, 24 * l + u + 1)
                        v.tensor_reduce(stat[:, 32 + u:33 + u], psum[SCORE_BANK[u % 3]][:, 0:nk], axis=AX.X, op=ALU.max, negate=True)\
                            .then_inc(negmax, 1)

                    def divide(t):
                        o = 96 + HEADS * t
                        dve.wait_ge(exp_made, 24 * l + HEADS * (t + 1))
                        link(v.reciprocal(pstat[:, o:o + 8], pstat[:, o:o + 8]))
                        dve.wait_ge(pv_psum, 24 * l + HEADS * (t + 1))
                        v.tensor_tensor(proj[:, t, Q:Q + 512].rearrange("p (h e) -> p h e", h=HEADS),
                                        psum[4 + t % 2][:].rearrange("p (h e) -> p h e", h=HEADS),
                                        pstat[:, o:o + 8].unsqueeze(2).to_broadcast([P, HEADS, VD]), ALU.mult).then_inc(a_made, 1)

                    for u in range(3):
                        row_max(u)
                    for u in range(24):
                        nk = P if u < HEADS else 3 * P
                        dve.wait_ge(pT_psum, 24 * l + u + 1)
                        if u >= 3:
                            dve.wait_ge(pv_psum, 24 * l + u - 2)
                        v.tensor_copy(m["pT"][:, u % 3, 0:nk], psum[2 + u % 2][:, 0:nk]).then_inc(pT_made, 1)
                        if u + 3 < 24:
                            row_max(u + 3)
                        if u % HEADS == 1 and u > HEADS:
                            divide(u // HEADS - 1)
                        if u in OUT_AT:
                            split_to(OUT[l, OUT_AT[u]]["m"])
                    divide(NT - 1)
                    if l == 0:
                        make_modrow(ADA_UNITS)
                    split_to(OUT[l, 0]["m"] + 1)
                    for t in range(NT):
                        for b in range(2):
                            dve.wait_ge(mT_hi, 2 * NT * l + 2 * t + b + 1)
                            c = slice(4 * b, 4 * b + 4)
                            v.tensor_tensor(m["mTl"][:, c, P * t:P * (t + 1)], psum[2 * t + b][:].rearrange("p (c i) -> p c i", c=4),
                                            m["mTh"][:, c, P * t:P * (t + 1)].bitcast(f32), ALU.subtract).then_inc(mT_made, 1)
                    make_scale(2 * l + 1)
                    dve.wait_ge(gate_loaded, 32 * (2 * l + 1))
                    for j in range(4):
                        split_to(OUT[l, j]["m"] + 2 if l == 0 else min(OUT[l, j]["m"] + 2, MM - 1))
                        for t in range(NT):
                            dve.wait_ge(out_psum, 12 * l + 3 * j + t + 1)
                            cs = slice(BLK * j, BLK * (j + 1))
                            n = 3 * j + t
                            if n >= 2:
                                dve.wait_ge(x1_made, 12 * l + n - 1)
                            link(v.tensor_tensor(m["tmp"][:, n % 2, :], psum[3 * (j % 2) + t][:, 0:BLK], modg[:, KIND[t], cs], ALU.mult))
                            v.tensor_tensor(x[:, t, cs], x[:, t, cs], m["tmp"][:, n % 2, :], ALU.add).then_inc(x1_made, 1)
                    norm(2 * l + 1, (ffn, moe)[l], lambda: split_to(DM + 2) if l == 0 else None)
                    if l == 0:
                        def dense_split(off, it):
                            n0, m0 = DN + off, DM + off
                            dve.wait_ge(hi_made, m0 + 1 + 3 * it)
                            v.tensor_tensor(wlo[:, m0 % RING, :], raw[:, n0 % RING, :], whi[:, m0 % RING, :].bitcast(f32),
                                            ALU.subtract).then_inc(lo_made, 1)

                        def dense_evac(i, par):
                            for ft in range(2):
                                dve.wait_ge(gate_silu, 2 * i + ft + 1)
                                dve.wait_ge(up_done, 2 * i + ft + 1)
                                v.tensor_tensor(ffn["act"][:, ft, :], psum[7][:, 0:TOK], ffn["sg"][:, ft, :], ALU.mult).then_inc(act_made, 1)
                                dve.wait_ge(acth_made, 2 * i + ft + 1)
                                v.tensor_tensor(ffn["actl"][:, par, ft, :], ffn["act"][:, ft, :],
                                                ffn["acth"][:, par, ft, :].bitcast(f32), ALU.subtract).then_inc(actl_made, 1)

                        dense_evac(0, 0)
                        with dve.Fori(0, (DENSE - 1) // 2) as b:
                            for h in range(2):
                                i = 2 * b + h
                                dense_split(3, i)
                                dense_split(4, i)
                                dense_evac(2 * b + (h + 1), (h + 1) % 2)
                                dense_split(5, i)
                        nxt[0] = DM + 3 * DENSE
                        make_scale(2)
                        split_to(IN[1, 0]["m"] + 1)
                        dve.wait_ge(gate_loaded, 64)
                        residual(0)
                        residual(1)
                    else:
                        dve_moe(dve, v, link, barrier)

            @block.tensor
            def _(pe):
                mm = nc.tensor.matmul
                phase = [0]
                ada = [0]

                def barrier(pool_too=False):
                    phase[0] += 1
                    nc.tensor.drain().then_inc(pe_phase, 1)
                    for q in (act_phase, dve_phase):
                        pe.wait_ge(q, phase[0])
                    if pool_too:
                        pe.wait_ge(pool_phase, 1)

                def mm3(out, ah, al, bh, bl, first, last):
                    mm(out, ah, bh, start=first, stop=False)
                    mm(out, ah, bl, start=False, stop=False)
                    return mm(out, al, bh, start=False, stop=last)

                def ada_chunk():
                    a = ada[0]
                    q = [z for z in chunks if z["m"] is None][a]
                    u, k = divmod(a, DK)
                    raw_wait(pe, q["n"])
                    if k == 0 and u >= 2:
                        pe.wait_ge(modrow_made, u - 1)
                    for j in range(4):
                        last = mm(psum[6 + u % 2][32 * j:32 * j + 32, :], cT[:, k, :], raw[:, q["n"] % RING, 512 * j:512 * (j + 1)],
                                  start=(k == 0), stop=(k == DK - 1))
                    last.then_inc(ada_used, 1)
                    ada[0] += 1

                def norm(n, m, tiles=range(NT)):
                    for t in tiles:
                        pe.wait_ge(htok_made, NT * n + t + 1)
                        for c_ in range(DK):
                            last = nc.tensor.transpose(psum[2 * t + c_ // 4][:, P * (c_ % 4):P * (c_ % 4 + 1)],
                                                       m["htok"][:, t, P * c_:P * (c_ + 1)], ident)
                        last.then_inc(hT_psum, 1)

                pe.wait_ge(ident_loaded, 16)
                pe.wait_ge(c_silu, 1)
                nc.tensor.transpose(psum[5][:, 0:2 * DK], craw, ident[0:2 * DK, 0:2 * DK]).then_inc(cT_psum, 1)
                pe.wait_ge(cT_made, 1)
                for k in range(DK):
                    ada_chunk()
                pe.wait_ge(modrow_made, 1)
                for i, bank in enumerate(SPREAD_BANK):
                    kind, b, hf = i // 4, 1 - i // 2 % 2, i % 2
                    r0 = 32 * (2 * b + hf) + kind
                    mm(psum[bank][:], ident[:, r0:r0 + 1].to_broadcast([P, P]), modrow[:], start=True, stop=True).then_inc(spread_psum, 1)
                for l in range(DEPTH):
                    m = mix[l]
                    proj = m["proj"]
                    norm(2 * l, m, (0, 1))
                    for p in range(NB):
                        q = IN[l, p]
                        wd = q["shape"]
                        pe.wait_ge(lo_made, q["m"] + 1)
                        wh = whi[:, q["m"] % RING, 0:q["size"]].rearrange("p (k n) -> p k n", n=wd)
                        wl = wlo[:, q["m"] % RING, 0:q["size"]].rearrange("p (k n) -> p k n", n=wd)
                        for t in range(NT):
                            if p == 0:
                                if t == 1:
                                    norm(2 * l, m, (2,))
                                pe.wait_ge(hT_made, 2 * NT * 2 * l + 2 * (t + 1))
                            if p >= 2:
                                pe.wait_ge(proj_made, NB * NT * l + NT * (p - 2) + t + 1)
                            ts = slice(P * t, P * (t + 1))
                            for k in range(DK):
                                last = mm3(psum[3 * (p % 2) + t][:, 0:wd], m["hTh"][:, k, ts], m["hTl"][:, k, ts],
                                           wh[:, k, :], wl[:, k, :], k == 0, k == DK - 1)
                            last.then_inc(proj_psum, 1)
                        for _ in range(ada_extra[p]):
                            ada_chunk()
                    barrier()
                    for t in range(NT):
                        if t:
                            pe.wait_ge(kr_roped, 2 * l + t)
                        for b, part in enumerate((QR, KR)):
                            for h in range(RH):
                                last = nc.tensor.transpose(psum[2 * t + b][:, P * h:P * (h + 1)],
                                                           proj[:, t, part + RD * h:part + RD * (h + 1)], ident)
                            last.then_inc(rT_psum, 1)
                        if t == 0:
                            ada_chunk()
                    for t in range(NT):
                        pe.wait_ge(rT_made, NT * (l + 1))
                        pe.wait_ge(qd_made, 7 * l + (1, 4, 7)[t])
                        for h in range(RH):
                            last = mm(psum[t][:, P * h:P * (h + 1)], m["krT"][:, t, h, :], m["qrT"][:, t, h, :], start=True, stop=True)
                        last.then_inc(sc_psum, 1)
                        if t < ADA_RET - 1:
                            ada_chunk()
                    pe.wait_ge(qd_made, 7 * (l + 1))
                    for i, t in enumerate((0, 0, 1, 2)):
                        pe.wait_ge(kd_made, 4 * l + i + 1)
                        if i == 3:
                            pe.wait_ge(st_made, 4 * l + 1)
                        for h in range(RH):
                            last = mm(psum[3 + i % 3][:, P * h:P * (h + 1)], m["kd"][:, i, h, :],
                                      proj[:, t, VR + RD * h:VR + RD * (h + 1)], start=True, stop=True)
                        last.then_inc(st_psum, 1)
                    pe.wait_ge(s0_loaded, 16 * (l + 1))
                    for t in range(NT):
                        pe.wait_ge(sc_masked, NT * l + t + 1)
                        if t == 1:
                            pe.wait_ge(st_made, 4 * (l + 1))
                        for h in range(RH):
                            o = psum[t][:, P * h:P * (h + 1)]
                            last = mm(o, m["at"][:, t, h, :], proj[:, t, VR + RD * h:VR + RD * (h + 1)], start=True, stop=(t == 0))
                            if t:
                                sf, sb_ = (S0, S1) if t == 1 else (S1, S0)
                                mm(o, m["qd"][:, 2 * (t - 1), h, :], sf[:, 0, h, :], start=False, stop=False)
                                last = mm(o, m["qd"][:, 2 * (t - 1) + 1, h, :], sb_[:, 1, h, :], start=False, stop=True)
                        last.then_inc(ro_psum, 1)
                    pe.wait_ge(ckvc_loaded, 32 * (l + 1))
                    pe.wait_ge(modrow_made, ADA_UNITS * (l + 1))
                    for b in range(2):
                        for i in range(2):
                            kt = 2 * b + i
                            src = cc[:] if kt == 1 else proj[:, (0, 1, 1, 2)[kt], CKV:CKV + LORA]
                            for k in range(2):
                                last = nc.tensor.transpose(psum[CKV_BANK[b]][:, 256 * k + P * i:256 * k + P * (i + 1)], src[:, P * k:P * (k + 1)], ident)
                        last.then_inc(ckvT_psum, 1)
                    q = UKV[l]
                    pe.wait_ge(lo_made, q["m"] + 1)
                    wh = whi[:, q["m"] % RING, :].rearrange("p (k n) -> p k n", n=1024)
                    wl = wlo[:, q["m"] % RING, :].rearrange("p (k n) -> p k n", n=1024)

                    def heads(i):
                        if i < NT:
                            pe.wait_ge(ro_made, NT * (l + 1))
                        else:
                            pe.wait_ge(qk_made, 7 * l + i + 1)
                        for hb in range(2):
                            if i not in (0, 4, 6):
                                pe.wait_ge((headT_lo, headT_hi)[hb], 7 * l + (4 if i == 5 else i))
                            for h in range(4):
                                hh = 4 * hb + h
                                src = m["kcat"][i - NT][:, hh, :] if i >= NT else proj[:, i, Q + HD * hh:Q + HD * (hh + 1)]
                                last = nc.tensor.transpose(psum[HEAD_BANK[i] + hb][0:HD, P * h:P * (h + 1)], src, ident)
                            last.then_inc(hT2_psum, 1)

                    for kt in range(4):
                        pe.wait_ge(ckvT_made, 2 * l + kt // 2 + 1)
                        ts = slice(P * kt, P * (kt + 1))
                        if kt == 0:
                            pe.wait_ge(st_made, 4 * (l + 1))
                        if kt == 3:
                            pe.wait_ge(qk_made, 7 * l + NT + 1)
                            pe.wait_ge(v_made, 8 * l + 2)
                        for hb in range(2):
                            for k in range(2):
                                cs = slice(512 * hb, 512 * (hb + 1))
                                last = mm3(psum[UKV_BANK[kt] + hb][:], m["cTh"][:, k, ts], m["cTl"][:, k, ts],
                                           wh[:, k, cs], wl[:, k, cs], k == 0, k == 1)
                            last.then_inc(ukv_psum, 1)
                        if kt < NT:
                            heads(kt)
                    pe.wait_ge(v_made, 8 * (l + 1))
                    for i in range(NT, 7):
                        heads(i)
                    pe.wait_ge(headT_lo, 7 * (l + 1))
                    pe.wait_ge(headT_hi, 7 * (l + 1))

                    def scores(u):
                        t, h = divmod(u, HEADS)
                        k0, nk = (0, P) if t == 0 else (P, 3 * P)
                        mm(psum[SCORE_BANK[u % 3]][:, 0:nk], m["qT"][:, h, P * t:P * (t + 1)], kT[:, h, k0:k0 + nk], start=True, stop=True)\
                            .then_inc(s_psum, 1)

                    def values(u):
                        t, h = divmod(u, HEADS)
                        n = 1 if t == 0 else 3
                        pe.wait_ge(pT_made, 24 * l + u + 1)
                        if h == 0 and t == 2:
                            pe.wait_ge(a_made, 3 * l + 1)
                        for i in range(n):
                            kt = i + (0 if t == 0 else 1)
                            last = mm(psum[4 + t % 2][:, VD * h:VD * (h + 1)], m["pT"][:, u % 3, P * i:P * (i + 1)],
                                      m["v"][:, kt, h, :], start=(i == 0), stop=(i == n - 1))
                        last.then_inc(pv_psum, 1)

                    for u in range(3):
                        scores(u)
                    for u in range(24):
                        n = 1 if u < HEADS else 3
                        pe.wait_ge(exp_made, 24 * l + u + 1)
                        for i in range(n):
                            last = nc.tensor.transpose(psum[2 + u % 2][:, P * i:P * (i + 1)], proj[:, u % 3, KR + P * i:KR + P * (i + 1)], ident)
                        last.then_inc(pT_psum, 1)
                        if u + 3 < 24:
                            scores(u + 3)
                        if l == 0 and u in ADA_AT:
                            ada_chunk()
                        if u:
                            values(u - 1)
                    values(23)
                    for t in range(NT):
                        pe.wait_ge(a_made, 3 * l + t + 1)
                        for c_ in range(DK):
                            o = Q + P * c_ if c_ < 4 else QR + P * (c_ - 4)
                            last = nc.tensor.transpose(psum[2 * t + c_ // 4][:, P * (c_ % 4):P * (c_ % 4 + 1)], proj[:, t, o:o + P], ident)
                        last.then_inc(mT_psum, 1)
                    for j in range(4):
                        q = OUT[l, j]
                        pe.wait_ge(lo_made, q["m"] + 1)
                        wh = whi[:, q["m"] % RING, :].rearrange("p (k n) -> p k n", n=BLK)
                        wl = wlo[:, q["m"] % RING, :].rearrange("p (k n) -> p k n", n=BLK)
                        for t in range(NT):
                            if j == 0:
                                pe.wait_ge(mT_made, 2 * NT * l + 2 * (t + 1))
                            if j >= 2:
                                pe.wait_ge(x1_made, 12 * l + 3 * (j - 2) + t + 1)
                            ts = slice(P * t, P * (t + 1))
                            for k in range(DK):
                                last = mm3(psum[3 * (j % 2) + t][:, 0:BLK], m["mTh"][:, k, ts], m["mTl"][:, k, ts],
                                           wh[:, k, :], wl[:, k, :], k == 0, k == DK - 1)
                            last.then_inc(out_psum, 1)
                    norm(2 * l + 1, (ffn, moe)[l])
                    if l == 0:
                        pe_dense(pe, mm)
                    else:
                        pe_moe(pe, mm, mm3, barrier)



_INS = ["x_prompt", "x_sample", "cache_ckv", "cache_krope", "state_ret", "c", "c_ctx", "attn_norm", "ffn_norm", "w_ada",
        "b_ada", "w_in", "kv_norm", "w_ukv", "q_norm", "k_norm", "decay_logit", "w_out", "w_ffn_gate", "w_ffn_up",
        "w_ffn_down", "w_router", "w_exp_gate", "w_exp_up", "w_exp_down"]
_OUTS = [(1, 128, 1024), (1, 256, 1024), (1, 2, 128, 256), (1, 2, 128, 32), (1, 2, 2, 4, 128, 128)]
GRID_W = 64
ROPE_BASE = 10000.0


def shape_constants():
    import numpy as np

    tab = np.zeros((P, N_CONST), np.float32)

    def put(name, a):
        lo, hi = CONST[name]
        tab[:, lo:hi] = np.asarray(a, np.float32).reshape(P, hi - lo)

    def rotary(dim):
        n = (NT - 1) * P
        half = dim // 2
        freqs = (np.float32(ROPE_BASE) ** (-np.arange(0, half, 2, dtype=np.float32) / np.float32(half))).astype(np.float32)
        tok = np.arange(n)

        def ang(p):
            a = p.astype(np.float32)[:, None] * freqs[None, :]
            return np.concatenate([a, a], -1)
        a = np.concatenate([ang(tok // GRID_W), ang(tok % GRID_W)], -1)
        cos, sin = np.cos(a).astype(np.float32), np.sin(a).astype(np.float32)
        sin = sin.reshape(n, 2, 2, dim // 4).copy()
        sin[:, :, 0] *= -1
        lay = lambda z: z.reshape(NT - 1, P, dim).transpose(1, 0, 2)
        return lay(cos), lay(sin.reshape(n, dim))

    i = np.arange(P)
    put("ident", np.eye(P))
    for tag, dim in (("m", ROPE), ("r", RD)):
        cos, sin = rotary(dim)
        put("cos" + tag, cos)
        put("sin" + tag, sin)
    put("kexp", np.stack([P - 1 - i, i], 1))
    put("qexp", np.broadcast_to(np.stack([i + 1, P - i]), (P, 2, P)))
    d = i[None, :] - i[:, None]
    put("dexp", np.stack([np.maximum(d, 0), np.maximum(-d, 0)], 1))
    put("tri", np.stack([d >= 0, d <= 0], 1))
    put("upper", d > 0)
    put("ones", np.ones((P, P)))
    put("number", np.broadcast_to(1 + np.arange(EXPERTS * CHUNKS_OVER), (P, EXPERTS * CHUNKS_OVER)))
    put("iota", np.broadcast_to(i, (P, P)))
    return tab


def kernel(**inputs):
    import numpy as _np
    import concourse.bacc as _bacc
    from concourse import mybir as _mybir
    from concourse.bass_utils import run_bass_kernel_spmd as _run

    nc = _bacc.Bacc("TRN2", target_bir_lowering=False, num_devices=1)
    arrays, args = {}, []
    for name in _INS:
        a = _np.ascontiguousarray(inputs[name])
        arrays[f"in_{name}"] = a
        args.append(nc.dram_tensor(f"in_{name}", a.shape, _mybir.dt.from_np(a.dtype), kind="ExternalInput").ap())
    tab = shape_constants()
    arrays["in_const"] = tab
    args.append(nc.dram_tensor("in_const", tab.shape, _mybir.dt.float32, kind="ExternalInput").ap())
    for i, shape in enumerate(_OUTS):
        args.append(nc.dram_tensor(f"out_{i}", shape, _mybir.dt.float32, kind="ExternalOutput").ap())
    hybrid_step(nc, *args)
    r = _run(nc, [arrays], core_ids=[0])
    return tuple(r.results[0][f"out_{i}"] for i in range(len(_OUTS)))
```
